# Optimizing a Trainium2 kernel written in Bass

```python
import math
import jax, jax.numpy as jnp
from jax import lax
import numpy as np
import jax
import jax.numpy as jnp

D_MODEL = 1024
BATCH = 1
SEQ = 512
DEPTH = 2

N_A_LAYERS = max(1, DEPTH // 2)
N_B_LAYERS = DEPTH - N_A_LAYERS

DIFF_HEADS = 8
DIFF_QK_DIM = 64
DIFF_V_DIM = 2 * DIFF_QK_DIM
T5_BUCKETS = 32
T5_MAX_DISTANCE = 128
MLA_HEADS = 16
MLA_QK_NOPE = 128
MLA_QK_ROPE = 64
MLA_V_DIM = 128
MLA_Q_LORA = 512
MLA_KV_LORA = 256
ROPE_BASE = 10000.0
D_FF = 2816
CONV_WIDTH = 3
PLE_DIM = 256
Q_BLOCK = 128
RMS_EPS = 1e-6
NEG_INF = -1e30
POS_OFFSET_MAX = 1024


def rms_norm(x, gain):
    xf = x.astype(jnp.float32)
    y = xf * lax.rsqrt(jnp.mean(xf * xf, axis=-1, keepdims=True) + RMS_EPS)
    return (y * gain.astype(jnp.float32)).astype(x.dtype)

def rotary(x, pos):
    d = x.shape[-1]
    half = d // 2
    inv_freq = jnp.exp(-math.log(ROPE_BASE) * jnp.arange(half, dtype=jnp.float32) * (2.0 / d))
    ang = pos.astype(jnp.float32)[..., None] * inv_freq
    if x.ndim == 4:
        ang = ang[:, :, None, :]
    cos, sin = jnp.cos(ang), jnp.sin(ang)
    xf = x.astype(jnp.float32)
    x1, x2 = xf[..., :half], xf[..., half:]
    return jnp.concatenate([x1 * cos - x2 * sin, x1 * sin + x2 * cos], axis=-1).astype(x.dtype)

def t5_bucket(dist):
    n = jnp.maximum(dist, 0)
    max_exact = T5_BUCKETS // 2
    log_ratio = jnp.log(jnp.maximum(n, 1).astype(jnp.float32) / max_exact) / math.log(T5_MAX_DISTANCE / max_exact)
    large = max_exact + (log_ratio * (T5_BUCKETS - max_exact)).astype(jnp.int32)
    large = jnp.minimum(large, T5_BUCKETS - 1)
    return jnp.where(n < max_exact, n, large)

def to_blocks(t):
    b, s = t.shape[:2]
    return t.reshape((b, s // Q_BLOCK, Q_BLOCK) + t.shape[2:]).swapaxes(0, 1)

def from_blocks(t):
    nb, b, q = t.shape[:3]
    return t.swapaxes(0, 1).reshape((b, nb * q) + t.shape[3:])

def causal_mask(blk_idx, seq):
    q_idx = blk_idx * Q_BLOCK + jnp.arange(Q_BLOCK)
    return jnp.arange(seq)[None, :] <= q_idx[:, None]

def diff_attention(h, pos, w_qkv, q_gain, k_gain, lam_q1, lam_k1, lam_q2, lam_k2, sub_gain, w_o, rel_table, lam_init):
    b, s, _ = h.shape
    qk_w = DIFF_HEADS * 2 * DIFF_QK_DIM
    qkv = h @ w_qkv
    q = rms_norm(qkv[..., :qk_w].reshape(b, s, DIFF_HEADS, 2, DIFF_QK_DIM), q_gain)
    k = rms_norm(qkv[..., qk_w:2 * qk_w].reshape(b, s, DIFF_HEADS, 2, DIFF_QK_DIM), k_gain)
    v = qkv[..., 2 * qk_w:].reshape(b, s, DIFF_HEADS, DIFF_V_DIM)
    f32 = jnp.float32
    lam = (jnp.exp(jnp.sum(lam_q1.astype(f32) * lam_k1.astype(f32)))
           - jnp.exp(jnp.sum(lam_q2.astype(f32) * lam_k2.astype(f32))) + lam_init)
    scale = DIFF_QK_DIM ** -0.5
    nb = s // Q_BLOCK

    def block(args):
        i, q_blk, p_blk = args
        sc = jnp.einsum('bqhcd,bkhcd->bhcqk', q_blk, k).astype(f32) * scale
        bucket = t5_bucket(p_blk[:, :, None] - pos[:, None, :])
        bias = jnp.take(rel_table, bucket, axis=0).astype(f32)
        bias = bias.transpose(0, 3, 1, 2)[:, :, None]
        sc = jnp.where(causal_mask(i, s), sc + bias, NEG_INF)
        a = jax.nn.softmax(sc, axis=-1)
        wts = a[:, :, 0] - lam * a[:, :, 1]
        return jnp.einsum('bhqk,bkhv->bqhv', wts.astype(v.dtype), v)

    o = lax.map(block, (jnp.arange(nb), to_blocks(q), to_blocks(pos)))
    o = from_blocks(o)
    o = rms_norm(o, sub_gain) * (1.0 - lam_init)
    return o.reshape(b, s, DIFF_HEADS * DIFF_V_DIM) @ w_o

def shared_latent_kv(h, pos, kv_norm, w_dkv, ckv_norm, w_ukv, k_nope_norm, k_pe_norm):
    b, s, _ = h.shape
    hn = rms_norm(h, kv_norm)
    ckv_full = hn @ w_dkv
    c_kv = rms_norm(ckv_full[..., :MLA_KV_LORA], ckv_norm)
    k_pe = rotary(rms_norm(ckv_full[..., MLA_KV_LORA:], k_pe_norm), pos)
    kv = (c_kv @ w_ukv).reshape(b, s, MLA_HEADS, MLA_QK_NOPE + MLA_V_DIM)
    k_nope = rms_norm(kv[..., :MLA_QK_NOPE], k_nope_norm)
    v = kv[..., MLA_QK_NOPE:]
    return k_nope, k_pe, v

def mla_attention(h, pos, w_dq, cq_norm, w_uq, q_nope_norm, q_pe_norm, w_o, k_nope, k_pe, v):
    b, s, _ = h.shape
    c_q = rms_norm(h @ w_dq, cq_norm)
    q = (c_q @ w_uq).reshape(b, s, MLA_HEADS, MLA_QK_NOPE + MLA_QK_ROPE)
    q_nope = rms_norm(q[..., :MLA_QK_NOPE], q_nope_norm)
    q_pe = rotary(rms_norm(q[..., MLA_QK_NOPE:], q_pe_norm), pos)
    scale = (MLA_QK_NOPE + MLA_QK_ROPE) ** -0.5
    nb = s // Q_BLOCK

    def block(args):
        i, qn, qp = args
        sc = (jnp.einsum('bqhd,bkhd->bhqk', qn, k_nope)
              + jnp.einsum('bqhr,bkr->bhqk', qp, k_pe)).astype(jnp.float32) * scale
        sc = jnp.where(causal_mask(i, s), sc, NEG_INF)
        a = jax.nn.softmax(sc, axis=-1)
        return jnp.einsum('bhqk,bkhv->bqhv', a.astype(v.dtype), v)

    o = from_blocks(lax.map(block, (jnp.arange(nb), to_blocks(q_nope), to_blocks(q_pe))))
    return o.reshape(b, s, MLA_HEADS * MLA_V_DIM) @ w_o

def conv_gated_ffn(h, w_in, conv_w, conv_b, w_out):
    s = h.shape[1]
    u = h @ w_in
    u_pad = jnp.pad(u, ((0, 0), (CONV_WIDTH - 1, 0), (0, 0)))
    c = conv_b
    for j in range(CONV_WIDTH):
        c = c + u_pad[:, j:j + s, :] * conv_w[j]
    a, g = jnp.split(c, 2, axis=-1)
    return (jax.nn.silu(g) * a) @ w_out

def per_layer_embedding(h, p_i, norm_g, w_proj, w_gate):
    gate = jax.nn.sigmoid(rms_norm(h, norm_g) @ w_gate)
    return (p_i @ w_proj) * gate

def first_inputs(seed: int = 0) -> dict:
    key = jax.random.key(seed)
    keys = iter(jax.random.split(key, 48))
    f32 = jnp.float32

    def dense(shape, fan_in):
        return jax.random.normal(next(keys), shape, f32) * fan_in ** -0.5

    def gain(shape):
        return 1.0 + 0.05 * jax.random.normal(next(keys), shape, f32)

    def small(shape, scale):
        return scale * jax.random.normal(next(keys), shape, f32)

    na, nbl = N_A_LAYERS, N_B_LAYERS
    qkv_w = 2 * DIFF_HEADS * 2 * DIFF_QK_DIM + DIFF_HEADS * DIFF_V_DIM
    x = jax.random.normal(next(keys), (BATCH, SEQ, D_MODEL), f32)
    p = jax.random.normal(next(keys), (DEPTH, BATCH, SEQ, PLE_DIM), f32)
    offsets = jax.random.randint(next(keys), (BATCH, 1), 0, POS_OFFSET_MAX, dtype=jnp.int32)
    positions = offsets + jnp.arange(SEQ, dtype=jnp.int32)[None, :]
    return {
        'x': x,
        'p': p,
        'positions': positions,
        'rel_bias_table': small((T5_BUCKETS, DIFF_HEADS), 0.5),
        'attn_norm': gain((DEPTH, D_MODEL)),
        'a_w_qkv': dense((na, D_MODEL, qkv_w), D_MODEL),
        'a_q_norm': gain((na, DIFF_QK_DIM)),
        'a_k_norm': gain((na, DIFF_QK_DIM)),
        'a_lam_q1': small((na, DIFF_QK_DIM), 0.1),
        'a_lam_k1': small((na, DIFF_QK_DIM), 0.1),
        'a_lam_q2': small((na, DIFF_QK_DIM), 0.1),
        'a_lam_k2': small((na, DIFF_QK_DIM), 0.1),
        'a_sub_norm': gain((na, DIFF_V_DIM)),
        'a_w_o': dense((na, DIFF_HEADS * DIFF_V_DIM, D_MODEL), DIFF_HEADS * DIFF_V_DIM),
        'kv_norm': gain((D_MODEL,)),
        'w_dkv': dense((D_MODEL, MLA_KV_LORA + MLA_QK_ROPE), D_MODEL),
        'ckv_norm': gain((MLA_KV_LORA,)),
        'w_ukv': dense((MLA_KV_LORA, MLA_HEADS * (MLA_QK_NOPE + MLA_V_DIM)), MLA_KV_LORA),
        'k_nope_norm': gain((MLA_QK_NOPE,)),
        'k_pe_norm': gain((MLA_QK_ROPE,)),
        'b_w_dq': dense((nbl, D_MODEL, MLA_Q_LORA), D_MODEL),
        'b_cq_norm': gain((nbl, MLA_Q_LORA)),
        'b_w_uq': dense((nbl, MLA_Q_LORA, MLA_HEADS * (MLA_QK_NOPE + MLA_QK_ROPE)), MLA_Q_LORA),
        'b_q_nope_norm': gain((nbl, MLA_QK_NOPE)),
        'b_q_pe_norm': gain((nbl, MLA_QK_ROPE)),
        'b_w_o': dense((nbl, MLA_HEADS * MLA_V_DIM, D_MODEL), MLA_HEADS * MLA_V_DIM),
        'ffn_norm': gain((DEPTH, D_MODEL)),
        'ffn_w_in': dense((DEPTH, D_MODEL, 2 * D_FF), D_MODEL),
        'ffn_conv_w': dense((DEPTH, CONV_WIDTH, 2 * D_FF), CONV_WIDTH),
        'ffn_conv_b': small((DEPTH, 2 * D_FF), 0.02),
        'ffn_w_out': dense((DEPTH, D_FF, D_MODEL), D_FF),
        'ple_norm': gain((DEPTH, D_MODEL)),
        'ple_w_proj': dense((DEPTH, PLE_DIM, D_MODEL), PLE_DIM),
        'ple_w_gate': dense((DEPTH, D_MODEL, D_MODEL), D_MODEL),
    }

def first_block(x, p, positions, rel_bias_table, attn_norm,
              a_w_qkv, a_q_norm, a_k_norm, a_lam_q1, a_lam_k1, a_lam_q2, a_lam_k2, a_sub_norm, a_w_o,
              kv_norm, w_dkv, ckv_norm, w_ukv, k_nope_norm, k_pe_norm,
              b_w_dq, b_cq_norm, b_w_uq, b_q_nope_norm, b_q_pe_norm, b_w_o,
              ffn_norm, ffn_w_in, ffn_conv_w, ffn_conv_b, ffn_w_out,
              ple_norm, ple_w_proj, ple_w_gate):
    h = x
    shared = None
    for i in range(DEPTH):
        hn = rms_norm(h, attn_norm[i])
        if i < N_A_LAYERS:
            lam_init = 0.8 - 0.6 * math.exp(-0.3 * i)
            mix = diff_attention(hn, positions, a_w_qkv[i], a_q_norm[i], a_k_norm[i],
                                 a_lam_q1[i], a_lam_k1[i], a_lam_q2[i], a_lam_k2[i],
                                 a_sub_norm[i], a_w_o[i], rel_bias_table, lam_init)
        else:
            if shared is None:
                shared = shared_latent_kv(h, positions, kv_norm, w_dkv, ckv_norm, w_ukv,
                                          k_nope_norm, k_pe_norm)
            j = i - N_A_LAYERS
            k_nope, k_pe, v = shared
            mix = mla_attention(hn, positions, b_w_dq[j], b_cq_norm[j], b_w_uq[j],
                                b_q_nope_norm[j], b_q_pe_norm[j], b_w_o[j], k_nope, k_pe, v)
        h = h + mix
        h = h + conv_gated_ffn(rms_norm(h, ffn_norm[i]), ffn_w_in[i], ffn_conv_w[i],
                               ffn_conv_b[i], ffn_w_out[i])
        h = h + per_layer_embedding(h, p[i], ple_norm[i], ple_w_proj[i], ple_w_gate[i])
    return h


DEPTH_2 = 1

HEAD_DIM = 64
NSA_HEADS = 8
NSA_KV_HEADS = 2
NSA_GROUP = NSA_HEADS // NSA_KV_HEADS
CMP_BLOCK = 32
CMP_STRIDE = 16
CMP_HIDDEN = 256
SLC_BLOCK = 64
N_SELECT = 16
WINDOW = 512
NSA_Q_BLOCK = 64
N_BRANCH = 3
CONV_CHANNELS = 256
CONV_WIDTH_2 = 31
GLA_HEADS = 4
GLA_KEY_DIM = 128
GLA_VALUE_DIM = 256
GLA_GATE_RANK = 16
GLA_TAU = 16.0
GLA_CHUNK = 64
REL_BUCKETS = 32
REL_MAX_DIST = 128
D_FF_2 = -(-8 * D_MODEL // (3 * 256)) * 256
EPS = 1e-6
NEG = -1e30
BIG = 1e30

D_MIX = NSA_HEADS * HEAD_DIM + CONV_CHANNELS + GLA_VALUE_DIM
IN_SPLITS = (
    NSA_HEADS * HEAD_DIM,
    NSA_KV_HEADS * HEAD_DIM, NSA_KV_HEADS * HEAD_DIM,
    NSA_KV_HEADS * HEAD_DIM, NSA_KV_HEADS * HEAD_DIM,
    NSA_KV_HEADS * HEAD_DIM, NSA_KV_HEADS * HEAD_DIM,
    NSA_HEADS * N_BRANCH,
    2 * CONV_CHANNELS,
    GLA_KEY_DIM, GLA_KEY_DIM, GLA_VALUE_DIM,
    GLA_GATE_RANK,
    GLA_VALUE_DIM,
)
D_IN = sum(IN_SPLITS)


def rms_norm_2(x, g):
    x32 = x.astype(jnp.float32)
    y = x32 * lax.rsqrt(jnp.mean(x32 * x32, axis=-1, keepdims=True) + EPS)
    return (y * g.astype(jnp.float32)).astype(x.dtype)

def layer_norm(x, g, b):
    x32 = x.astype(jnp.float32)
    mu = jnp.mean(x32, axis=-1, keepdims=True)
    xc = x32 - mu
    y = xc * lax.rsqrt(jnp.mean(xc * xc, axis=-1, keepdims=True) + EPS)
    return (y * g.astype(jnp.float32) + b.astype(jnp.float32)).astype(x.dtype)

def t5_bucket_2(dist):
    n = jnp.maximum(dist, 0)
    max_exact = REL_BUCKETS // 2
    nf = jnp.maximum(n, 1).astype(jnp.float32)
    large = max_exact + (jnp.log(nf / max_exact) / math.log(REL_MAX_DIST / max_exact)
                         * (REL_BUCKETS - max_exact)).astype(jnp.int32)
    large = jnp.minimum(large, REL_BUCKETS - 1)
    return jnp.where(n < max_exact, n, large)

def masked_softmax(s, mask):
    p = jax.nn.softmax(jnp.where(mask, s, NEG), axis=-1)
    return jnp.where(mask, p, 0.0)

def compress_kv(kv, pos, w1, b1, w2):
    B, S, Hk, D = kv.shape
    r = CMP_BLOCK // CMP_STRIDE
    nsub = S // CMP_STRIDE
    ncmp = nsub - r + 1
    sub = kv.reshape(B, nsub, CMP_STRIDE, Hk, D)
    blocks = jnp.concatenate([sub[:, j:ncmp + j] for j in range(r)], axis=2)
    blocks = blocks + pos[None, None, :, None, :]
    flat = blocks.transpose(0, 1, 3, 2, 4).reshape(B, ncmp, Hk, CMP_BLOCK * D)
    return jax.nn.silu(flat @ w1 + b1) @ w2

def nsa_attention(q, kc, vc, ks, vs, kw, vw, gates, rel_bias):
    B, S = q.shape[0], q.shape[1]
    Hk, G, D = NSA_KV_HEADS, NSA_GROUP, HEAD_DIM
    ncmp = kc.shape[1]
    nsel = S // SLC_BLOCK
    n_top = min(N_SELECT, nsel)
    q = q.reshape(B, S, Hk, G, D) * (D ** -0.5)
    gates = gates.reshape(B, S, Hk, G, N_BRANCH)
    bias_h = rel_bias.T.astype(jnp.float32)
    bias_hkg = bias_h.reshape(Hk, G, REL_BUCKETS).transpose(0, 2, 1)
    cmp_end = jnp.arange(ncmp, dtype=jnp.int32) * CMP_STRIDE + (CMP_BLOCK - 1)
    rs, rc = SLC_BLOCK // CMP_STRIDE, CMP_BLOCK // CMP_STRIDE
    agg = (np.arange(nsel)[:, None, None] * rs + np.arange(rs)[None, :, None]
           - np.arange(rc)[None, None, :]).reshape(nsel, rs * rc)
    agg_valid = jnp.asarray((agg >= 0) & (agg < ncmp))
    agg_idx = jnp.asarray(np.clip(agg, 0, ncmp - 1), dtype=jnp.int32)
    ks_blk = ks.reshape(B, nsel, SLC_BLOCK, Hk, D).transpose(0, 3, 1, 2, 4)
    vs_blk = vs.reshape(B, nsel, SLC_BLOCK, Hk, D).transpose(0, 3, 1, 2, 4)
    kw_pad = jnp.pad(kw, ((0, 0), (WINDOW, 0), (0, 0), (0, 0)))
    vw_pad = jnp.pad(vw, ((0, 0), (WINDOW, 0), (0, 0), (0, 0)))
    b_idx = jnp.arange(B)[:, None, None, None]
    h_idx = jnp.arange(Hk)[None, :, None, None]
    blk_ids = jnp.arange(nsel, dtype=jnp.int32)
    offs = jnp.arange(SLC_BLOCK, dtype=jnp.int32)
    win_offs = jnp.arange(NSA_Q_BLOCK + WINDOW, dtype=jnp.int32)
    Q = NSA_Q_BLOCK

    def head_bias(dist):
        return bias_h[:, t5_bucket_2(dist)].reshape(Hk, G, *dist.shape)

    def block_fn(c):
        q0 = c * Q
        t = q0 + jnp.arange(Q, dtype=jnp.int32)
        qc = lax.dynamic_slice_in_dim(q, q0, Q, axis=1)
        gc = lax.dynamic_slice_in_dim(gates, q0, Q, axis=1)
        dist_c = t[:, None] - cmp_end[None, :]
        s_c = jnp.einsum('bqhgd,bnhd->bhgqn', qc, kc).astype(jnp.float32) + head_bias(dist_c)
        p_c = masked_softmax(s_c, dist_c >= 0)
        o_c = jnp.einsum('bhgqn,bnhd->bqhgd', p_c.astype(vc.dtype), vc)
        imp = p_c.sum(axis=2)
        imp = jnp.where(agg_valid, jnp.take(imp, agg_idx, axis=-1), 0.0).sum(-1)
        cur = t // SLC_BLOCK
        forced = ((blk_ids[None, :] == 0) | (blk_ids[None, :] == cur[:, None])
                  | (blk_ids[None, :] == cur[:, None] - 1))
        causal_blk = blk_ids[None, :] * SLC_BLOCK <= t[:, None]
        score = jnp.where(causal_blk, jnp.where(forced, BIG, imp), NEG)
        top_val, top_idx = lax.top_k(score, n_top)
        sel_ok = top_val > 0.5 * NEG
        k_sel = ks_blk[b_idx, h_idx, top_idx]
        v_sel = vs_blk[b_idx, h_idx, top_idx]
        key_pos = top_idx[..., None] * SLC_BLOCK + offs
        dist_s = t[None, None, :, None, None] - key_pos
        s_s = jnp.einsum('bqhgd,bhqnkd->bhgqnk', qc, k_sel).astype(jnp.float32)
        bias_s = bias_hkg[h_idx[..., None], t5_bucket_2(dist_s)]
        s_s = s_s + jnp.moveaxis(bias_s, -1, 2)
        mask_s = (sel_ok[..., None] & (dist_s >= 0))[:, :, None]
        p_s = masked_softmax(s_s.reshape(B, Hk, G, Q, n_top * SLC_BLOCK),
                             mask_s.reshape(B, Hk, 1, Q, n_top * SLC_BLOCK)).reshape(s_s.shape)
        o_s = jnp.einsum('bhgqnk,bhqnkd->bqhgd', p_s.astype(v_sel.dtype), v_sel)
        kwc = lax.dynamic_slice_in_dim(kw_pad, q0, Q + WINDOW, axis=1)
        vwc = lax.dynamic_slice_in_dim(vw_pad, q0, Q + WINDOW, axis=1)
        key_pos_w = q0 - WINDOW + win_offs
        dist_w = t[:, None] - key_pos_w[None, :]
        mask_w = (dist_w >= 0) & (dist_w < WINDOW) & (key_pos_w[None, :] >= 0)
        s_w = jnp.einsum('bqhgd,bkhd->bhgqk', qc, kwc).astype(jnp.float32) + head_bias(dist_w)
        p_w = masked_softmax(s_w, mask_w)
        o_w = jnp.einsum('bhgqk,bkhd->bqhgd', p_w.astype(vwc.dtype), vwc)
        return gc[..., 0:1] * o_c + gc[..., 1:2] * o_s + gc[..., 2:3] * o_w

    out = lax.map(block_fn, jnp.arange(S // Q, dtype=jnp.int32))
    return out.transpose(1, 0, 2, 3, 4, 5).reshape(B, S, NSA_HEADS * HEAD_DIM)

def conformer_conv(u, w_dw, b_dw, ln_g, ln_b):
    a, g = jnp.split(u, 2, axis=-1)
    h = a * jax.nn.sigmoid(g)
    h = lax.conv_general_dilated(h, w_dw[:, None, :], window_strides=(1,),
                                 padding=[(CONV_WIDTH_2 - 1, 0)],
                                 dimension_numbers=('NWC', 'WIO', 'NWC'),
                                 feature_group_count=CONV_CHANNELS) + b_dw
    return jax.nn.silu(layer_norm(h, ln_g, ln_b))

def gla_chunked(q, k, v, log_a):
    B, S, H, dk = q.shape
    dv = v.shape[-1]
    C = GLA_CHUNK
    N = S // C

    def chunks(a):
        return a.astype(jnp.float32).reshape(B, N, C, H, a.shape[-1]).transpose(0, 3, 1, 2, 4)

    q, k, v, la = chunks(q), chunks(k), chunks(v), chunks(log_a)
    b = jnp.cumsum(la, axis=3)
    b_last = b[:, :, :, -1:]
    q_t = q * (dk ** -0.5) * jnp.exp(b)
    k_t = k * jnp.exp(-b)
    k_d = k * jnp.exp(b_last - b)
    causal = jnp.tril(jnp.ones((C, C), dtype=bool))
    attn = jnp.where(causal, jnp.einsum('bhncd,bhnsd->bhncs', q_t, k_t), 0.0)
    o_intra = jnp.einsum('bhncs,bhnsv->bhncv', attn, v)

    def step(state, xs):
        qn, kn, vn, dn = xs
        o = jnp.einsum('bhcd,bhdv->bhcv', qn, state)
        state = dn[..., None] * state + jnp.einsum('bhcd,bhcv->bhdv', kn, vn)
        return state, o

    xs = (jnp.moveaxis(q_t, 2, 0), jnp.moveaxis(k_d, 2, 0), jnp.moveaxis(v, 2, 0),
          jnp.moveaxis(jnp.exp(b_last[:, :, :, 0]), 2, 0))
    _, o_inter = lax.scan(step, jnp.zeros((B, H, dk, dv), jnp.float32), xs)
    o = o_intra + jnp.moveaxis(o_inter, 0, 2)
    return o.transpose(0, 2, 3, 1, 4).reshape(B, S, H, dv)

def second_inputs(seed: int = 0) -> dict:
    key = jax.random.key(seed)
    ks = jax.random.split(key, 32)
    L = DEPTH_2

    def nrm(k, shape, scale):
        return jax.random.normal(k, shape, jnp.float32) * scale

    def gain(k, shape):
        return 1.0 + 0.05 * jax.random.normal(k, shape, jnp.float32)

    return {
        "x": nrm(ks[0], (BATCH, SEQ, D_MODEL), 1.0),
        "p": nrm(ks[1], (DEPTH_2, BATCH, SEQ, PLE_DIM), 1.0),
        "rel_bias": nrm(ks[2], (REL_BUCKETS, NSA_HEADS), 0.5),
        "mix_norm_g": gain(ks[3], (L, D_MODEL)),
        "w_in": nrm(ks[4], (L, D_MODEL, D_IN), D_MODEL ** -0.5),
        "w_out": nrm(ks[5], (L, D_MIX, D_MODEL), D_MIX ** -0.5),
        "cmp_pos_k": nrm(ks[6], (L, CMP_BLOCK, HEAD_DIM), 0.1),
        "cmp_w1_k": nrm(ks[7], (L, CMP_BLOCK * HEAD_DIM, CMP_HIDDEN), (CMP_BLOCK * HEAD_DIM) ** -0.5),
        "cmp_b1_k": nrm(ks[8], (L, CMP_HIDDEN), 0.02),
        "cmp_w2_k": nrm(ks[9], (L, CMP_HIDDEN, HEAD_DIM), CMP_HIDDEN ** -0.5),
        "cmp_pos_v": nrm(ks[10], (L, CMP_BLOCK, HEAD_DIM), 0.1),
        "cmp_w1_v": nrm(ks[11], (L, CMP_BLOCK * HEAD_DIM, CMP_HIDDEN), (CMP_BLOCK * HEAD_DIM) ** -0.5),
        "cmp_b1_v": nrm(ks[12], (L, CMP_HIDDEN), 0.02),
        "cmp_w2_v": nrm(ks[13], (L, CMP_HIDDEN, HEAD_DIM), CMP_HIDDEN ** -0.5),
        "conv_w": nrm(ks[14], (L, CONV_WIDTH_2, CONV_CHANNELS), CONV_WIDTH_2 ** -0.5),
        "conv_b": nrm(ks[15], (L, CONV_CHANNELS), 0.02),
        "conv_ln_g": gain(ks[16], (L, CONV_CHANNELS)),
        "conv_ln_b": nrm(ks[17], (L, CONV_CHANNELS), 0.02),
        "gla_w_alpha": nrm(ks[18], (L, GLA_GATE_RANK, GLA_KEY_DIM), GLA_GATE_RANK ** -0.5),
        "gla_b_alpha": nrm(ks[19], (L, GLA_KEY_DIM), 0.02),
        "gla_norm_g": gain(ks[20], (L, GLA_VALUE_DIM)),
        "ffn_norm_g": gain(ks[21], (L, D_MODEL)),
        "ffn_w_gate": nrm(ks[22], (L, D_MODEL, D_FF_2), D_MODEL ** -0.5),
        "ffn_w_up": nrm(ks[23], (L, D_MODEL, D_FF_2), D_MODEL ** -0.5),
        "ffn_w_down": nrm(ks[24], (L, D_FF_2, D_MODEL), D_FF_2 ** -0.5),
        "ple_norm_g": gain(ks[25], (L, D_MODEL)),
        "ple_w_gate": nrm(ks[26], (L, D_MODEL, D_MODEL), D_MODEL ** -0.5),
        "ple_w_proj": nrm(ks[27], (L, PLE_DIM, D_MODEL), PLE_DIM ** -0.5),
        "final_norm_g": gain(ks[28], (D_MODEL,)),
    }

def second_block(x, p, rel_bias, mix_norm_g, w_in, w_out,
              cmp_pos_k, cmp_w1_k, cmp_b1_k, cmp_w2_k,
              cmp_pos_v, cmp_w1_v, cmp_b1_v, cmp_w2_v,
              conv_w, conv_b, conv_ln_g, conv_ln_b,
              gla_w_alpha, gla_b_alpha, gla_norm_g,
              ffn_norm_g, ffn_w_gate, ffn_w_up, ffn_w_down,
              ple_norm_g, ple_w_gate, ple_w_proj, final_norm_g):
    B, S, _ = x.shape
    split_at = np.cumsum(IN_SPLITS)[:-1].tolist()

    def heads(a, n):
        return a.reshape(B, S, n, -1)

    for i in range(DEPTH_2):
        h = rms_norm_2(x, mix_norm_g[i])
        z = h @ w_in[i]
        (nq, kc, vc, ks_, vs_, kw, vw, ng, cu, gq, gk, gv, ga, gr) = jnp.split(z, split_at, axis=-1)
        kc = compress_kv(heads(kc, NSA_KV_HEADS), cmp_pos_k[i], cmp_w1_k[i], cmp_b1_k[i], cmp_w2_k[i])
        vc = compress_kv(heads(vc, NSA_KV_HEADS), cmp_pos_v[i], cmp_w1_v[i], cmp_b1_v[i], cmp_w2_v[i])
        y_nsa = nsa_attention(heads(nq, NSA_HEADS), kc, vc,
                              heads(ks_, NSA_KV_HEADS), heads(vs_, NSA_KV_HEADS),
                              heads(kw, NSA_KV_HEADS), heads(vw, NSA_KV_HEADS),
                              jax.nn.sigmoid(ng).reshape(B, S, NSA_HEADS, N_BRANCH), rel_bias)
        y_conv = conformer_conv(cu, conv_w[i], conv_b[i], conv_ln_g[i], conv_ln_b[i])
        log_a = jax.nn.log_sigmoid((ga @ gla_w_alpha[i] + gla_b_alpha[i]).astype(jnp.float32)) / GLA_TAU
        o = gla_chunked(heads(gq, GLA_HEADS), heads(gk, GLA_HEADS), heads(gv, GLA_HEADS),
                        heads(log_a, GLA_HEADS))
        o = rms_norm_2(o, gla_norm_g[i].reshape(GLA_HEADS, -1)).reshape(B, S, GLA_VALUE_DIM)
        y_gla = (o * jax.nn.silu(gr)).astype(x.dtype)
        x = x + jnp.concatenate([y_nsa, y_conv, y_gla], axis=-1) @ w_out[i]
        h = rms_norm_2(x, ffn_norm_g[i])
        x = x + (jax.nn.silu(h @ ffn_w_gate[i]) * (h @ ffn_w_up[i])) @ ffn_w_down[i]
        gate = jax.nn.sigmoid(rms_norm_2(x, ple_norm_g[i]) @ ple_w_gate[i])
        x = x + (p[i] @ ple_w_proj[i]) * gate
    return rms_norm_2(x, final_norm_g)


def setup_inputs(seed=0):
    out = dict(first_inputs(seed))
    for name, value in second_inputs(seed + 1).items():
        if name != "x":
            out[name + "_2"] = value
    return out


def reference(
    x, p, positions, rel_bias_table, attn_norm, a_w_qkv, a_q_norm, a_k_norm, a_lam_q1, a_lam_k1,
    a_lam_q2, a_lam_k2, a_sub_norm, a_w_o, kv_norm, w_dkv, ckv_norm, w_ukv, k_nope_norm,
    k_pe_norm, b_w_dq, b_cq_norm, b_w_uq, b_q_nope_norm, b_q_pe_norm, b_w_o, ffn_norm, ffn_w_in,
    ffn_conv_w, ffn_conv_b, ffn_w_out, ple_norm, ple_w_proj, ple_w_gate, p_2, rel_bias_2,
    mix_norm_g_2, w_in_2, w_out_2, cmp_pos_k_2, cmp_w1_k_2, cmp_b1_k_2, cmp_w2_k_2, cmp_pos_v_2,
    cmp_w1_v_2, cmp_b1_v_2, cmp_w2_v_2, conv_w_2, conv_b_2, conv_ln_g_2, conv_ln_b_2,
    gla_w_alpha_2, gla_b_alpha_2, gla_norm_g_2, ffn_norm_g_2, ffn_w_gate_2, ffn_w_up_2,
    ffn_w_down_2, ple_norm_g_2, ple_w_gate_2, ple_w_proj_2, final_norm_g_2,
):
    x = first_block(
        x, p, positions, rel_bias_table, attn_norm, a_w_qkv, a_q_norm, a_k_norm, a_lam_q1,
        a_lam_k1, a_lam_q2, a_lam_k2, a_sub_norm, a_w_o, kv_norm, w_dkv, ckv_norm, w_ukv,
        k_nope_norm, k_pe_norm, b_w_dq, b_cq_norm, b_w_uq, b_q_nope_norm, b_q_pe_norm, b_w_o,
        ffn_norm, ffn_w_in, ffn_conv_w, ffn_conv_b, ffn_w_out, ple_norm, ple_w_proj, ple_w_gate,
    )
    return second_block(
        x, p_2, rel_bias_2, mix_norm_g_2, w_in_2, w_out_2, cmp_pos_k_2, cmp_w1_k_2, cmp_b1_k_2,
        cmp_w2_k_2, cmp_pos_v_2, cmp_w1_v_2, cmp_b1_v_2, cmp_w2_v_2, conv_w_2, conv_b_2,
        conv_ln_g_2, conv_ln_b_2, gla_w_alpha_2, gla_b_alpha_2, gla_norm_g_2, ffn_norm_g_2,
        ffn_w_gate_2, ffn_w_up_2, ffn_w_down_2, ple_norm_g_2, ple_w_gate_2, ple_w_proj_2,
        final_norm_g_2,
    )


_drawn_inputs = setup_inputs


def setup_inputs(seed=0):
    import zlib

    import numpy as np

    out = dict(_drawn_inputs(seed))
    spreads = {}
    factors = {'a_lam_k1': 8.0,
     'a_lam_q2': 8.0,
     'kv_norm': 4.376,
     'ckv_norm': 4.806,
     'k_nope_norm': 8.0,
     'k_pe_norm': 8.0,
     'b_cq_norm': 8.0,
     'b_q_nope_norm': 8.0,
     'b_q_pe_norm': 8.0,
     'ffn_conv_b': 3.396,
     'ple_norm': 5.78,
     'mix_norm_g_2': 2.68,
     'cmp_pos_k_2': 8.0,
     'cmp_w1_k_2': 3.303,
     'cmp_b1_k_2': 64.0,
     'cmp_w2_k_2': 3.269,
     'cmp_pos_v_2': 15.627,
     'cmp_b1_v_2': 64.0,
     'conv_b_2': 23.45,
     'conv_ln_g_2': 22.548,
     'conv_ln_b_2': 64.0,
     'gla_b_alpha_2': 8.0,
     'gla_norm_g_2': 7.083,
     'ple_norm_g_2': 200.0,
     'ffn_norm_g_2': 8.0,
     'p_2': 3.754,
     'ple_w_gate_2': 5.343,
     'ple_w_proj_2': 3.758}
    for name, (base, spread) in spreads.items():
        noise = np.random.default_rng([zlib.crc32(name.encode()), seed]).standard_normal(out[name].shape)
        drawn = base * np.exp(spread * noise) if base else spread * noise
        out[name] = jnp.asarray(drawn.astype(out[name].dtype))
    for name, factor in factors.items():
        out[name] = (out[name] * factor).astype(out[name].dtype)
    return out
```

```python
import math
from collections import namedtuple
from contextlib import ExitStack

import concourse.bass as bass
import numpy as np
from concourse import mybir

P = 128
S = 512
D = 1024
DC = D // P
NQ = S // P
FF = 2816
FC = FF // P
EPS = 1e-6
NEG = -1e30
BUCKETS, MAX_EXACT, MAX_DIST = 32, 16, 128
AH, AQK = 8, 64
LAM_INIT = 0.8 - 0.6 * math.exp(0.0)
BH, NOPE, ROPE = 16, 128, 64
QL, KVL = 512, 256
ROPE_BASE = 10000.0
CH, CKV, CD = 8, 2, 64
CMPB, CMPS, HID = 32, 16, 256
NCMP = S // CMPS - CMPB // CMPS + 1
CC, CW = 256, 31
GH, GK, GV, GCH, TAU = 4, 32, 64, 64, 16.0
NCH = S // GCH
SLOT = 24 * P
LEN = [(i + 1) * P for i in range(NQ)]
OFF = [sum(LEN[:i]) for i in range(NQ)]
CAUSAL = sum(LEN)
B_PAIRS = BH // 2

F32 = mybir.dt.float32
I32 = mybir.dt.int32
ALU = mybir.AluOpType
ACT = mybir.ActivationFunctionType
AX = mybir.AxisListType

STREAM = [
    ("a_qkv", AH, 3 * DC * P, 3), ("a_wo", 4, 2 * DC * P, 2),
    ("ffn0_in", FC, 2 * DC * P, 2), ("ffn0_out", DC, FC * P, 1), ("ple0", 4, 2 * (DC + 2) * P, 4),
    ("b_dkv", 1, 3 * DC * P, 3), ("b_dq", 2, 2 * DC * P, 2), ("b_pair", B_PAIRS, 20 * P, 7), ("b_wo", DC, BH * P, 1),
    ("ffn1_in", FC, 2 * DC * P, 2), ("ffn1_out", DC, FC * P, 1), ("ple1", 4, 2 * (DC + 2) * P, 4),
    ("c_in", 7, 3 * DC * P, 3), ("c_in_last", 1, 2 * DC * P, 2), ("c_cmp", 4, 16 * P, 1), ("c_out", 4, 2 * DC * P, 2),
    ("ffn2_in", FC, 2 * DC * P, 2), ("ffn2_out", DC, FC * P, 1), ("ple2", 4, 2 * (DC + 2) * P, 4),
]
GROUP, TILE, PER = {}, {}, {}
GROUP_END = []
_g = _t = 0
for _n, _c, _f, _per in STREAM:
    GROUP[_n], TILE[_n], PER[_n] = _g, _t, _per
    _g += _c
    for _ in range(_c):
        _t += _per
        GROUP_END.append(_t)
NORM = {n: i for i, n in enumerate(
    ["attn0", "ffn0", "ple0", "attn1", "ffn1", "ple1", "mix2", "ffn2", "ple2", "final"])}
RESIDUALS = ["a_wo", "ffn0_out", "b_wo", "ffn1_out", "c_out", "ffn2_out"]

SIGNALS = """
consts_in x_in positions_in lam_in table_in p_in extra_in stage_end h_squared h_gained h_gained2 h_summed
r_logged r_ready tile_done tile_taken residual_added out_stored setup_step lam_dots lam_exps bias_built
angles_ready trig_ready f_first f_conv f_silu f_through s_gate ple_sigmoid a_squared a_summed a_logged
a_factor a_normed a_vturned a_vcopied a_scored a_biased a_min a_exped a_recip a_scaled a_weights a_turned
a_tcopied a_pv a_otaken a_osquared a_osummed a_ologged a_ofactor a_onormed bd_squared bd_summed bd_logged
bd_factor bd_normed bd_rotated bd_terms b_squared b_summed b_logged b_factor b_normed b_rotated b_terms
b_rope b_vturned b_vcopied b_scored b_biased b_min b_exped b_recip b_weights b_turned b_tcopied b_pv
b_otaken g_made g_rowed g_written g_read  c_sigmoid c_glu conv_step zp_made hid_act kc_made
kc_copied c_vturned c_vcopied gates_turned gates_made cb_made cc_scored cc_biased cc_min cc_sub cc_exped
cc_sum cc_recip cc_scaled cc_turned cc_copied c_scored c_biased c_min c_exped c_recip c_gated c_weights
c_turned c_tcopied c_pv c_otaken gl_alpha gl_abs gl_exp gl_ln gl_la gl_scale gl_scan gl_diff gl_exps
gl_prod gl_att gl_attc gl_mask gl_kdt gl_kdc gl_u gl_uc gl_state gl_bd gl_out gl_sum gl_add gl_sq gl_ss
gl_log gl_fac gl_norm gl_silu ln_mean ln_cent ln_sq ln_var ln_log ln_fac ln_norm
""".split()
Signals = namedtuple("Signals", SIGNALS)

VEC_COLS = [("attn0", DC), ("attn1", DC), ("kv", DC), ("ffn0", DC), ("ffn1", DC), ("ple0", DC), ("ple1", DC),
            ("mix2", DC), ("ffn2", DC), ("ple2", DC), ("final", DC), ("a_q", 1), ("a_k", 1), ("a_sub", 1),
            ("ckv", 2), ("cq", 4), ("k_nope", 1), ("k_pe", 1), ("q_nope", 1), ("q_pe", 1), ("inv_freq", 1),
            ("conv0", 8 * FC), ("conv1", 8 * FC), ("cmp_b1", 4), ("cmp_pos", 32), ("dw", 2 * CW), ("dw_b", 2),
            ("ln_g", 2), ("ln_b", 2), ("b_alpha", 1), ("gla_g", 2), ("first_block", 1),
            ("t5_start", BUCKETS - 1)]
VEC = {}
NVEC = 0
for _n, _c in VEC_COLS:
    VEC[_n] = NVEC
    NVEC += _c
ARENA = 29824
G_ROWED, G_READ = 1 + AH, 16 * NQ
PI_IN = 3.1415925
BAND = CH * 2 * S


def bucket_starts():
    ratio = MAX_DIST / MAX_EXACT
    return [b if b <= MAX_EXACT else math.ceil(MAX_EXACT * ratio ** ((b - MAX_EXACT) / (BUCKETS - MAX_EXACT)))
            for b in range(1, BUCKETS)]


def wait(eng, sem, value):
    if not (isinstance(value, int) and value <= 0):
        eng.wait_ge(sem, value)


def a_steps(eng, step):
    step(0, 0, True, False, False)
    step(1, 1, True, True, False)
    with eng.Fori(0, (AH - 2) // 2) as i:
        for par in range(2):
            step(2 * i + 2 + par, par, True, True, True)
    step(AH, 0, False, True, True)
    step(AH + 1, 1, False, False, True)


def b_steps(eng, step):
    step(0, 0, True, False)
    step(1, 1, True, True)
    with eng.Fori(0, (B_PAIRS - 2) // 2) as i:
        for par in range(2):
            step(2 * i + 2 + par, par, True, True)
    step(B_PAIRS, 0, False, True)


def build_program(nc, a, out):
    with ExitStack() as ctx:
        def sb(name, *shape, dt=F32):
            return ctx.enter_context(nc.sbuf_tensor(name, list(shape), dt))

        def sem(name):
            return ctx.enter_context(nc.semaphore(name))

        lin = ctx.enter_context(nc.psum_tensor("lin", [P, 2, 512], F32))
        scores = ctx.enter_context(nc.psum_tensor("scores", [P, 2, 512], F32))
        stat = ctx.enter_context(nc.psum_tensor("stat", [P, 512], F32))
        turn = ctx.enter_context(nc.psum_tensor("turn", [P, 2, 512], F32))
        obank = ctx.enter_context(nc.psum_tensor("obank", [P, 512], F32))

        h = sb("h", P, DC, S)
        g = sb("g", P, DC, S)
        slots = sb("slots", P, 2, SLOT)
        r = sb("r", P, S)
        lnr = sb("lnr", P, S)
        vec = sb("vec", P, NVEC)
        consts = sb("consts", P, 8 * P)
        ones, ones64, ident, rot = (consts[:, k * P:(k + 1) * P] for k in range(4))
        maskt = consts[:, 4 * P:8 * P]
        eps = sb("eps", P, 1)
        small = sb("small", P, 64)
        p_in_t = sb("p_in_t", P, 2, S)
        arena = sb("arena", P, ARENA)

        def area(at, *shape):
            n = int(np.prod(shape))
            assert at + n <= ARENA, (at, shape)
            v = arena[:, at:at + n]
            names = "abcd"[:len(shape)]
            if len(shape) == 1:
                return v
            return v.rearrange(f"p ({' '.join(names)}) -> p {' '.join(names)}", **dict(zip(names[:-1], shape[:-1])))

        def v1(name, j=0, n=1):
            c = VEC[name] + j
            return vec[:, c:c + n]

        sq = area(0, DC, S)
        at = DC * S
        a_bias = area(at, AH, CAUSAL); at += AH * CAUSAL
        a_raw = area(at, 3, S); at += 3 * S
        a_sq = a_ri = area(at, 3, S); at += 3 * S
        a_rawo = area(at, S); at += S
        a_qk = area(at, 2, 2, S); at += 4 * S
        a_v = area(at, 2, NQ, P); at += 2 * S
        a_sc = area(at, NQ, 2, S); a_dist = area(at, CAUSAL); a_mask = area(at + CAUSAL, CAUSAL); a_grow = area(at, AH, S); at += 8 * S
        a_pt = area(at, NQ, S)
        pos_i = area(at, S).bitcast(I32); at += S
        posf = area(at, S); at += S
        a_tab = area(at, BUCKETS * AH); at += BUCKETS * AH
        a_diff = area(at, BUCKETS * AH); at += BUCKETS * AH
        a_lam = area(at, 5, AQK); at += 5 * AQK
        a_neg = area(at, P)
        a_step_ok = a_raw[:, 0, 0:S - 1]
        a_onehot, a_relt = a_v[0:BUCKETS, 0, :, :].rearrange("p j c -> p (j c)"), a_v[0:BUCKETS, 1, 0, 0:AH]
        a_o = sq
        regular = sb("regular", P, 2)
        regular_i = sb("regular_i", P, 1, dt=I32)
        posq_i = sb("posq_i", P, NQ, dt=I32)
        cosb = sb("cosb", P, S)
        sinb = sb("sinb", P, S)
        posq = small[:, 0:4]
        nlam, asub, lamd, lame = small[:, 4:5], small[:, 5:6], small[:, 6:8], small[:, 8:10]
        nmax = small[:, 16:32]
        den = small[:, 32:48]
        f_t = area(4096, FC, S)
        f_u = area(4096 + FC * S, 4, S + 2)
        f_c = area(4096 + FC * S + 4 * (S + 2), 4, S)
        f_sg = area(4096 + FC * S + 4 * (S + 2) + 4 * S, 2, S)
        p_gp = area(4096, 2, S)
        p_sg = area(4096 + 2 * S, 2, S)
        p_t = area(4096 + 4 * S, 2, S)
        at = DC * S
        b_g2 = area(at, DC, S); b_o = area(0, BH, S); at += DC * S
        b_sc = g[:, :, :].rearrange("p (x i) s -> p x i s", x=2)
        b_cr = area(at, 7, S); b_raw = b_cr; at += 7 * S
        b_sq = b_ri = area(at, 5, S); at += 5 * S
        b_ckv = area(at, 2, S); at += 2 * S
        b_cq = area(at, 4, S); at += 4 * S
        b_kp = area(at, S); at += S
        b_dsq = area(at, 7, S)
        b_qn = area(at, 2, 2, S); at += 4 * S
        b_kn = area(at, 2, 2, S); at += 4 * S
        b_qp = area(at, 2, S); at += 2 * S
        b_rt = area(at, 3, S); at += 3 * S
        b_v = area(at, 2, 2, S); at += 4 * S
        b_pt = area(at, NQ, S); at += 4 * S
        at = 0
        c_sc = area(at, NQ, 2, S); c_gl = at; at += 8 * S
        c_z = area(at, 23, S); at += 23 * S
        c_ct = c_z[:, 8:16, :]
        c_hp = area(at, 2, S + CW - 1); at += 2 * (S + CW - 1)
        c_acc = area(at, 2, S); at += 2 * S
        c_bias = area(at, CH, S); at += CH * S
        c_cb = area(at, CH, NQ, NCMP); at += CH * NQ * NCMP
        c_pt = area(at, 2, NQ, S); c_zp = area(at, 2, 16, 2 * NCMP)
        neg = area(at + 4 * S, P); onehot = area(at + 6 * S, S)[0:BUCKETS, :]
        relt = area(at + 7 * S, CH)[0:BUCKETS, :]; at += 8 * S
        c_v = area(at, 2, NQ, P); at += 2 * S
        c_ga = area(at, NQ, 24); at += NQ * 24
        c_kc = area(at, 32); at += 32
        c_vc = area(at, 2, CD); at += 2 * CD
        c_hid = area(at, 4, 2 * NCMP); at += 4 * 2 * NCMP
        c_cs = area(at, CH, NQ, NCMP); at += CH * NQ * NCMP
        c_cden = area(at, CH * NQ); at += CH * NQ
        c_cmin = area(at, CH * NQ); at += CH * NQ
        c_small_end = at
        at = c_gl
        gl_qt = area(at, S); at += S
        gl_kt = area(at, S); at += S
        gl_kd = area(at, S); at += S
        gl_b = area(at, S); at += S
        gl_t = area(at, 2, S); at += 2 * S
        gl_s = area(at, 2, S); at += 2 * S
        at = DC * S + 23 * S + 2 * (S + CW - 1) + 2 * S
        gl_am = area(at, GH, NCH // 2, GCH); at += GH * NCH // 2 * GCH
        gl_kdt = area(at, NQ, P); at += S
        gl_vt = area(at, NQ, 2 * P); at += 2 * S
        gl_us = area(at, NCH, GV); at += NCH * GV
        gl_st = area(at, NCH, GV); at += NCH * GV
        gl_bds = area(at, NCH, 2 * P); at += NCH * 2 * P
        gl_o = area(at, 2, S); at += 2 * S
        gl_e = area(at, 3, S); at += 3 * S
        gl_reset = area(at, S); at += S
        gl_dn = small[:, 48:48 + NCH]
        w2c = sb("w2c", P, 4, CD)
        walpha = sb("walpha", P, P)

        landed = [sem("weights_landed_in_slot0"), sem("weights_landed_in_slot1")]

        q = Signals(*(sem(name) for name in SIGNALS))

        ab_dram = nc.dram_tensor("a_bias_by_distance", [P + 1, BAND], F32, kind="Internal").ap()
        g_dram = nc.dram_tensor("bias_by_distance", [P + 1, BAND], F32, kind="Internal").ap()
        block = ctx.enter_context(nc.Block())

        def end_stage(eng, n):
            eng.drain().then_inc(q.stage_end, 1)
            eng.wait_ge(q.stage_end, 4 * (n - 1))

        def group(name, k):
            n = GROUP[name] + k
            return slots[:, n % 2, :], landed[n % 2], 16 * (n // 2 + 1)

        @block.sync
        def _(sp):
            sp.dma_start(a_onehot, a["onehot"]).then_inc(q.table_in, 16)
            sp.dma_start(a_relt, a["table"].rearrange("a (b h) -> (a b) h", h=AH)).then_inc(q.table_in, 16)
            sp.dma_start(vec[:, :], a["vec"]).then_inc(q.consts_in, 16)
            sp.dma_start(consts[:, :], a["consts"]).then_inc(q.consts_in, 16)
            for c in range(DC):
                sp.dma_start(h[:, c, :], a["x_t"][:, c, :]).then_inc(q.x_in, 16)

            def bias_by_distance(n, dram, rows, tail, parts):
                skewed = [[BAND + 1, P], [2 * S, AH]]
                sp.wait_ge(q.g_rowed, (n + 1) * (1 + AH))
                sp.dma_start(bass.AP(tensor=dram.tensor, offset=0, ap=skewed + [[1, S]]), rows).then_inc(q.g_written, 16)
                sp.dma_start(bass.AP(tensor=dram.tensor, offset=S, ap=skewed + [[1, P]]),
                             tail.unsqueeze(1).broadcast_to([P, AH, P])).then_inc(q.g_written, 16)
                sp.wait_ge(q.g_written, 32 * (n + 1))
                for dst, c in parts:
                    band = bass.AP(tensor=dram.tensor, offset=P - 1 + c, ap=[[BAND, P], [2 * S, AH], [1, S - c]])
                    sp.dma_start(dst, band).then_inc(q.g_read, 16)

            for name, count, floats, per in STREAM:
                src = a["w_" + name]

                def load(k, k_loop=0, waited=None):
                    n = GROUP[name] + k
                    if waited is not None:
                        sp.wait_ge(q.tile_done, waited)
                    sp.dma_start(slots[:, n % 2, 0:floats], src[k + k_loop]).then_inc(landed[n % 2], 16)

                for k in range(min(2, count)):
                    n = GROUP[name] + k
                    load(k, 0, GROUP_END[n - 2] if n >= 2 else None)
                if name == "a_qkv":
                    bias_by_distance(0, ab_dram, a_grow, a_neg,
                                     [(a_bias[:, :, OFF[i]:OFF[i] + LEN[i]], S - LEN[i]) for i in range(NQ)])
                if name == "c_in":
                    bias_by_distance(1, g_dram, c_bias, neg, [(c_bias, 0)])
                loops = max(0, count - 2) // 2
                if loops:
                    with sp.Fori(0, loops) as i:
                        for u in range(2):
                            load(2 + u, 2 * i, GROUP_END[GROUP[name] + u] + 2 * per * i)
                if count > 2 and count % 2:
                    load(count - 1, 0, GROUP_END[GROUP[name] + count - 3])
            sp.wait_ge(q.out_stored, 16 * DC)

        @block.tensor
        def _(pe):
            def norm_sums(name):
                for c in range(DC):
                    pe.wait_ge(q.h_squared, DC * NORM[name] + c + 1)
                    mm = pe.matmul(stat[:, :], ones, sq[:, c, :], start=c == 0, stop=c == DC - 1)
                mm.then_inc(q.h_summed, 1)
                if name != "final":
                    pe.wait_ge(q.h_gained, DC * (NORM[name] + 1))

            def tile(t, parity, blocks, rhs):
                wait(pe, q.tile_taken, t - 1)
                for k, b in enumerate(blocks):
                    mm = pe.matmul(lin[:, parity, :], b, rhs[k], start=k == 0, stop=k == len(blocks) - 1)
                mm.then_inc(q.tile_done, 1)

            def blocks_of(w, first, n):
                return [w[:, (first + k) * P:(first + k + 1) * P] for k in range(n)]

            def linear(name, kc, rhs, groups):
                per = PER[name]

                def turn_(i, us):
                    for u in us:
                        w, s, v = group(name, u)
                        pe.wait_ge(s, v + 16 * i)
                        for j in range(per):
                            t = TILE[name] + u * per + j
                            tile(t + 2 * per * i, t % 2, blocks_of(w, j * kc, kc), rhs)
                if groups >= 2:
                    with pe.Fori(0, groups // 2) as i:
                        turn_(i, (0, 1))
                if groups % 2:
                    turn_(groups // 2, (0,))

            def ple(n):
                name = f"ple{n}"
                pe.wait_ge(q.p_in, 16 * (n + 1))
                with pe.Fori(0, 2) as i:
                    for u in range(2):
                        w, s, v = group(name, u)
                        pe.wait_ge(s, v + 16 * i)
                        for j in range(2):
                            t = TILE[name] + u * 4 + 2 * j
                            tile(t + 8 * i, t % 2, blocks_of(w, j * (DC + 2), DC), [g[:, c, :] for c in range(DC)])
                            tile(t + 1 + 8 * i, (t + 1) % 2, blocks_of(w, j * (DC + 2) + DC, 2),
                                 [p_in_t[:, c, :] for c in range(2)])

            gs = [g[:, c, :] for c in range(DC)]

            def ffn(n):
                norm_sums(f"ffn{n}")
                linear(f"ffn{n}_in", DC, gs, FC)
                pe.wait_ge(q.f_through, FC * (n + 1))
                linear(f"ffn{n}_out", FC, [f_t[:, c, :] for c in range(FC)], DC)

            def turn_weights(src, i, dst_bank):
                for j in range(i + 1):
                    mm = pe.transpose(dst_bank[:, j * P:(j + 1) * P], src[:, j * P:(j + 1) * P], ident)
                return mm

            pe.wait_ge(q.table_in, 48)
            for hd in range(AH):
                b = (scores[:, 0, :], scores[:, 1, :], turn[:, 0, :], turn[:, 1, :])[hd % 4]
                if hd >= 4:
                    pe.wait_ge(q.g_rowed, hd - 2)
                pe.matmul(b, a_relt[:, hd:hd + 1].broadcast_to([BUCKETS, P]), a_onehot, start=True, stop=True)\
                    .then_inc(q.g_made, 1)
            pe.wait_ge(q.consts_in, 32)

            norm_sums("attn0")

            def a_step(s, par, proj, attn, tail):
                def lin_(j):
                    if proj:
                        w, sm, v = group("a_qkv", par)
                        if j == 0:
                            pe.wait_ge(sm, v + 8 * (s - par))
                        tile(TILE["a_qkv"] + 3 * s + j, (TILE["a_qkv"] + 3 * par + j) % 2, blocks_of(w, j * DC, DC), gs)

                def score(i):
                    if attn:
                        hd = s - 1
                        if i == 0:
                            pe.wait_ge(q.a_normed, 2 * hd + 2)
                        wait(pe, q.a_biased, 4 * hd + i)
                        for c in range(2):
                            rows = slice(64 * c, 64 * c + 64)
                            mm = pe.matmul(scores[:, c, 0:LEN[i]], a_qk[rows, 1 - par, 0, i * P:(i + 1) * P],
                                           a_qk[rows, 1 - par, 1, 0:LEN[i]], start=True, stop=True)
                        mm.then_inc(q.a_scored, 1)

                def sums(j):
                    if proj:
                        pe.wait_ge(q.a_squared, 2 * s + j + 1)
                        wait(pe, q.a_logged, 2 * s + j)
                        if j == 0:
                            wait(pe, q.a_ologged, s - 1 if tail else 0)
                        pe.matmul(stat[:, :], ones64, a_sq[:, j, :], start=True, stop=True).then_inc(q.a_summed, 1)

                if proj:
                    lin_(0)
                if tail:
                    pe.wait_ge(q.a_osquared, s - 1)
                    pe.wait_ge(q.a_logged, 2 * s if proj or attn else 2 * AH)
                    pe.matmul(stat[:, :], ones, a_sq[:, 2, :], start=True, stop=True).then_inc(q.a_osummed, 1)
                score(0)
                lin_(1)
                score(1)
                sums(0)
                lin_(2)
                score(2)
                sums(1)
                score(3)
                if proj:
                    pe.wait_ge(q.tile_taken, TILE["a_qkv"] + 3 * s + 3)
                    wait(pe, q.a_otaken, s - 1)
                    for j in range(NQ):
                        mm = pe.transpose(obank[:, j * P:(j + 1) * P], a_raw[:, 2, j * P:(j + 1) * P], ident)
                    mm.then_inc(q.a_vturned, 1)
                if attn:
                    hd = s - 1
                    for i in range(NQ):
                        pe.wait_ge(q.a_weights, 4 * hd + i + 1)
                        wait(pe, q.a_tcopied, 4 * hd + i - 1)
                        turn_weights(a_sc[:, i, 0, :], i, turn[:, i % 2, :]).then_inc(q.a_turned, 1)
                    pe.wait_ge(q.a_vcopied, s + 1 if proj else AH)
                    pe.wait_ge(q.a_tcopied, 4 * hd + 4)
                    for j in range(NQ):
                        mm = pe.matmul(obank[:, j * P:S], a_v[:, 1 - par, j, :], a_pt[:, j, j * P:S],
                                       start=j == 0, stop=j == NQ - 1)
                    mm.then_inc(q.a_pv, 1)

            a_steps(pe, a_step)
            pe.wait_ge(q.a_onormed, AH)
            linear("a_wo", DC, [a_o[:, c, :] for c in range(DC)], 4)
            end_stage(pe, 2)
            ffn(0)
            end_stage(pe, 3)
            norm_sums("ple0")
            ple(0)
            end_stage(pe, 4)

            norm_sums("attn1")
            pe.wait_ge(q.h_gained2, DC)
            g2 = [b_g2[:, c, :] for c in range(DC)]
            for name, k, kc_rhs in (("b_dkv", 0, g2), ("b_dq", 0, gs), ("b_dq", 1, gs)):
                w, s_, v = group(name, k)
                pe.wait_ge(s_, v)
                for j in range(PER[name]):
                    t = TILE[name] + PER[name] * k + j
                    tile(t, t % 2, blocks_of(w, j * DC, DC), kc_rhs)
            for n, (tiles, m) in enumerate((((0, 1), ones), ((2,), ones64), ((3, 4, 5, 6), ones))):
                pe.wait_ge(q.bd_squared, tiles[-1] + 1)
                wait(pe, q.bd_logged, n)
                for t in tiles:
                    mm = pe.matmul(stat[:, :], m, b_dsq[:, t, :], start=t == tiles[0], stop=t == tiles[-1])
                mm.then_inc(q.bd_summed, 1)
            pe.wait_ge(q.bd_normed, 7)
            pe.matmul(obank[:, :], rot, b_rt[:, 0, :], start=True, stop=True).then_inc(q.bd_rotated, 1)
            end_stage(pe, 5)

            def b_step(s, par, proj, attn):
                if proj:
                    w, sm, v = group("b_pair", par)
                    pe.wait_ge(sm, v + 8 * (s - par))
                cq = [b_cq[:, c, :] for c in range(4)]
                ck = [b_ckv[:, c, :] for c in range(2)]
                at_ = (0, 4, 8, 12, 14, 16, 18)

                def lin_(j):
                    if proj:
                        t = TILE["b_pair"] + 7 * par + j
                        tile(TILE["b_pair"] + 7 * s + j, t % 2, blocks_of(w, at_[j], 4 if j < 3 else 2),
                             cq if j < 3 else ck)

                def score(x, i):
                    if attn:
                        n = 8 * (s - 1) + 4 * x + i
                        if x == 0 and i == 0:
                            pe.wait_ge(q.b_normed, 5 * s)
                            pe.wait_ge(q.b_rope, s)
                        wait(pe, q.b_biased, n - 1)
                        qb = slice(i * P, (i + 1) * P)
                        rows = slice(64 * x, 64 * x + 64)
                        pe.matmul(scores[:, i % 2, 0:LEN[i]], b_qn[:, 1 - par, x, qb], b_kn[:, 1 - par, x, 0:LEN[i]],
                                  start=True, stop=False)
                        pe.matmul(scores[:, i % 2, 0:LEN[i]], b_qp[rows, 1 - par, qb], b_kp[rows, 0:LEN[i]],
                                  start=False, stop=True).then_inc(q.b_scored, 1)

                def sums(j):
                    if proj:
                        pe.wait_ge(q.b_squared, 5 * s + j + 1)
                        wait(pe, q.b_logged, 5 * s + j)
                        pe.matmul(stat[:, :], ones64 if j == 2 else ones, b_sq[:, j, :], start=True, stop=True)\
                            .then_inc(q.b_summed, 1)

                lin_(0); score(0, 0); lin_(1); score(0, 1); lin_(2); sums(0); score(0, 2); lin_(3); sums(1)
                score(0, 3); lin_(4); sums(2); score(1, 0); lin_(5); sums(3); score(1, 1); lin_(6); sums(4)
                score(1, 2)
                if proj:
                    pe.wait_ge(q.b_normed, 5 * s + 3)
                    wait(pe, q.b_otaken, 2 * s - 2)
                    wait(pe, q.b_vcopied, 2 * s)
                    pe.matmul(obank[:, :], rot, b_rt[:, 0, :], start=True, stop=True).then_inc(q.b_rotated, 1)
                score(1, 3)
                if proj:
                    for x in range(2):
                        pe.wait_ge(q.tile_taken, TILE["b_pair"] + 7 * s + 6 + x)
                        if x == 0:
                            pe.wait_ge(q.b_rope, s + 1)
                        else:
                            pe.wait_ge(q.b_vcopied, 2 * s + 1)
                        for j in range(NQ):
                            mm = pe.transpose(obank[:, j * P:(j + 1) * P], b_raw[:, 5 + x, j * P:(j + 1) * P], ident)
                        mm.then_inc(q.b_vturned, 1)
                if attn:
                    for x in range(2):
                        n = 8 * (s - 1) + 4 * x
                        for i in range(NQ):
                            pe.wait_ge(q.b_weights, n + i + 1)
                            wait(pe, q.b_tcopied, n + i - 1)
                            turn_weights(b_sc[:, x, i, :], i, turn[:, i % 2, :]).then_inc(q.b_turned, 1)
                        pe.wait_ge(q.b_tcopied, n + 4)
                        if x == 0:
                            pe.wait_ge(q.b_vcopied, 2 * s + 2 if proj else 2 * B_PAIRS)
                            wait(pe, q.b_otaken, 2 * s - 2)
                        else:
                            pe.wait_ge(q.b_otaken, 2 * s - 1)
                        for j in range(NQ):
                            mm = pe.matmul(obank[:, j * P:S], b_v[:, 1 - par, x, j * P:(j + 1) * P], b_pt[:, j, j * P:S],
                                           start=j == 0, stop=j == NQ - 1)
                        mm.then_inc(q.b_pv, 1)

            b_steps(pe, b_step)
            pe.wait_ge(q.b_otaken, BH)
            linear("b_wo", BH, [b_o[:, k, :] for k in range(BH)], DC)
            end_stage(pe, 6)
            ffn(1)
            end_stage(pe, 7)
            norm_sums("ple1")
            ple(1)
            end_stage(pe, 8)
            pe.wait_ge(q.extra_in, 16 * 4)
            for hd in range(CH):
                b = (scores[:, 0, :], scores[:, 1, :], turn[:, 0, :], turn[:, 1, :])[hd % 4]
                if hd >= 4:
                    pe.wait_ge(q.g_rowed, G_ROWED + hd - 2)
                pe.matmul(b, relt[:, hd:hd + 1].broadcast_to([BUCKETS, P]), onehot, start=True, stop=True)\
                    .then_inc(q.g_made, 1)
            norm_sums("mix2")
            linear("c_in", DC, gs, 7)
            w, s_, v = group("c_in_last", 0)
            pe.wait_ge(s_, v)
            for j in range(2):
                tile(TILE["c_in_last"] + j, (TILE["c_in_last"] + j) % 2, blocks_of(w, j * DC, DC), gs)
            end_stage(pe, 9)

            for k in range(4):
                w, s_, v = group("c_cmp", k)
                pe.wait_ge(s_, v)
                pe.wait_ge(q.zp_made, 16)
                t = TILE["c_cmp"] + k
                pe.wait_ge(q.tile_taken, t - 1)
                kv = k // 2
                for c in range(16):
                    mm = pe.matmul(lin[:, t % 2, 0:2 * NCMP], w[:, c * P:(c + 1) * P], c_zp[:, kv, c, :],
                                   start=c == 0, stop=c == 15)
                mm.then_inc(q.tile_done, 1)
            for k in range(NQ):
                mm = pe.transpose(stat[:, k * P:(k + 1) * P], c_z[:, 22, k * P:(k + 1) * P], ident)
            mm.then_inc(q.gates_turned, 1)
            for x in range(2):
                for j in range(NQ):
                    mm = pe.transpose(turn[:, x, j * P:(j + 1) * P], c_z[:, 6 + x, j * P:(j + 1) * P], ident)
                mm.then_inc(q.c_vturned, 1)
            pe.wait_ge(q.hid_act, 4)
            for x in range(2):
                for c in range(2):
                    mm = pe.matmul(obank[64 * x:64 * x + 64, 0:NCMP], w2c[:, c, :],
                                   c_hid[:, c, x * NCMP:(x + 1) * NCMP], start=c == 0, stop=c == 1)
            mm.then_inc(q.kc_made, 1)
            pe.wait_ge(q.kc_copied, 1)
            for x in range(2):
                for c in range(2):
                    mm = pe.matmul(obank[0:NCMP, x * CD:(x + 1) * CD], c_hid[:, 2 + c, x * NCMP:(x + 1) * NCMP],
                                   w2c[:, 2 + c, :], start=c == 0, stop=c == 1)
            mm.then_inc(q.kc_made, 1)
            pe.wait_ge(q.kc_copied, 3)
            for kv in range(2):
                for t in range(4):
                    for i in range(NQ):
                        hd = 4 * kv + t
                        at_ = (t * NQ + i) * NCMP
                        mm = pe.matmul(scores[:, kv, at_:at_ + NCMP], c_z[64 * kv:64 * kv + 64, t, i * P:(i + 1) * P],
                                       c_kc[64 * kv:64 * kv + 64, 0:NCMP], start=True, stop=True)
                mm.then_inc(q.cc_scored, 1)
            for hd in range(CH):
                pe.wait_ge(q.cc_scaled, 1)
                pe.wait_ge(q.c_vcopied, 2)
                wait(pe, q.cc_copied, hd - 1)
                for i in range(NQ):
                    mm = pe.transpose(turn[0:NCMP, hd % 2, i * P:(i + 1) * P], c_cs[:, hd, i, :], ident)
                mm.then_inc(q.cc_turned, 1)
            end_stage(pe, 10)

            for s in range(CH + 1):
                for i in range(NQ):
                    if s < CH:
                        rows = slice(64 * (s // 4), 64 * (s // 4) + 64)
                        wait(pe, q.c_biased, 4 * s + i)
                        for x in range(2):
                            mm = pe.matmul(scores[:, x, 0:LEN[i]], c_z[rows, s % 4, i * P:(i + 1) * P],
                                           c_z[rows, 4 + x, 0:LEN[i]], start=True, stop=True)
                        mm.then_inc(q.c_scored, 1)
                    if s > 0:
                        n = 4 * (s - 1) + i
                        pe.wait_ge(q.c_weights, 2 * n + 2)
                        for x in range(2):
                            wait(pe, q.c_tcopied, 2 * n - 1 + x)
                            turn_weights(c_sc[:, i, x, :], i, turn[:, x, :]).then_inc(q.c_turned, 1)
                if s > 0:
                    hd = s - 1
                    out_rows = slice(64 * (hd % 2), 64 * (hd % 2) + 64)
                    kv = hd // 4
                    pe.wait_ge(q.c_tcopied, 8 * hd + 8)
                    wait(pe, q.c_otaken, hd // 2)
                    for j in range(NQ):
                        for x in range(2):
                            pe.matmul(obank[out_rows, j * P:S], c_v[:, x, j, kv * CD:(kv + 1) * CD],
                                      c_pt[:, x, j, j * P:S], start=j == 0 and x == 0, stop=False)
                    pe.matmul(obank[out_rows, :], c_vc[0:NCMP, kv, :], c_ct[0:NCMP, hd, :],
                              start=False, stop=True).then_inc(q.c_pv, 1)
            end_stage(pe, 11)

            pe.matmul(stat[:, :], walpha[32:48, :], c_z[32:48, 22, :], start=True, stop=True).then_inc(q.gl_alpha, 1)
            pe.wait_ge(q.gl_prod, 3)
            for hd in range(GH):
                rows = slice(GK * hd, GK * hd + GK)
                b = (scores[:, 0, :], scores[:, 1, :], turn[:, 0, :], turn[:, 1, :])[hd]
                for n in range(NCH):
                    ch = slice(n * GCH, (n + 1) * GCH)
                    mm = pe.matmul(b[64 * (n % 2):64 * (n % 2) + 64, (n // 2) * GCH:(n // 2 + 1) * GCH],
                                   gl_kt[rows, ch], gl_qt[rows, ch], start=True, stop=True)
                mm.then_inc(q.gl_att, 1)
            for j in range(NQ):
                mm = pe.transpose(obank[:, j * P:(j + 1) * P], gl_kd[:, j * P:(j + 1) * P], ident)
            mm.then_inc(q.gl_kdt, 1)
            for x in range(2):
                for j in range(NQ):
                    mm = pe.transpose(lin[:, x, j * P:(j + 1) * P], c_z[:, 18 + x, j * P:(j + 1) * P], ident)
                mm.then_inc(q.gl_kdt, 1)
            pe.wait_ge(q.gl_kdc, 3)
            pe.wait_ge(q.gl_attc, 4)
            for n in range(NCH):
                rows = slice(64 * (n % 2), 64 * (n % 2) + 64)
                b = (scores[:, 0, :], scores[:, 1, :])[n % 2]
                if n >= 2:
                    pe.wait_ge(q.gl_uc, 4 * (n - 1))
                mm = pe.matmul(b[:, 0:2 * P], gl_kdt[rows, n // 2, :], gl_vt[rows, n // 2, :], start=True, stop=True)
                mm.then_inc(q.gl_u, 1)
            pe.wait_ge(q.gl_mask, 2)
            for x in range(2):
                for odd in range(2):
                    rows = slice(64 * odd, 64 * odd + 64)
                    b = (lin[:, 0, :], lin[:, 1, :], turn[:, 0, :], turn[:, 1, :])[2 * x + odd]
                    for y in range(2):
                        for n2 in range(NCH // 2):
                            mm = pe.matmul(b[64 * y:64 * y + 64, n2 * GCH:(n2 + 1) * GCH],
                                           gl_vt[rows, n2, (2 * x + y) * GV:(2 * x + y + 1) * GV],
                                           gl_am[rows, 2 * x + y, n2, :], start=True, stop=True)
                    mm.then_inc(q.gl_out, 1)
            pe.wait_ge(q.gl_bd, 4)
            for x in range(2):
                b = (stat, obank)[x]
                for n in range(NCH):
                    ch = slice(n * GCH, (n + 1) * GCH)
                    mm = pe.matmul(b[:, ch], gl_bds[:, n, x * P:(x + 1) * P], gl_qt[:, ch], start=True, stop=True)
                mm.then_inc(q.gl_out, 1)
            for x in range(2):
                pe.wait_ge(q.gl_sq, x + 1)
                pe.wait_ge(q.gl_sum, 2)
                wait(pe, q.gl_log, x)
                pe.matmul(stat[:, :], ones64, gl_s[:, x, :], start=True, stop=True).then_inc(q.gl_ss, 1)
            pe.wait_ge(q.gl_log, 2)
            pe.wait_ge(q.conv_step, 2 * CW)
            for x in range(2):
                mm = pe.matmul(stat[:, :], ones, c_acc[:, x, :], start=x == 0, stop=x == 1)
            mm.then_inc(q.ln_mean, 1)
            pe.wait_ge(q.ln_sq, 2)
            for x in range(2):
                mm = pe.matmul(obank[:, :], ones, gl_s[:, x, :], start=x == 0, stop=x == 1)
            mm.then_inc(q.ln_var, 1)
            end_stage(pe, 12)
            linear("c_out", DC, gs, 4)
            end_stage(pe, 13)
            norm_sums("ffn2")
            linear("ffn2_in", DC, gs, FC)
            pe.wait_ge(q.f_through, FC * 3)
            linear("ffn2_out", FC, [f_t[:, c, :] for c in range(FC)], DC)
            end_stage(pe, 14)
            norm_sums("ple2")
            ple(2)
            end_stage(pe, 15)
            norm_sums("final")


        @block.vector
        def _(ve):
            def gains(name, out=g, signal=None, vname=None):
                for c in range(DC):
                    ve.tensor_scalar(out[:, c, :], h[:, c, :], v1(vname or name, c), None, ALU.mult)\
                        .then_inc(signal or q.h_gained, 1)

            def residual(name):
                t = TILE[name]
                with ve.Fori(0, DC // 2) as i:
                    for u in range(2):
                        ve.wait_ge(q.tile_done, 2 * i + t + u + 1)
                        ve.tensor_tensor(h[:, 2 * i + u, :], lin[:, (t + u) % 2, :], h[:, 2 * i + u, :], ALU.add)\
                            .then_inc(q.tile_taken, 1)

            def take(t, par, dst):
                ve.wait_ge(q.tile_done, t + 1)
                ve.tensor_tensor(dst, lin[:, par, :], r[:, :], ALU.mult).then_inc(q.tile_taken, 1)

            def bias_of_any_positions():
                def built(ins, value):
                    ins.then_inc(q.bias_built, 1)
                    ve.wait_ge(q.bias_built, value)

                ve.wait_ge(q.table_in, 48)
                built(ve.tensor_tensor(a_diff[:, AH:], a_tab[:, AH:], a_tab[:, 0:(BUCKETS - 1) * AH], ALU.subtract), 1)
                for i in range(NQ):
                    ve.tensor_scalar(a_dist[:, OFF[i]:OFF[i] + LEN[i]], posf[:, 0:LEN[i]], -1.0, posq[:, i:i + 1],
                                     ALU.mult, ALU.add).then_inc(q.bias_built, 1)
                    for hd in range(AH):
                        ve.tensor_scalar(a_bias[:, hd, OFF[i]:OFF[i] + LEN[i]], maskt[:, S - LEN[i]:S],
                                         a_tab[:, hd:hd + 1], None, ALU.add).then_inc(q.bias_built, 1)
                base = 1 + NQ * (1 + AH)
                with ve.Fori(0, BUCKETS - 1) as b:
                    ve.wait_ge(q.bias_built, base + (1 + AH) * b)
                    ve.tensor_scalar(a_mask, a_dist, vec[:, bass.ds(VEC["t5_start"] + b, 1)], None, ALU.is_ge)\
                        .then_inc(q.bias_built, 1)
                    ve.wait_ge(q.bias_built, base + 1 + (1 + AH) * b)
                    for hd in range(AH):
                        ve.scalar_tensor_tensor(out=a_bias[:, hd, :], in0=a_mask, scalar=a_diff[:, bass.ds(AH * b + AH + hd, 1)],
                                                in1=a_bias[:, hd, :], op0=ALU.mult, op1=ALU.add).then_inc(q.bias_built, 1)
                ve.wait_ge(q.bias_built, base + (1 + AH) * (BUCKETS - 1))

            def conv_ffn(n):
                gains(f"ffn{n}")
                ve.wait_ge(q.r_ready, NORM[f"ffn{n}"] + 1)
                t0, f0 = TILE[f"ffn{n}_in"], 2 * FC * n

                def pair(i, u):
                    for j in range(2):
                        k = 2 * u + j
                        ve.wait_ge(q.tile_done, t0 + k + 1 + 4 * i)
                        wait(ve, q.f_first, f0 + 4 * i + k - 3)
                        ve.tensor_tensor(f_u[:, k, 2:S + 2], lin[:, (t0 + k) % 2, :], r[:, :], ALU.mult)\
                            .then_inc(q.tile_taken, 1)
                    for j in range(2):
                        k = 2 * u + j
                        w = VEC[f"conv{n}"] + 4 * k + 16 * i
                        ve.wait_ge(q.f_first, f0 + k + 1 + 4 * i)
                        ve.scalar_tensor_tensor(out=f_c[:, k, :], in0=f_u[:, k, 1:S + 1], scalar=vec[:, bass.ds(w + 1, 1)],
                                                in1=f_c[:, k, :], op0=ALU.mult, op1=ALU.add).then_inc(q.f_conv, 1)
                        ve.wait_ge(q.f_conv, 2 * f0 + 2 * k + 1 + 8 * i)
                        ve.scalar_tensor_tensor(out=f_c[:, k, :], in0=f_u[:, k, 0:S], scalar=vec[:, bass.ds(w, 1)],
                                                in1=f_c[:, k, :], op0=ALU.mult, op1=ALU.add).then_inc(q.f_conv, 1)
                    ve.wait_ge(q.f_silu, FC * n + u + 1 + 2 * i)
                    ve.wait_ge(q.f_conv, 2 * f0 + 4 * u + 4 + 8 * i)
                    ve.tensor_tensor(f_t[:, 2 * i + u, :], f_c[:, 2 * u, :], f_sg[:, u, :], ALU.mult)\
                        .then_inc(q.f_through, 1)

                ve.memset(f_u[:, :, 0:2], 0.0).then_inc(q.setup_step, 1)
                ve.wait_ge(q.setup_step, SETUP + n + 1)
                pair(0, 0)
                pair(0, 1)
                with ve.Fori(1, FC // 2) as i:
                    pair(i, 0)
                    pair(i, 1)
                residual(f"ffn{n}_out")

            def ple(n):
                gains(f"ple{n}")
                ve.wait_ge(q.r_ready, NORM[f"ple{n}"] + 1)
                t0, g0 = TILE[f"ple{n}"], DC * n

                def one(i, j):
                    b = j % 2
                    ve.wait_ge(q.tile_done, t0 + 2 * j + 1 + 8 * i)
                    ve.tensor_tensor(p_gp[:, b, :], lin[:, (t0 + 2 * j) % 2, :], r[:, :], ALU.mult)\
                        .then_inc(q.tile_taken, 1)
                    ve.wait_ge(q.tile_done, t0 + 2 * j + 2 + 8 * i)
                    ve.wait_ge(q.ple_sigmoid, g0 + j + 1 + 4 * i)
                    ve.tensor_tensor(p_t[:, b, :], lin[:, (t0 + 2 * j + 1) % 2, :], p_sg[:, b, :], ALU.mult)\
                        .then_inc(q.tile_taken, 1)
                    ve.wait_ge(q.tile_taken, t0 + 2 * j + 2 + 8 * i)
                    ve.tensor_tensor(h[:, 4 * i + j, :], h[:, 4 * i + j, :], p_t[:, b, :], ALU.add)\
                        .then_inc(q.residual_added, 1)
                with ve.Fori(0, 2) as i:
                    for j in range(4):
                        one(i, j)

            steps = [0]

            def did(ins):
                steps[0] += 1
                ins.then_inc(q.setup_step, 1)
                ve.wait_ge(q.setup_step, steps[0])

            ve.memset(a_neg, NEG).then_inc(q.g_rowed, 1)
            did(ve.memset(eps[:, :], EPS))
            for hd in range(AH):
                ve.wait_ge(q.g_made, hd + 1)
                b = (scores[:, 0, :], scores[:, 1, :], turn[:, 0, :], turn[:, 1, :])[hd % 4]
                ve.tensor_copy(a_grow[:, hd, :], b).then_inc(q.g_rowed, 1)
            ve.wait_ge(q.consts_in, 32)
            ve.wait_ge(q.x_in, 16 * DC)
            gains("attn0")
            ve.wait_ge(q.positions_in, 16 * (NQ + 1))
            did(ve.tensor_copy(posf, pos_i))
            did(ve.tensor_copy(posq, posq_i[:, :]))
            did(ve.tensor_tensor(a_step_ok, posf[:, 1:S], posf[:, 0:S - 1], ALU.subtract))
            did(ve.tensor_scalar(a_step_ok, a_step_ok, 1.0, None, ALU.is_equal))
            did(ve.tensor_reduce(regular[:, 0:1], a_step_ok, AX.X, ALU.min))
            did(ve.tensor_copy(regular_i[:, :], regular[:, 0:1]))
            ve.wait_ge(q.lam_in, 16)
            for x in range(2):
                did(ve.tensor_tensor(a_lam[:, 4, :], a_lam[:, 2 * x, :], a_lam[:, 2 * x + 1, :], ALU.mult))
                did(ve.tensor_reduce(lamd[:, x:x + 1], a_lam[:, 4, :], AX.X, ALU.add))
            ve.sem_inc(q.lam_dots, 1)
            turn_parts = (6.28125, 0.0019340515136718750, 2 * math.pi - 6.28125 - 0.0019340515136718750)
            ang, k_ = cosb[:, :], a_rawo
            did(ve.tensor_scalar(ang, posf, v1("inv_freq"), None, ALU.mult))
            did(ve.tensor_scalar(k_, ang, 1 / (2 * math.pi), 12582912.0, ALU.mult, ALU.add))
            did(ve.tensor_scalar(k_, k_, 12582912.0, None, ALU.subtract))
            for part in turn_parts:
                did(ve.scalar_tensor_tensor(out=ang, in0=k_, scalar=-part, in1=ang, op0=ALU.mult, op1=ALU.add))
            did(ve.tensor_scalar(sinb[:, :], ang, PI_IN, -PI_IN, ALU.min, ALU.max))
            did(ve.tensor_scalar(ang, ang, math.pi / 2, None, ALU.add))
            did(ve.tensor_scalar(k_, ang, math.pi, -2 * math.pi, ALU.is_gt, ALU.mult))
            did(ve.tensor_tensor(ang, ang, k_, ALU.add))
            did(ve.tensor_scalar(ang, ang, PI_IN, -PI_IN, ALU.min, ALU.max))
            ve.sem_inc(q.angles_ready, 1)
            ve.wait_ge(q.lam_exps, 1)
            did(ve.tensor_tensor(nlam, lame[:, 1:2], lame[:, 0:1], ALU.subtract))
            did(ve.tensor_scalar(nlam, nlam, LAM_INIT, None, ALU.subtract))
            did(ve.tensor_scalar(asub, v1("a_sub"), 1.0 - LAM_INIT, None, ALU.mult))
            SETUP = steps[0]
            ve.wait_ge(q.g_read, 16 * NQ)
            in_a_row = ve.value_load(regular_i[0:1, 0:1])
            with ve.If(in_a_row < 1):
                bias_of_any_positions()
            ve.wait_ge(q.r_ready, 1)

            def a_step(s, par, proj, attn, tail):
                hd = s - 1

                def take_(j):
                    if proj:
                        take(TILE["a_qkv"] + 3 * s + j, (TILE["a_qkv"] + 3 * par + j) % 2, a_raw[:, j, :])

                def biased(i):
                    if attn:
                        n = 4 * hd + i
                        ve.wait_ge(q.a_scored, n + 1)
                        wait(ve, q.a_turned, n - 3)
                        bias = a_bias[:, hd, OFF[i]:OFF[i] + LEN[i]] if isinstance(hd, int) else \
                            a_bias[:, bass.ds(hd, 1), OFF[i]:OFF[i] + LEN[i]].rearrange("p a l -> p (a l)")
                        ve.scalar_tensor_tensor(out=a_sc[:, i, :, 0:LEN[i]], in0=scores[:, :, 0:LEN[i]],
                                                scalar=-(AQK ** -0.5),
                                                in1=bias.unsqueeze(1).broadcast_to([P, 2, LEN[i]]),
                                                op0=ALU.mult, op1=ALU.subtract).then_inc(q.a_biased, 1)
                        ve.wait_ge(q.a_biased, n + 1)
                        ve.tensor_reduce(nmax[:, 2 * i:2 * i + 2], a_sc[:, i, :, 0:LEN[i]], AX.X, ALU.min)\
                            .then_inc(q.a_min, 1)

                def weights_(i):
                    if attn:
                        n = 4 * hd + i
                        d = den[:, 2 * i:2 * i + 2]
                        ve.wait_ge(q.a_exped, 2 * n + 2)
                        ve.reciprocal(d, d).then_inc(q.a_recip, 1)
                        ve.wait_ge(q.a_recip, 2 * n + 1)
                        ve.tensor_tensor(d[:, 1:2], d[:, 1:2], nlam, ALU.mult).then_inc(q.a_recip, 1)
                        ve.tensor_scalar(a_sc[:, i, 0, 0:LEN[i]], a_sc[:, i, 0, 0:LEN[i]], d[:, 0:1], None, ALU.mult)\
                            .then_inc(q.a_scaled, 1)
                        ve.wait_ge(q.a_recip, 2 * n + 2)
                        ve.wait_ge(q.a_scaled, n + 1)
                        ve.scalar_tensor_tensor(out=a_sc[:, i, 0, 0:LEN[i]], in0=a_sc[:, i, 1, 0:LEN[i]],
                                                scalar=d[:, 1:2], in1=a_sc[:, i, 0, 0:LEN[i]], op0=ALU.mult,
                                                op1=ALU.add).then_inc(q.a_weights, 1)

                def normed(j):
                    if proj:
                        ve.wait_ge(q.a_factor, 2 * s + j + 1)
                        ve.scalar_tensor_tensor(out=a_qk[:, par, j, :], in0=a_raw[:, j, :],
                                                scalar=v1("a_q" if j == 0 else "a_k"), in1=a_ri[:, j, :],
                                                op0=ALU.mult, op1=ALU.mult).then_inc(q.a_normed, 1)

                take_(0)
                if tail:
                    ve.wait_ge(q.a_ofactor, s - 1)
                    ve.scalar_tensor_tensor(out=a_o[:, s - 2, :], in0=a_rawo, scalar=asub, in1=a_ri[:, 2, :],
                                            op0=ALU.mult, op1=ALU.mult).then_inc(q.a_onormed, 1)
                biased(0)
                take_(1)
                biased(1)
                weights_(0)
                normed(0)
                take_(2)
                biased(2)
                weights_(1)
                normed(1)
                biased(3)
                weights_(2)
                weights_(3)
                if attn:
                    ve.wait_ge(q.a_pv, s)
                    ve.tensor_copy(a_rawo, obank[:, :]).then_inc(q.a_otaken, 1)

            a_steps(ve, a_step)
            residual("a_wo")
            end_stage(ve, 2)
            conv_ffn(0)
            end_stage(ve, 3)
            ple(0)
            end_stage(ve, 4)

            gains("kv", b_g2, q.h_gained2)
            gains("attn1")
            ve.wait_ge(q.r_ready, NORM["attn1"] + 1)
            t0 = TILE["b_dkv"]
            for j in range(7):
                take(t0 + j, (t0 + j) % 2, b_cr[:, j, :])
            for n, (tiles, vname) in enumerate((((0, 1), "ckv"), ((2,), "k_pe"), ((3, 4, 5, 6), "cq"))):
                ve.wait_ge(q.bd_factor, n + 1)
                for k, j in enumerate(tiles):
                    dst = (b_ckv, b_rt, b_cq)[n][:, k, :]
                    ve.scalar_tensor_tensor(out=dst, in0=b_cr[:, j, :], scalar=v1(vname, k), in1=b_ri[:, n, :],
                                            op0=ALU.mult, op1=ALU.mult).then_inc(q.bd_normed, 1)
            ve.wait_ge(q.bd_rotated, 1)
            ve.tensor_tensor(b_rt[:, 1, :], obank[:, :], sinb[:, :], ALU.mult).then_inc(q.bd_terms, 1)
            ve.tensor_tensor(b_rt[:, 2, :], b_rt[:, 0, :], cosb[:, :], ALU.mult).then_inc(q.bd_terms, 1)
            ve.wait_ge(q.bd_terms, 2)
            ve.tensor_tensor(b_kp, b_rt[:, 1, :], b_rt[:, 2, :], ALU.add).then_inc(q.bd_terms, 1)
            end_stage(ve, 5)

            def b_step(s, par, proj, attn):
                def take_(j):
                    if proj:
                        ve.wait_ge(q.tile_done, TILE["b_pair"] + 7 * s + j + 1)
                        ve.tensor_copy(b_raw[:, j, :], lin[:, (TILE["b_pair"] + 7 * par + j) % 2, :])\
                            .then_inc(q.tile_taken, 1)

                def biased(x, i):
                    if attn:
                        n = 8 * (s - 1) + 4 * x + i
                        ve.wait_ge(q.b_scored, n + 1)
                        wait(ve, q.b_turned, n - 7)
                        ve.scalar_tensor_tensor(out=b_sc[:, x, i, 0:LEN[i]], in0=scores[:, i % 2, 0:LEN[i]],
                                                scalar=-((NOPE + ROPE) ** -0.5), in1=maskt[:, S - LEN[i]:S],
                                                op0=ALU.mult, op1=ALU.subtract).then_inc(q.b_biased, 1)
                        ve.wait_ge(q.b_biased, n + 1)
                        ve.tensor_reduce(nmax[:, 4 * x + i:4 * x + i + 1], b_sc[:, x, i, 0:LEN[i]], AX.X, ALU.min)\
                            .then_inc(q.b_min, 1)

                def weights_(x, i):
                    if attn:
                        n = 8 * (s - 1) + 4 * x + i
                        d = den[:, 4 * x + i:4 * x + i + 1]
                        ve.wait_ge(q.b_exped, n + 1)
                        ve.reciprocal(d, d).then_inc(q.b_recip, 1)
                        ve.wait_ge(q.b_recip, n + 1)
                        ve.tensor_scalar(b_sc[:, x, i, 0:LEN[i]], b_sc[:, x, i, 0:LEN[i]], d, None, ALU.mult)\
                            .then_inc(q.b_weights, 1)

                def normed(j):
                    if proj:
                        ve.wait_ge(q.b_factor, 5 * s + j + 1)
                        dst = (b_qn[:, par, 0, :], b_qn[:, par, 1, :], b_rt[:, 0, :], b_kn[:, par, 0, :],
                               b_kn[:, par, 1, :])[j]
                        vname = ("q_nope", "q_nope", "q_pe", "k_nope", "k_nope")[j]
                        ve.scalar_tensor_tensor(out=dst, in0=b_raw[:, j, :], scalar=v1(vname), in1=b_ri[:, j, :],
                                                op0=ALU.mult, op1=ALU.mult).then_inc(q.b_normed, 1)

                take_(0); biased(0, 0); take_(1); biased(0, 1); weights_(0, 0); take_(2); biased(0, 2)
                weights_(0, 1); normed(0); take_(3); biased(0, 3); weights_(0, 2); normed(1); take_(4)
                biased(1, 0); weights_(0, 3); normed(2); take_(5); biased(1, 1); weights_(1, 0); normed(3)
                take_(6); biased(1, 2); weights_(1, 1); normed(4)
                if proj:
                    ve.wait_ge(q.b_rotated, s + 1)
                    ve.tensor_tensor(b_rt[:, 1, :], obank[:, :], sinb[:, :], ALU.mult).then_inc(q.b_terms, 1)
                    ve.tensor_tensor(b_rt[:, 2, :], b_rt[:, 0, :], cosb[:, :], ALU.mult).then_inc(q.b_terms, 1)
                    ve.wait_ge(q.b_terms, 2 * s + 2)
                    ve.tensor_tensor(b_qp[:, par, :], b_rt[:, 1, :], b_rt[:, 2, :], ALU.add).then_inc(q.b_rope, 1)
                biased(1, 3); weights_(1, 2); weights_(1, 3)
                if attn:
                    for x in range(2):
                        ve.wait_ge(q.b_pv, 2 * s - 1 + x)
                        ve.tensor_copy(b_o[:, 2 * (s - 1) + x, :], obank[:, :]).then_inc(q.b_otaken, 1)

            b_steps(ve, b_step)
            residual("b_wo")
            end_stage(ve, 6)
            conv_ffn(1)
            end_stage(ve, 7)
            ple(1)
            end_stage(ve, 8)

            gains("mix2")
            ve.memset(neg, NEG).then_inc(q.g_rowed, 1)
            for hd in range(CH):
                ve.wait_ge(q.g_made, AH + hd + 1)
                b = (scores[:, 0, :], scores[:, 1, :], turn[:, 0, :], turn[:, 1, :])[hd % 4]
                ve.tensor_copy(c_bias[:, hd, :], b).then_inc(q.g_rowed, 1)
            ve.wait_ge(q.r_ready, NORM["mix2"] + 1)
            t0 = TILE["c_in"]
            assert TILE["c_in_last"] == t0 + 21

            def c_take(j, jj):
                ve.wait_ge(q.tile_done, t0 + j + 1)
                ve.tensor_tensor(c_z[:, j, :], lin[:, (t0 + jj) % 2, :], r[:, :], ALU.mult).then_inc(q.tile_taken, 1)
            with ve.Fori(0, 11) as i:
                for u in range(2):
                    c_take(2 * i + u, u)
            c_take(22, 22)
            ve.memset(c_hp[:, :, 0:CW - 1], 0.0).then_inc(q.c_glu, 1)
            for x in range(2):
                ve.wait_ge(q.c_sigmoid, x + 1)
                ve.tensor_tensor(c_hp[:, x, CW - 1:], c_z[:, 12 + x, :], c_acc[:, x, :], ALU.mult)\
                    .then_inc(q.c_glu, 1)
            end_stage(ve, 9)

            for k in range(4):
                z = c_z[:, 8 + k, :].rearrange("p (n l) -> p l n", l=CMPS)
                for half in range(2):
                    rows = slice(64 * half, 64 * half + 64)
                    for over in range(2):
                        pos = vec[rows, VEC["cmp_pos"] + 16 * (k // 2) + 8 * over:VEC["cmp_pos"] + 16 * (k // 2) + 8 * over + 8]
                        ins = ve.tensor_tensor(c_zp[rows, k // 2, 8 * over:8 * over + 8, (k % 2) * NCMP:(k % 2 + 1) * NCMP],
                                               z[rows, half::2, over:over + NCMP],
                                               pos.unsqueeze(2).broadcast_to([64, 8, NCMP]), ALU.add)
                        ins.then_inc(q.zp_made, 1)
            for k in range(4):
                t = TILE["c_cmp"] + k
                ve.wait_ge(q.tile_done, t + 1)
                ve.tensor_copy(c_hid[:, k, :], lin[:, t % 2, 0:2 * NCMP]).then_inc(q.tile_taken, 1)
            ve.memset(c_cb[:, :, :, :], NEG).then_inc(q.cb_made, 1)
            ve.wait_ge(q.cb_made, 1)
            ve.wait_ge(q.g_read, G_READ + 16)
            for i in range(NQ):
                n = min(NCMP, 7 + 8 * i)
                first = S - P - P * i + CMPB - 1
                ve.tensor_copy(c_cb[:, :, i, 0:n], c_bias[:, :, first:first + CMPS * (n - 1) + 1:CMPS]).then_inc(q.cb_made, 1)
            ve.wait_ge(q.cb_made, 1 + NQ)
            ve.wait_ge(q.kc_made, 1)
            ve.tensor_copy(c_kc[:, 0:NCMP], obank[:, 0:NCMP]).then_inc(q.kc_copied, 1)
            ve.wait_ge(q.kc_made, 2)
            for x in range(2):
                ve.tensor_copy(c_vc[0:NCMP, x, :], obank[0:NCMP, x * CD:(x + 1) * CD]).then_inc(q.kc_copied, 1)
            for kv in range(2):
                ve.wait_ge(q.cc_scored, kv + 1)
                ve.scalar_tensor_tensor(
                    out=c_cs[:, 4 * kv:4 * kv + 4, :, :].rearrange("p h i n -> p (h i n)"), in0=scores[:, kv, 0:4 * NQ * NCMP],
                    scalar=-(CD ** -0.5), in1=c_cb[:, 4 * kv:4 * kv + 4, :, :].rearrange("p h i n -> p (h i n)"),
                    op0=ALU.mult, op1=ALU.subtract).then_inc(q.cc_biased, 1)
            ve.wait_ge(q.cc_biased, 2)
            cs3 = c_cs[:, :, :, :].rearrange("p h i n -> p (h i) n")
            ve.tensor_reduce(c_cmin, cs3, AX.X, ALU.min).then_inc(q.cc_min, 1)
            ve.wait_ge(q.cc_min, 1)
            ve.tensor_tensor(cs3, cs3, c_cmin.unsqueeze(2).broadcast_to([P, CH * NQ, NCMP]), ALU.subtract)\
                .then_inc(q.cc_sub, 1)
            ve.wait_ge(q.cc_exped, 1)
            ve.tensor_reduce(c_cden, cs3, AX.X, ALU.add).then_inc(q.cc_sum, 1)
            ve.wait_ge(q.cc_sum, 1)
            ve.reciprocal(c_cden, c_cden).then_inc(q.cc_recip, 1)
            ve.wait_ge(q.cc_recip, 1)
            ve.wait_ge(q.gates_made, 1)
            d3 = c_cden.rearrange("p (h i) -> p h i", i=NQ)
            ve.tensor_tensor(d3, d3, c_ga[:, :, :].rearrange("p i (h b) -> p h i b", b=3)[:, :, :, 0], ALU.mult)\
                .then_inc(q.cc_recip, 1)
            ve.wait_ge(q.cc_recip, 2)
            ve.tensor_scalar(d3[:, :, 0], d3[:, :, 0], v1("first_block"), None, ALU.mult).then_inc(q.cc_recip, 1)
            ve.wait_ge(q.cc_recip, 3)
            ve.tensor_tensor(cs3, cs3, c_cden.unsqueeze(2).broadcast_to([P, CH * NQ, NCMP]), ALU.mult)\
                .then_inc(q.cc_scaled, 1)
            end_stage(ve, 10)

            def conv_tap(k):
                x, j = k % 2, k // 2
                if j == 0:
                    ve.wait_ge(q.c_glu, 3)
                    ve.tensor_scalar(c_acc[:, x, :], c_hp[:, x, 0:S], v1("dw", CW * x), v1("dw_b", x), ALU.mult,
                                     ALU.add).then_inc(q.conv_step, 1)
                elif j < CW:
                    ve.wait_ge(q.conv_step, k - 1)
                    ve.scalar_tensor_tensor(out=c_acc[:, x, :], in0=c_hp[:, x, j:j + S], scalar=v1("dw", CW * x + j),
                                            in1=c_acc[:, x, :], op0=ALU.mult, op1=ALU.add).then_inc(q.conv_step, 1)

            for s in range(CH):
                def weights_(i):
                    n = 4 * s + i
                    d = den[:, 2 * i:2 * i + 2]
                    ve.wait_ge(q.c_exped, 2 * n + 2)
                    ve.reciprocal(d, d).then_inc(q.c_recip, 1)
                    ve.wait_ge(q.c_recip, n + 1)
                    ve.tensor_tensor(d, d, c_ga[:, i, 3 * s + 1:3 * s + 3], ALU.mult).then_inc(q.c_gated, 1)
                    ve.wait_ge(q.c_gated, n + 1)
                    for x in range(2):
                        ve.tensor_scalar(c_sc[:, i, x, 0:LEN[i]], c_sc[:, i, x, 0:LEN[i]], d[:, x:x + 1], None,
                                         ALU.mult).then_inc(q.c_weights, 1)

                for i in range(NQ):
                    n = 4 * s + i
                    ve.wait_ge(q.c_scored, n + 1)
                    wait(ve, q.c_turned, 2 * n - 6)
                    ve.scalar_tensor_tensor(out=c_sc[:, i, :, 0:LEN[i]], in0=scores[:, :, 0:LEN[i]], scalar=-(CD ** -0.5),
                                            in1=c_bias[:, s:s + 1, S - LEN[i]:S].broadcast_to([P, 2, LEN[i]]),
                                            op0=ALU.mult, op1=ALU.subtract).then_inc(q.c_biased, 1)
                    ve.wait_ge(q.c_biased, n + 1)
                    ve.tensor_reduce(nmax[:, 2 * i:2 * i + 2], c_sc[:, i, :, 0:LEN[i]], AX.X, ALU.min).then_inc(q.c_min, 1)
                    if i:
                        weights_(i - 1)
                    for k in range(2):
                        conv_tap(8 * s + 2 * i + k)
                weights_(3)
                if s % 2 and s >= 3:
                    ve.wait_ge(q.c_pv, s - 1)
                    ve.tensor_copy(g[:, (s - 3) // 2, :], obank[:, :]).then_inc(q.c_otaken, 1)
            ve.wait_ge(q.c_pv, CH)
            ve.tensor_copy(g[:, 3, :], obank[:, :]).then_inc(q.c_otaken, 1)
            end_stage(ve, 11)

            ve.memset(gl_reset, 1.0).then_inc(q.gl_scale, 1)
            ve.wait_ge(q.gl_scale, 1)
            ve.memset(gl_reset.rearrange("p (n c) -> p n c", c=GCH)[:, :, 0:1], 0.0).then_inc(q.gl_scale, 1)
            ve.memset(gl_bds[:, :, :], 0.0).then_inc(q.gl_scale, 1)
            ve.wait_ge(q.gl_ln, 1)
            ve.scalar_tensor_tensor(out=gl_b, in0=gl_e[:, 1, :], scalar=0.0, in1=gl_e[:, 0, :], op0=ALU.min,
                                    op1=ALU.subtract).then_inc(q.gl_la, 1)
            ve.wait_ge(q.gl_la, 1)
            ve.tensor_scalar(gl_e[:, 0, :], gl_b, 1.0 / TAU, None, ALU.mult).then_inc(q.gl_la, 1)
            ve.wait_ge(q.gl_la, 2)
            ve.wait_ge(q.gl_scale, 3)
            ve.tensor_tensor_scan(gl_b, gl_reset, gl_e[:, 0, :], 0.0, ALU.mult, ALU.add).then_inc(q.gl_scan, 1)
            ve.wait_ge(q.gl_scan, 1)
            b3 = gl_b.rearrange("p (n c) -> p n c", c=GCH)
            ve.tensor_tensor(gl_e[:, 0, :].rearrange("p (n c) -> p n c", c=GCH), b3[:, :, GCH - 1:GCH].broadcast_to([P, NCH, GCH]),
                             b3, ALU.subtract).then_inc(q.gl_diff, 1)
            ve.wait_ge(q.gl_exps, 4)
            ve.scalar_tensor_tensor(out=gl_qt, in0=c_z[:, 16, :], scalar=GK ** -0.5, in1=gl_t[:, 0, :], op0=ALU.mult,
                                    op1=ALU.mult).then_inc(q.gl_prod, 1)
            ve.tensor_tensor(gl_kt, c_z[:, 17, :], gl_t[:, 1, :], ALU.mult).then_inc(q.gl_prod, 1)
            ve.tensor_tensor(gl_kd, c_z[:, 17, :], gl_e[:, 1, :], ALU.mult).then_inc(q.gl_prod, 1)
            for hd in range(GH):
                b = (scores[:, 0, :], scores[:, 1, :], turn[:, 0, :], turn[:, 1, :])[hd]
                ve.wait_ge(q.gl_att, hd + 1)
                ve.tensor_copy(gl_am[:, hd, :, :].rearrange("p n c -> p (n c)"), b[:, 0:NCH // 2 * GCH])\
                    .then_inc(q.gl_attc, 1)
            ve.wait_ge(q.gl_kdt, 1)
            ve.tensor_copy(gl_kdt[:, :, :].rearrange("p j c -> p (j c)"), obank[:, :]).then_inc(q.gl_kdc, 1)
            for x in range(2):
                ve.wait_ge(q.gl_kdt, 2 + x)
                ve.tensor_copy(gl_vt[:, :, x * P:(x + 1) * P], lin[:, x, :].rearrange("p (j c) -> p j c", c=P))\
                    .then_inc(q.gl_kdc, 1)
            for n in range(NCH):
                b = (scores[:, 0, :], scores[:, 1, :])[n % 2]
                ve.wait_ge(q.gl_u, n + 1)
                for hd in range(GH):
                    rows = slice(GK * hd, GK * hd + GK)
                    ve.tensor_copy(gl_us[rows, n, :], b[rows, hd * GV:(hd + 1) * GV]).then_inc(q.gl_uc, 1)
            ve.wait_ge(q.gl_uc, 4 * NCH)
            ve.memset(gl_st[:, 0, :], 0.0).then_inc(q.gl_state, 1)
            for n in range(1, NCH):
                ve.wait_ge(q.gl_state, n)
                ve.scalar_tensor_tensor(out=gl_st[:, n, :], in0=gl_st[:, n - 1, :], scalar=gl_dn[:, n - 1:n],
                                        in1=gl_us[:, n - 1, :], op0=ALU.mult, op1=ALU.add).then_inc(q.gl_state, 1)
            ve.wait_ge(q.gl_state, NCH)
            for hd in range(GH):
                rows = slice(GK * hd, GK * hd + GK)
                ve.tensor_copy(gl_bds[rows, :, hd * GV:(hd + 1) * GV], gl_st[rows, :, :]).then_inc(q.gl_bd, 1)
            for x in range(2):
                ve.wait_ge(q.gl_out, 5 + x)
                ve.tensor_copy(gl_o[:, x, :], (stat, obank)[x][:, :]).then_inc(q.gl_sum, 1)
            for x in range(2):
                for odd in range(2):
                    b = (lin[:, 0, :], lin[:, 1, :], turn[:, 0, :], turn[:, 1, :])[2 * x + odd]
                    o4 = gl_o[:, x, :].rearrange("p (n o c) -> p n o c", o=2, c=GCH)[:, :, odd, :]
                    ve.wait_ge(q.gl_sum, x + 1)
                    ve.tensor_tensor(o4, b[:, 0:NCH // 2 * GCH].rearrange("p (n c) -> p n c", c=GCH), o4, ALU.add)\
                        .then_inc(q.gl_add, 1)
            for x in range(2):
                ve.wait_ge(q.gl_fac, x + 1)
                ve.scalar_tensor_tensor(out=gl_t[:, x, :], in0=gl_o[:, x, :], scalar=v1("gla_g", x), in1=gl_e[:, x, :],
                                        op0=ALU.mult, op1=ALU.mult).then_inc(q.gl_norm, 1)
                ve.wait_ge(q.gl_norm, x + 1)
                ve.wait_ge(q.gl_silu, x + 1)
                ve.tensor_tensor(g[:, 6 + x, :], gl_t[:, x, :], c_z[:, 20 + x, :], ALU.mult)
            ve.wait_ge(q.ln_mean, 1)
            for x in range(2):
                ve.scalar_tensor_tensor(out=c_acc[:, x, :], in0=stat[:, :], scalar=-1.0 / CC, in1=c_acc[:, x, :],
                                        op0=ALU.mult, op1=ALU.add).then_inc(q.ln_cent, 1)
            for x in range(2):
                ve.wait_ge(q.ln_fac, 1)
                ve.scalar_tensor_tensor(out=gl_o[:, x, :], in0=c_acc[:, x, :], scalar=v1("ln_g", x), in1=gl_e[:, 2, :],
                                        op0=ALU.mult, op1=ALU.mult).then_inc(q.ln_norm, 1)
            end_stage(ve, 12)
            residual("c_out")
            end_stage(ve, 13)

            gains("ffn2")
            ve.wait_ge(q.r_ready, NORM["ffn2"] + 1)
            t0 = TILE["ffn2_in"]

            def gated(i, u):
                ve.wait_ge(q.tile_done, t0 + 2 * u + 1 + 4 * i)
                ve.tensor_tensor(f_c[:, 2 * u, :], lin[:, (t0 + 2 * u) % 2, :], r[:, :], ALU.mult)\
                    .then_inc(q.tile_taken, 1)
                ve.wait_ge(q.tile_done, t0 + 2 * u + 2 + 4 * i)
                ve.tensor_tensor(f_c[:, 2 * u + 1, :], lin[:, (t0 + 2 * u + 1) % 2, :], r[:, :], ALU.mult)\
                    .then_inc(q.tile_taken, 1)
                ve.wait_ge(q.tile_taken, t0 + 2 * u + 2 + 4 * i)
                ve.wait_ge(q.s_gate, u + 1 + 2 * i)
                ve.tensor_tensor(f_t[:, 2 * i + u, :], f_c[:, 2 * u + 1, :], f_sg[:, u, :], ALU.mult)\
                    .then_inc(q.f_through, 1)
            with ve.Fori(0, FC // 2) as i:
                gated(i, 0)
                gated(i, 1)
            residual("ffn2_out")
            end_stage(ve, 14)
            ple(2)
            end_stage(ve, 15)
            ve.wait_ge(q.r_ready, NORM["final"] + 1)
            for c in range(DC):
                ve.scalar_tensor_tensor(out=g[:, c, :], in0=h[:, c, :], scalar=v1("final", c), in1=r[:, :],
                                        op0=ALU.mult, op1=ALU.mult).then_inc(q.residual_added, 1)

        @block.scalar
        def _(ac):
            def factor(name):
                n = NORM[name]
                for c in range(DC):
                    ac.activation(sq[:, c, :], h[:, c, :], ACT.Square).then_inc(q.h_squared, 1)
                ac.wait_ge(q.h_summed, n + 1)
                ac.activation(lnr[:, :], stat[:, :], ACT.Ln, bias=eps[:, 0:1], scale=1.0 / D).then_inc(q.r_logged, 1)
                ac.wait_ge(q.r_logged, n + 1)
                ac.activation(r[:, :], lnr[:, :], ACT.Exp, scale=-0.5).then_inc(q.r_ready, 1)

            def inv_sqrt(dst, n, summed, logged, factor_, summed_v, logged_v):
                ac.wait_ge(summed, summed_v)
                ac.activation(dst, stat[:, :], ACT.Ln, bias=eps[:, 0:1], scale=1.0 / n).then_inc(logged, 1)
                ac.wait_ge(logged, logged_v)
                ac.activation(dst, dst, ACT.Exp, scale=-0.5).then_inc(factor_, 1)

            def conv_ffn(n):
                factor(f"ffn{n}")
                t0, f0 = TILE[f"ffn{n}_in"], 2 * FC * n

                def pair(i, u):
                    for j in range(2):
                        k = 2 * u + j
                        w = VEC[f"conv{n}"] + 4 * k + 16 * i
                        ac.wait_ge(q.tile_taken, t0 + k + 1 + 4 * i)
                        wait(ac, q.f_through, FC * n + 2 * i + u - 1)
                        ac.activation(f_c[:, k, :], f_u[:, k, 2:S + 2], ACT.Identity, bias=vec[:, bass.ds(w + 3, 1)],
                                      scale=vec[:, bass.ds(w + 2, 1)]).then_inc(q.f_first, 1)
                    ac.wait_ge(q.f_conv, 2 * f0 + 4 * u + 4 + 8 * i)
                    ac.activation(f_sg[:, u, :], f_c[:, 2 * u + 1, :], ACT.Silu).then_inc(q.f_silu, 1)
                pair(0, 0)
                pair(0, 1)
                with ac.Fori(1, FC // 2) as i:
                    pair(i, 0)
                    pair(i, 1)

            def ple(n):
                factor(f"ple{n}")
                t0, g0 = TILE[f"ple{n}"], DC * n
                with ac.Fori(0, 2) as i:
                    for j in range(4):
                        ac.wait_ge(q.tile_taken, t0 + 2 * j + 1 + 8 * i)
                        ac.activation(p_sg[:, j % 2, :], p_gp[:, j % 2, :], ACT.Sigmoid).then_inc(q.ple_sigmoid, 1)

            def load_p(n):
                ac.dma_start(p_in_t[:, :, :].rearrange("p c s -> p (c s)"), a["p_t"][n]).then_inc(q.p_in, 16)

            ac.dma_start(pos_i, a["positions"].broadcast_to([P, S])).then_inc(q.positions_in, 16)
            for i in range(NQ):
                ac.dma_start(posq_i[:, i:i + 1], a["positions"][0, i * P:(i + 1) * P].rearrange("(p a) -> p a", a=1))\
                    .then_inc(q.positions_in, 16)
            ac.dma_start(a_lam[:, 0:4, :].rearrange("p k d -> p (k d)"), a["lam"].broadcast_to([P, 4 * AQK])).then_inc(q.lam_in, 16)
            ac.dma_start(a_tab, a["table"].broadcast_to([P, BUCKETS * AH])).then_inc(q.table_in, 16)
            ac.dma_start(walpha[32:48, :], a["w_alpha"]).then_inc(q.extra_in, 16)
            ac.dma_start(w2c[:, :, :].rearrange("p c d -> p (c d)"), a["cmp_w2"]).then_inc(q.extra_in, 16)
            load_p(0)
            ac.wait_ge(q.setup_step, 1)
            ac.wait_ge(q.x_in, 16 * DC)
            factor("attn0")
            ac.wait_ge(q.lam_dots, 1)
            ac.activation(lame, lamd, ACT.Exp).then_inc(q.lam_exps, 1)
            ac.wait_ge(q.angles_ready, 1)
            ac.activation(sinb[:, :], sinb[:, :], ACT.Sin).then_inc(q.trig_ready, 1)
            ac.activation(cosb[:, :], cosb[:, :], ACT.Sin).then_inc(q.trig_ready, 1)

            def a_step(s, par, proj, attn, tail):
                hd = s - 1

                def squared(j):
                    if proj:
                        ac.wait_ge(q.tile_taken, TILE["a_qkv"] + 3 * s + j + 1)
                        ac.activation(a_sq[:, j, :], a_raw[:, j, :], ACT.Square).then_inc(q.a_squared, 1)

                def exps(i):
                    if attn:
                        n = 4 * hd + i
                        ac.wait_ge(q.a_min, n + 1)
                        for x in range(2):
                            e = a_sc[:, i, x, 0:LEN[i]]
                            ac.activation(e, e, ACT.Exp, bias=nmax[:, 2 * i + x:2 * i + x + 1], scale=-1.0,
                                          accum_out=den[:, 2 * i + x:2 * i + x + 1]).then_inc(q.a_exped, 1)

                def factor_(j):
                    if proj:
                        inv_sqrt(a_ri[:, j, :], AQK, q.a_summed, q.a_logged, q.a_factor, 2 * s + j + 1, 2 * s + j + 1)

                if tail:
                    ac.wait_ge(q.a_otaken, s - 1)
                    ac.activation(a_sq[:, 2, :], a_rawo, ACT.Square).then_inc(q.a_osquared, 1)
                squared(0)
                if tail:
                    inv_sqrt(a_ri[:, 2, :], 2 * AQK, q.a_osummed, q.a_ologged, q.a_ofactor, s - 1, s - 1)
                exps(0)
                squared(1)
                exps(1)
                factor_(0)
                exps(2)
                factor_(1)
                exps(3)
                if proj:
                    ac.wait_ge(q.a_vturned, s + 1)
                    ac.activation(a_v[:, par, :, :].rearrange("p j c -> p (j c)"), obank[:, :], ACT.Copy)\
                        .then_inc(q.a_vcopied, 1)
                if attn:
                    for i in range(NQ):
                        ac.wait_ge(q.a_turned, 4 * hd + i + 1)
                        ac.activation(a_pt[:, 0:i + 1, i * P:(i + 1) * P],
                                      turn[:, i % 2, 0:LEN[i]].rearrange("p (j c) -> p j c", c=P), ACT.Copy)\
                            .then_inc(q.a_tcopied, 1)

            a_steps(ac, a_step)
            end_stage(ac, 2)
            conv_ffn(0)
            end_stage(ac, 3)
            ple(0)
            end_stage(ac, 4)

            load_p(1)
            factor("attn1")
            for j in range(7):
                ac.wait_ge(q.tile_taken, TILE["b_dkv"] + j + 1)
                ac.activation(b_dsq[:, j, :], b_cr[:, j, :], ACT.Square).then_inc(q.bd_squared, 1)
            for n, width in enumerate((KVL, ROPE, QL)):
                inv_sqrt(b_ri[:, n, :], width, q.bd_summed, q.bd_logged, q.bd_factor, n + 1, n + 1)
            end_stage(ac, 5)

            def b_step(s, par, proj, attn):
                def squared(j):
                    if proj:
                        ac.wait_ge(q.tile_taken, TILE["b_pair"] + 7 * s + j + 1)
                        ac.activation(b_sq[:, j, :], b_raw[:, j, :], ACT.Square).then_inc(q.b_squared, 1)

                def exps(x, i):
                    if attn:
                        n = 8 * (s - 1) + 4 * x + i
                        ac.wait_ge(q.b_min, n + 1)
                        e = b_sc[:, x, i, 0:LEN[i]]
                        ac.activation(e, e, ACT.Exp, bias=nmax[:, 4 * x + i:4 * x + i + 1], scale=-1.0,
                                      accum_out=den[:, 4 * x + i:4 * x + i + 1]).then_inc(q.b_exped, 1)

                def factor_(j):
                    if proj:
                        inv_sqrt(b_ri[:, j, :], ROPE if j == 2 else NOPE, q.b_summed, q.b_logged, q.b_factor,
                                 5 * s + j + 1, 5 * s + j + 1)

                squared(0); exps(0, 0); squared(1); exps(0, 1); squared(2); factor_(0); exps(0, 2); squared(3)
                factor_(1); exps(0, 3); squared(4); factor_(2); exps(1, 0); factor_(3); exps(1, 1); factor_(4)
                exps(1, 2); exps(1, 3)
                if proj:
                    for x in range(2):
                        ac.wait_ge(q.b_vturned, 2 * s + x + 1)
                        ac.activation(b_v[:, par, x, :], obank[:, :], ACT.Copy).then_inc(q.b_vcopied, 1)
                if attn:
                    for x in range(2):
                        for i in range(NQ):
                            ac.wait_ge(q.b_turned, 8 * (s - 1) + 4 * x + i + 1)
                            if x == 1 and i == 0:
                                ac.wait_ge(q.b_pv, 2 * s - 1)
                            ac.activation(b_pt[:, 0:i + 1, i * P:(i + 1) * P],
                                          turn[:, i % 2, 0:LEN[i]].rearrange("p (j c) -> p j c", c=P), ACT.Copy)\
                                .then_inc(q.b_tcopied, 1)

            b_steps(ac, b_step)
            end_stage(ac, 6)
            conv_ffn(1)
            end_stage(ac, 7)
            ac.dma_start(onehot, a["onehot"]).then_inc(q.extra_in, 16)
            ac.dma_start(relt, a["relt"]).then_inc(q.extra_in, 16)
            ple(1)
            end_stage(ac, 8)

            load_p(2)
            factor("mix2")
            for x in range(2):
                ac.wait_ge(q.tile_taken, TILE["c_in"] + 15 + x)
                ac.activation(c_acc[:, x, :], c_z[:, 14 + x, :], ACT.Sigmoid).then_inc(q.c_sigmoid, 1)
            for x in range(2):
                ac.wait_ge(q.tile_taken, TILE["c_in"] + 21 + x)
                ac.activation(c_z[:, 20 + x, :], c_z[:, 20 + x, :], ACT.Silu).then_inc(q.gl_silu, 1)
            end_stage(ac, 9)

            ac.wait_ge(q.gates_turned, 1)
            ac.activation(c_ga[:, :, :], stat[:, :].rearrange("p (i c) -> p i c", c=P)[:, :, 0:24], ACT.Sigmoid)\
                .then_inc(q.gates_made, 1)
            for x in range(2):
                ac.wait_ge(q.c_vturned, x + 1)
                ac.activation(c_v[:, x, :, :].rearrange("p j c -> p (j c)"), turn[:, x, :], ACT.Copy)\
                    .then_inc(q.c_vcopied, 1)
            for k in range(4):
                ac.wait_ge(q.tile_taken, TILE["c_cmp"] + k + 1)
                ac.activation(c_hid[:, k, :], c_hid[:, k, :], ACT.Silu, bias=v1("cmp_b1", k)).then_inc(q.hid_act, 1)
            ac.wait_ge(q.cc_sub, 1)
            cs3 = c_cs[:, :, :, :].rearrange("p h i n -> p (h i) n")
            ac.activation(cs3, cs3, ACT.Exp, scale=-1.0).then_inc(q.cc_exped, 1)
            for hd in range(CH):
                ac.wait_ge(q.cc_turned, hd + 1)
                ac.activation(c_ct[0:NCMP, hd, :], turn[0:NCMP, hd % 2, :], ACT.Copy).then_inc(q.cc_copied, 1)
            end_stage(ac, 10)

            for s in range(CH + 1):
                for i in range(NQ):
                    if s < CH:
                        n = 4 * s + i
                        ac.wait_ge(q.c_min, n + 1)
                        for x in range(2):
                            e = c_sc[:, i, x, 0:LEN[i]]
                            ac.activation(e, e, ACT.Exp, bias=nmax[:, 2 * i + x:2 * i + x + 1], scale=-1.0,
                                          accum_out=den[:, 2 * i + x:2 * i + x + 1]).then_inc(q.c_exped, 1)
                    if s > 0:
                        for x in range(2):
                            ac.wait_ge(q.c_turned, 8 * (s - 1) + 2 * i + x + 1)
                            if i == 0 and x == 0:
                                wait(ac, q.c_pv, s - 1)
                            ac.activation(c_pt[:, x, 0:i + 1, i * P:(i + 1) * P],
                                          turn[:, x, 0:LEN[i]].rearrange("p (j c) -> p j c", c=P), ACT.Copy)\
                                .then_inc(q.c_tcopied, 1)
            end_stage(ac, 11)

            ac.wait_ge(q.gl_alpha, 1)
            ac.activation(gl_e[:, 1, :], stat[:, :], ACT.Identity, bias=v1("b_alpha")).then_inc(q.gl_abs, 1)
            ac.wait_ge(q.gl_abs, 1)
            ac.activation(gl_e[:, 0, :], gl_e[:, 1, :], ACT.Abs).then_inc(q.gl_abs, 1)
            ac.wait_ge(q.gl_abs, 2)
            ac.activation(gl_e[:, 0, :], gl_e[:, 0, :], ACT.Exp, scale=-1.0).then_inc(q.gl_exp, 1)
            ac.wait_ge(q.gl_exp, 1)
            ac.activation(gl_e[:, 0, :], gl_e[:, 0, :], ACT.Ln, bias=ones[:, 0:1]).then_inc(q.gl_ln, 1)
            ac.wait_ge(q.gl_scan, 1)
            ac.activation(gl_t[:, 0, :], gl_b, ACT.Exp).then_inc(q.gl_exps, 1)
            ac.activation(gl_t[:, 1, :], gl_b, ACT.Exp, scale=-1.0).then_inc(q.gl_exps, 1)
            ac.activation(gl_dn, gl_b.rearrange("p (n c) -> p n c", c=GCH)[:, :, GCH - 1], ACT.Exp).then_inc(q.gl_exps, 1)
            ac.wait_ge(q.gl_diff, 1)
            ac.activation(gl_e[:, 1, :], gl_e[:, 0, :], ACT.Exp).then_inc(q.gl_exps, 1)
            for x in range(2):
                ac.wait_ge(q.gl_add, 2 * x + 2)
                ac.activation(gl_s[:, x, :], gl_o[:, x, :], ACT.Square).then_inc(q.gl_sq, 1)
            for x in range(2):
                inv_sqrt(gl_e[:, x, :], GV, q.gl_ss, q.gl_log, q.gl_fac, x + 1, x + 1)
            for x in range(2):
                ac.wait_ge(q.ln_cent, x + 1)
                ac.activation(gl_s[:, x, :], c_acc[:, x, :], ACT.Square).then_inc(q.ln_sq, 1)
            ac.wait_ge(q.ln_var, 1)
            ac.activation(gl_e[:, 2, :], obank[:, :], ACT.Ln, bias=eps[:, 0:1], scale=1.0 / CC).then_inc(q.ln_log, 1)
            ac.wait_ge(q.ln_log, 1)
            ac.activation(gl_e[:, 2, :], gl_e[:, 2, :], ACT.Exp, scale=-0.5).then_inc(q.ln_fac, 1)
            for x in range(2):
                ac.wait_ge(q.ln_norm, x + 1)
                ac.activation(g[:, 4 + x, :], gl_o[:, x, :], ACT.Silu, bias=v1("ln_b", x))
            end_stage(ac, 12)
            end_stage(ac, 13)

            factor("ffn2")
            t0 = TILE["ffn2_in"]

            def gate(i, u):
                ac.wait_ge(q.tile_taken, t0 + 2 * u + 1 + 4 * i)
                wait(ac, q.f_through, 2 * FC + 2 * i + u - 1)
                ac.activation(f_sg[:, u, :], f_c[:, 2 * u, :], ACT.Silu).then_inc(q.s_gate, 1)
            with ac.Fori(0, FC // 2) as i:
                gate(i, 0)
                gate(i, 1)
            end_stage(ac, 14)
            ple(2)
            end_stage(ac, 15)
            factor("final")
            for c in range(DC):
                ac.wait_ge(q.residual_added, 3 * DC + c + 1)
                ac.dma_start(out[c * P:(c + 1) * P, :], g[:, c, :]).then_inc(q.out_stored, 16)

        @block.gpsimd
        def _(po):
            for n in range(2, 12):
                end_stage(po, n)
            po.wait_ge(q.gl_attc, GH)
            for odd in range(2):
                half = gl_am[64 * odd:64 * odd + 64, :, :, :].rearrange("p h n c -> p (h n) c")
                po.affine_select(out=half, in_=half, compare_op=ALU.is_ge, fill=0.0, base=0,
                                 pattern=[[0, GH * NCH // 2], [1, GCH]], channel_multiplier=-1).then_inc(q.gl_mask, 1)
            for n in range(12, 16):
                end_stage(po, n)


def _blocks(w):
    k, m = w.shape
    return w.reshape(k // P, P, m // P, P).transpose(2, 1, 0, 3).reshape(m // P, P, k)


def _groups(tiles, per):
    n = tiles.shape[0] // per
    return tiles.reshape(n, per, P, -1).transpose(0, 2, 1, 3).reshape(n, P, -1)


def _columns(v):
    return np.ascontiguousarray(v.reshape(-1, P).T)


def _consts():
    i = np.arange(P)
    rot = np.zeros((P, P), np.float32)
    low = i % ROPE < ROPE // 2
    rot[i[low] + ROPE // 2, i[low]] = -1.0
    rot[i[~low] - ROPE // 2, i[~low]] = 1.0
    mask = np.where(np.arange(S)[None, :] - (S - P) <= i[:, None], 0.0, NEG)
    return np.concatenate([np.ones((P, P)), i[:, None] // 64 == i[None, :] // 64, np.eye(P), rot, mask], axis=1)\
        .astype(np.float32)


def _onehot():
    starts = np.array([0] + bucket_starts())
    dist = S - 1 - np.arange(S)
    bucket = np.searchsorted(starts, dist, side="right") - 1
    return (np.arange(BUCKETS)[:, None] == bucket[None, :]).astype(np.float32)


def _lay_out(x):
    f = {k: np.asarray(v) for k, v in x.items()}
    a = {}
    a["x_t"] = f["x"][0].T.reshape(DC, P, S).transpose(1, 0, 2)
    p = np.concatenate([f["p"][:, 0], f["p_2"][:, 0]], axis=0)
    a["p_t"] = p.transpose(0, 2, 1).reshape(3, 2, P, S).transpose(0, 2, 1, 3).reshape(3, P, -1)
    a["positions"] = f["positions"].astype(np.int32) if f["positions"].dtype != np.int32 else f["positions"]
    a["table"] = f["rel_bias_table"].reshape(1, -1)
    a["lam"] = np.concatenate([f["a_lam_q1"], f["a_lam_k1"], f["a_lam_q2"], f["a_lam_k2"]], axis=1)
    a["consts"] = _consts()
    a["onehot"] = _onehot()
    a["relt"] = f["rel_bias_2"]
    a["w_alpha"] = f["gla_w_alpha_2"][0]
    a["cmp_w2"] = np.concatenate([f["cmp_w2_k_2"][0].reshape(2, P, CD), f["cmp_w2_v_2"][0].reshape(2, P, CD)])\
        .transpose(1, 0, 2).reshape(P, -1)

    qkv = _blocks(f["a_w_qkv"][0]).reshape(3, AH, P, D).transpose(1, 0, 2, 3).reshape(3 * AH, P, D)
    a["w_a_qkv"] = _groups(qkv, 3)
    a["w_a_wo"] = _groups(_blocks(f["a_w_o"][0]), 2)

    def ffn_in(first, second):
        return _groups(np.stack([_blocks(first), _blocks(second)], axis=1).reshape(2 * FC, P, D), 2)

    def ple(gate, proj):
        return _groups(np.concatenate([_blocks(gate), _blocks(proj)], axis=2), 2)

    for n in range(2):
        w = f["ffn_w_in"][n]
        a[f"w_ffn{n}_in"] = ffn_in(w[:, :FF], w[:, FF:])
        a[f"w_ffn{n}_out"] = _blocks(f["ffn_w_out"][n])
        a[f"w_ple{n}"] = ple(f["ple_w_gate"][n], f["ple_w_proj"][n])
    a["w_ffn2_in"] = ffn_in(f["ffn_w_gate_2"][0], f["ffn_w_up_2"][0])
    a["w_ffn2_out"] = _blocks(f["ffn_w_down_2"][0])
    a["w_ple2"] = ple(f["ple_w_gate_2"][0], f["ple_w_proj_2"][0])

    dkv = f["w_dkv"]
    a["w_b_dkv"] = _groups(_blocks(np.concatenate([dkv, dkv[:, KVL:]], axis=1)), 3)
    a["w_b_dq"] = _groups(_blocks(f["b_w_dq"][0]), 2)
    uq = f["b_w_uq"][0].reshape(QL, B_PAIRS, 2, NOPE + ROPE)
    ukv = f["w_ukv"].reshape(KVL, B_PAIRS, 2, NOPE + P)
    pair = []
    for n in range(B_PAIRS):
        up = np.concatenate([uq[:, n, 0, :NOPE], uq[:, n, 1, :NOPE], uq[:, n, 0, NOPE:], uq[:, n, 1, NOPE:]], axis=1)
        kv = np.concatenate([ukv[:, n, 0, :NOPE], ukv[:, n, 1, :NOPE], ukv[:, n, 0, NOPE:], ukv[:, n, 1, NOPE:]], axis=1)
        pair.append(np.concatenate([_groups(_blocks(up), 3)[0], _groups(_blocks(kv), 4)[0]], axis=1))
    a["w_b_pair"] = np.stack(pair)
    a["w_b_wo"] = _blocks(f["b_w_o"][0])

    w = f["w_in_2"][0]
    splits = [512, 128, 128, 128, 128, 128, 128, 24, 512, 128, 128, 256, 16, 256]
    nq, kc, vc, ks, vs, kw, vw, ng, cu, gq, gk, gv, ga, gr = np.split(w, np.cumsum(splits)[:-1], axis=1)
    heads = [nq[:, CD * i:CD * (i + 1)] for i in range(CH)]
    cols = [c for t in range(4) for c in (heads[t], heads[t + 4])] + [ks, kw, vs, vw]
    for m in (kc, vc):
        for x in range(CKV):
            cols += [m[:, CD * x:CD * (x + 1)]] * 2
    cols += [cu, gq, gk, gv, gr, ng, np.zeros((D, 8), w.dtype), ga, np.zeros((D, 80), w.dtype)]
    tiles = _blocks(np.concatenate(cols, axis=1))
    a["w_c_in"] = _groups(tiles[:21], 3)
    a["w_c_in_last"] = _groups(tiles[21:23], 2)
    a["w_c_cmp"] = np.concatenate([_blocks(f["cmp_w1_k_2"][0]), _blocks(f["cmp_w1_v_2"][0])])
    a["w_c_out"] = _groups(_blocks(f["w_out_2"][0]), 2)

    def twice(v):
        return np.concatenate([v, v]).reshape(P, 1)

    def conv(n):
        t = np.concatenate([f["ffn_conv_w"][n], f["ffn_conv_b"][n][None]])
        t = t.reshape(4, 2, FC, P).transpose(3, 2, 1, 0)
        return t.reshape(P, -1)

    inv = np.exp(np.float32(-math.log(ROPE_BASE)) * np.arange(ROPE // 2, dtype=np.float32) * np.float32(2.0 / ROPE))
    dw = f["conv_w_2"][0]
    vecs = {
        "attn0": _columns(f["attn_norm"][0]), "attn1": _columns(f["attn_norm"][1]), "kv": _columns(f["kv_norm"]),
        "ffn0": _columns(f["ffn_norm"][0]), "ffn1": _columns(f["ffn_norm"][1]),
        "ple0": _columns(f["ple_norm"][0]), "ple1": _columns(f["ple_norm"][1]),
        "mix2": _columns(f["mix_norm_g_2"][0]), "ffn2": _columns(f["ffn_norm_g_2"][0]),
        "ple2": _columns(f["ple_norm_g_2"][0]), "final": _columns(f["final_norm_g_2"]),
        "a_q": twice(f["a_q_norm"][0]), "a_k": twice(f["a_k_norm"][0]), "a_sub": _columns(f["a_sub_norm"][0]),
        "ckv": _columns(f["ckv_norm"]), "cq": _columns(f["b_cq_norm"][0]), "k_nope": _columns(f["k_nope_norm"]),
        "k_pe": twice(f["k_pe_norm"]), "q_nope": _columns(f["b_q_nope_norm"][0]), "q_pe": twice(f["b_q_pe_norm"][0]),
        "inv_freq": np.tile(inv, 4).reshape(P, 1), "conv0": conv(0), "conv1": conv(1),
        "cmp_b1": np.concatenate([_columns(f["cmp_b1_k_2"][0]), _columns(f["cmp_b1_v_2"][0])], axis=1),
        "cmp_pos": np.concatenate([f[n][0].reshape(16, P).T for n in ("cmp_pos_k_2", "cmp_pos_v_2")], axis=1),
        "dw": dw.reshape(CW, 2, P).transpose(2, 1, 0).reshape(P, -1), "dw_b": _columns(f["conv_b_2"][0]),
        "ln_g": _columns(f["conv_ln_g_2"][0]), "ln_b": _columns(f["conv_ln_b_2"][0]),
        "b_alpha": _columns(f["gla_b_alpha_2"][0]), "gla_g": _columns(f["gla_norm_g_2"][0]),
        "t5_start": np.tile(np.array(bucket_starts(), np.float32), (P, 1)),
        "first_block": (np.arange(P) >= CMPB - 1).astype(np.float32).reshape(P, 1),
    }
    for name, n in VEC_COLS:
        assert vecs[name].shape == (P, n), (name, vecs[name].shape)
    a["vec"] = np.concatenate([vecs[name] for name, _ in VEC_COLS], axis=1)
    return {k: np.ascontiguousarray(v) for k, v in a.items()}


def kernel(**inputs):
    import concourse.bacc as bacc
    from concourse.bass_utils import run_bass_kernel_spmd as run

    arrays = {f"in_{k}": v for k, v in _lay_out(inputs).items()}
    nc = bacc.Bacc("TRN2", target_bir_lowering=False, num_devices=1)
    aps = {k[3:]: nc.dram_tensor(k, v.shape, mybir.dt.from_np(v.dtype), kind="ExternalInput").ap()
           for k, v in arrays.items()}
    out = nc.dram_tensor("out", [D, S], F32, kind="ExternalOutput").ap()
    build_program(nc, aps, out)
    result = run(nc, [arrays], core_ids=[0])
    return result.results[0]["out"].T.reshape(1, S, D)
```

```python
import math
from collections import namedtuple
from contextlib import ExitStack

import concourse.bass as bass
import numpy as np
from concourse import mybir

P = 128
S = 512
D = 1024
DC = D // P
NQ = S // P
FF = 2816
FC = FF // P
EPS = 1e-6
NEG = -1e30
BUCKETS, MAX_EXACT, MAX_DIST = 32, 16, 128
AH, AQK = 8, 64
LAM_INIT = 0.8 - 0.6 * math.exp(0.0)
BH, NOPE, ROPE = 16, 128, 64
QL, KVL = 512, 256
ROPE_BASE = 10000.0
CH, CKV, CD = 8, 2, 64
CMPB, CMPS, HID = 32, 16, 256
NCMP = S // CMPS - CMPB // CMPS + 1
CC, CW = 256, 31
GH, GK, GV, GCH, TAU = 4, 32, 64, 64, 16.0
NCH = S // GCH
SLOT = 12 * P
LEN = [(i + 1) * P for i in range(NQ)]
OFF = [sum(LEN[:i]) for i in range(NQ)]
CAUSAL = sum(LEN)
B_PAIRS = BH // 2

F32 = mybir.dt.float32
F32R = mybir.dt.float32r
I32 = mybir.dt.int32
ALU = mybir.AluOpType
ACT = mybir.ActivationFunctionType
AX = mybir.AxisListType

STREAM = [
    ("a_qkv", 3 * AH, (DC, DC), (1, 1)), ("a_wo", DC, (DC, DC), (1, 1)),
    ("ffn0_in", 2 * FC, (DC, DC), (1, 1)), ("ffn0_out", 2 * DC, (FC // 2, FC // 2), (1, 1)),
    ("ple0", DC, (DC + 2, DC + 2), (2, 2)),
    ("b_dkv", 3, (DC, DC), (1, 1)), ("b_dq", 4, (DC, DC), (1, 1)), ("b_pair", 2 * B_PAIRS, (12, 8), (3, 4)),
    ("b_wo", 2 * DC, (BH // 2, BH // 2), (1, 1)),
    ("ffn1_in", 2 * FC, (DC, DC), (1, 1)), ("ffn1_out", 2 * DC, (FC // 2, FC // 2), (1, 1)),
    ("ple1", DC, (DC + 2, DC + 2), (2, 2)),
    ("c_in", 23, (DC, DC), (1, 1)), ("c_cmp", 8, (8, 8), (1, 1)), ("c_out", DC, (DC, DC), (1, 1)),
    ("ffn2_in", 2 * FC, (DC, DC), (1, 1)), ("ffn2_out", 2 * DC, (FC // 2, FC // 2), (1, 1)),
    ("ple2", DC, (DC + 2, DC + 2), (2, 2)),
]
GROUP, TILE, PER = {}, {}, {}
GROUP_END = []
_g = _t = 0
for _n, _c, _b, _per in STREAM:
    GROUP[_n], TILE[_n], PER[_n] = _g, _t, _per
    _g += _c
    for _k in range(_c):
        _t += _per[_k % 2]
        GROUP_END.append(_t)
NORM = {n: i for i, n in enumerate(
    ["attn0", "ffn0", "ple0", "attn1", "ffn1", "ple1", "mix2", "ffn2", "ple2", "final"])}
RESIDUALS = ["a_wo", "ffn0_out", "b_wo", "ffn1_out", "c_out", "ffn2_out"]

SIGNALS = """
consts_in x_in positions_in lam_in table_in p_in extra_in stage_end h_squared h_rounded h_gained h_gained2 h_summed
r_logged r_ready hi_made weights_split out_rounded out_split p_split tile_done tile_taken residual_added out_stored setup_step lam_dots lam_exps bias_built
angles_ready f_first f_conv f_silu f_split f_through s_gate ple_sigmoid a_squared a_summed a_logged
a_factor a_normed a_vturned a_vcopied a_scored a_biased a_min a_exped a_recip a_scaled a_weights a_turned
a_tcopied a_pv a_otaken a_osquared a_osummed a_ologged a_ofactor a_onormed bd_squared bd_summed bd_logged
bd_factor bd_normed bd_rounded bd_rotated bd_terms b_squared b_summed b_logged b_factor b_normed b_rotated b_terms
b_rope b_vturned b_vcopied b_scored b_biased b_min b_exped b_recip b_weights b_turned b_tcopied b_pv
b_otaken g_made g_rowed g_written g_read  c_sigmoid c_glu conv_step zp_made hid_act kc_made
kc_copied c_vturned c_vcopied gates_turned gates_made cb_made cc_scored cc_biased cc_reduced cc_exped
 cc_recip cc_scaled cc_turned cc_copied c_scored c_biased c_min c_exped c_recip c_gated c_weights
c_turned c_tcopied c_pv c_otaken gl_alpha gl_abs gl_exp gl_ln gl_la gl_scale gl_scan gl_exps
gl_prod gl_att gl_attc gl_mask gl_kdt gl_kdc gl_u gl_uc gl_state gl_bd gl_out gl_sum gl_add gl_sq gl_ss
gl_log gl_fac gl_norm gl_silu ln_summed ln_cent ln_sq ln_logged ln_norm
""".split()
Signals = namedtuple("Signals", SIGNALS)

VEC_COLS = [("attn0", DC), ("attn1", DC), ("kv", DC), ("ffn0", DC), ("ffn1", DC), ("ple0", DC), ("ple1", DC),
            ("mix2", DC), ("ffn2", DC), ("ple2", DC), ("final", DC), ("a_q", 1), ("a_k", 1), ("a_sub", 1),
            ("ckv", 2), ("cq", 4), ("k_nope", 1), ("k_pe", 1), ("q_nope", 1), ("q_pe", 1), ("inv_freq", 1),
            ("conv0", 8 * FC), ("conv1", 8 * FC), ("cmp_b1", 4), ("cmp_pos", 32), ("dw", 2 * CW), ("dw_b", 2),
            ("ln_g", 2), ("ln_b", 2), ("b_alpha", 1), ("gla_g", 2), ("first_block", 1),
            ("t5_start", BUCKETS - 1)]
VEC = {}
NVEC = 0
for _n, _c in VEC_COLS:
    VEC[_n] = NVEC
    NVEC += _c
ARENA = 29824
DMA_SCRATCH, SBUF_BYTES = 1024, 229344
G_ROWED, G_READ = 1 + AH, 16 * NQ
PI_IN = 3.1415925
BAND = CH * 2 * S


def bucket_starts():
    ratio = MAX_DIST / MAX_EXACT
    return [b if b <= MAX_EXACT else math.ceil(MAX_EXACT * ratio ** ((b - MAX_EXACT) / (BUCKETS - MAX_EXACT)))
            for b in range(1, BUCKETS)]


def wait(eng, sem, value):
    if not (isinstance(value, int) and value <= 0):
        eng.wait_ge(sem, value)


def a_steps(eng, step):
    step(0, 0, True, False, False)
    step(1, 1, True, True, False)
    with eng.Fori(0, (AH - 2) // 2) as i:
        for par in range(2):
            step(2 * i + 2 + par, par, True, True, True)
    step(AH, 0, False, True, True)
    step(AH + 1, 1, False, False, True)


def b_steps(eng, step):
    step(0, 0, True, False)
    step(1, 1, True, True)
    with eng.Fori(0, (B_PAIRS - 2) // 2) as i:
        for par in range(2):
            step(2 * i + 2 + par, par, True, True)
    step(B_PAIRS, 0, False, True)


def build_program(nc, a, out):
    with ExitStack() as ctx:
        top = [DMA_SCRATCH]

        def sb(name, *shape, dt=F32, rounded=None):
            kw = {"offset": top[0]}
            main = nc.alloc_sbuf_tensor_at(name, list(shape), dt, **kw)
            both = (main, nc.alloc_sbuf_tensor_at(rounded, list(shape), F32R, **kw)) if rounded else main
            top[0] += -(-4 * int(np.prod(shape[1:])) // 32) * 32
            assert top[0] <= SBUF_BYTES, top[0]
            return both

        def sem(name):
            return ctx.enter_context(nc.semaphore(name))

        lin = ctx.enter_context(nc.psum_tensor("lin", [P, 2, 512], F32))
        scores = ctx.enter_context(nc.psum_tensor("scores", [P, 2, 512], F32))
        stat = ctx.enter_context(nc.psum_tensor("stat", [P, 512], F32))
        turn = ctx.enter_context(nc.psum_tensor("turn", [P, 2, 512], F32))
        obank = ctx.enter_context(nc.psum_tensor("obank", [P, 512], F32))

        h = sb("h", P, DC, S)
        g, g_hi = sb("g", P, DC, S, rounded="g_hi")
        low, g_lo = sb("low", P, DC, S, rounded="g_lo")
        slots = sb("slots", P, 2, SLOT)
        w_hi = nc.alloc_sbuf_tensor_at("w_hi", [P, 2, SLOT], F32R, offset=top[0]); top[0] += 8 * SLOT
        w_lo = nc.alloc_sbuf_tensor_at("w_lo", [P, 2, SLOT], F32R, offset=top[0]); top[0] += 8 * SLOT
        r = sb("r", P, S)
        lnr = sb("lnr", P, S)
        vec = sb("vec", P, NVEC)
        consts = sb("consts", P, 8 * P)
        ones, ones64, ident, rot = (consts[:, k * P:(k + 1) * P] for k in range(4))
        maskt = consts[:, 4 * P:8 * P]
        eps = sb("eps", P, 1)
        small = sb("small", P, 64)
        p_in_t = sb("p_in_t", P, 2, S)
        arena_at = top[0]
        arena = sb("arena", P, ARENA)

        def area_r(name, at, *shape):
            assert at + int(np.prod(shape)) <= ARENA, (at, shape)
            return nc.alloc_sbuf_tensor_at(name, [P, *shape], F32R, offset=arena_at + 4 * at)

        def area(at, *shape):
            n = int(np.prod(shape))
            assert at + n <= ARENA, (at, shape)
            v = arena[:, at:at + n]
            names = "abcd"[:len(shape)]
            if len(shape) == 1:
                return v
            return v.rearrange(f"p ({' '.join(names)}) -> p {' '.join(names)}", **dict(zip(names[:-1], shape[:-1])))

        def v1(name, j=0, n=1):
            c = VEC[name] + j
            return vec[:, c:c + n]

        sq = area(0, DC, S)
        at = DC * S
        a_bias = area(at, AH, CAUSAL); at += AH * CAUSAL
        a_raw = area(at, 3, S); at += 3 * S
        a_sq = a_ri = area(at, 3, S); at += 3 * S
        a_rawo = area(at, S); at += S
        a_qk = area(at, 2, 2, S); at += 4 * S
        a_v = area(at, 2, NQ, P); at += 2 * S
        a_sc = area(at, NQ, 2, S); a_dist = area(at, CAUSAL); a_mask = area(at + CAUSAL, CAUSAL); a_grow = area(at, AH, S); at += 8 * S
        a_pt = area(at, NQ, S)
        pos_i = area(at, S).bitcast(I32); at += S
        posf = area(at, S); at += S
        a_tab = area(at, BUCKETS * AH); at += BUCKETS * AH
        a_diff = area(at, BUCKETS * AH); at += BUCKETS * AH
        a_lam = area(at, 5, AQK); at += 5 * AQK
        a_neg = area(at, P)
        a_step_ok = a_raw[:, 0, 0:S - 1]
        a_onehot, a_relt = a_v[0:BUCKETS, 0, :, :].rearrange("p j c -> p (j c)"), a_v[0:BUCKETS, 1, 0, 0:AH]
        a_o = sq
        regular = sb("regular", P, 2)
        regular_i = sb("regular_i", P, 1, dt=I32)
        posq_i = sb("posq_i", P, NQ, dt=I32)
        cosb = sb("cosb", P, S)
        sinb = sb("sinb", P, S)
        posq = small[:, 0:4]
        nlam, asub, lamd, lame = small[:, 4:5], small[:, 5:6], small[:, 6:8], small[:, 8:10]
        nmax = small[:, 16:32]
        den = small[:, 32:48]
        f_hi = area_r("f_hi", 0, FC, S)
        f_lo = area_r("f_lo", FC * S, FC, S)
        f_u = area(2 * FC * S, 4, S + 2)
        f_c = area(2 * FC * S + 4 * (S + 2), 4, S)
        f_sg = area(2 * FC * S + 4 * (S + 2) + 4 * S, 2, S)
        p_gp = area(4096, 2, S)
        p_sg = area(4096 + 2 * S, 2, S)
        p_t = area(4096 + 4 * S, 2, S)
        p_hi = area_r("p_hi", 4096 + 6 * S, 2, S)
        p_lo = area_r("p_lo", 4096 + 8 * S, 2, S)
        at = DC * S
        b_g2_hi = area_r("b_g2_hi", at, DC, S); b_o = area(0, BH, S); at += DC * S
        b_o_hi = area_r("b_o_hi", at, BH, S); b_o_lo = area_r("b_o_lo", at + BH * S, BH, S)
        b_sc = g[:, :, :].rearrange("p (x i) s -> p x i s", x=2)
        b_cr = area(at, 7, S); b_raw = b_cr; at += 7 * S
        b_sq = b_ri = area(at, 5, S); at += 5 * S
        b_ckv_hi = area_r("b_ckv_hi", at, 2, S); at += 2 * S
        b_cq_hi = area_r("b_cq_hi", at, 4, S); at += 4 * S
        b_kp = area(at, S); at += S
        b_dsq = area(at, 7, S)
        b_qn = area(at, 2, 2, S); at += 4 * S
        b_kn = area(at, 2, 2, S); at += 4 * S
        b_qp = area(at, 2, S); at += 2 * S
        b_rt = area(at, 3, S); at += 3 * S
        b_g2_lo = area_r("b_g2_lo", at, DC, S)
        b_ckv_lo = area_r("b_ckv_lo", at, 2, S); at += 2 * S
        b_cq_lo = area_r("b_cq_lo", at, 4, S); at += 4 * S
        b_v = low[:, 0:4, :].rearrange("p (a b) s -> p a b s", a=2)
        b_pt = low[:, 4:8, :]
        at = 0
        c_sc = area(at, NQ, 2, S); c_gl = at; at += 8 * S
        c_z = area(at, 23, S); at += 23 * S
        c_ct = c_z[:, 8:16, :]
        c_hp = area(at, 2, S + CW - 1); at += 2 * (S + CW - 1)
        c_acc = area(at, 2, S); at += 2 * S
        c_bias = area(at, CH, S); at += CH * S
        c_cb = area(at, CH, NQ, NCMP); at += CH * NQ * NCMP
        c_pt = area(at, 2, NQ, S); c_zp = area(at, 2, 16, 2 * NCMP)
        neg = area(at + 4 * S, P); onehot = area(at + 6 * S, S)[0:BUCKETS, :]
        relt = area(at + 7 * S, CH)[0:BUCKETS, :]; at += 8 * S
        c_v = area(at, 2, NQ, P); at += 2 * S
        c_ga = area(at, NQ, 24); at += NQ * 24
        c_kc = area(at, 32); at += 32
        c_vc = area(at, 2, CD); at += 2 * CD
        c_hid = area(at, 4, 2 * NCMP); at += 4 * 2 * NCMP
        c_cs = area(at, CH, NQ, NCMP); at += CH * NQ * NCMP
        c_cden = area(at, CH * NQ); at += CH * NQ
        c_cmin = area(at, CH * NQ); at += CH * NQ
        c_small_end = at
        at = c_gl
        gl_qt = area(at, S); at += S
        gl_kt = area(at, S); at += S
        gl_kd = area(at, S); at += S
        gl_b = area(at, S); at += S
        gl_t = area(at, 2, S); at += 2 * S
        gl_s = area(at, 2, S); at += 2 * S
        at = DC * S + 23 * S + 2 * (S + CW - 1) + 2 * S
        gl_am = area(at, GH, NCH // 2, GCH); at += GH * NCH // 2 * GCH
        gl_kdt = area(at, NQ, P); at += S
        gl_vt = area(at, NQ, 2 * P); at += 2 * S
        gl_us = area(at, NCH, GV); at += NCH * GV
        gl_st = area(at, NCH, GV); at += NCH * GV
        gl_bds = area(at, NCH, 2 * P); at += NCH * 2 * P
        gl_o = area(at, 2, S); at += 2 * S
        gl_e = area(at, 3, S); at += 3 * S
        gl_reset = area(at, S); at += S
        gl_dn = small[:, 48:48 + NCH]
        w2c = sb("w2c", P, 4, CD)
        walpha = sb("walpha", P, P)

        landed = [sem("weights_landed_in_slot0"), sem("weights_landed_in_slot1")]

        q = Signals(*(sem(name) for name in SIGNALS))

        ab_dram = nc.dram_tensor("a_bias_by_distance", [P + 1, BAND], F32, kind="Internal").ap()
        g_dram = nc.dram_tensor("bias_by_distance", [P + 1, BAND], F32, kind="Internal").ap()
        block = ctx.enter_context(nc.Block())

        def end_stage(eng, n):
            eng.drain().then_inc(q.stage_end, 1)
            eng.wait_ge(q.stage_end, 3 * (n - 1))

        def stream(eng, name, count, step, between=None):
            pair = sum(PER[name])
            for k in range(min(2, count)):
                n = GROUP[name] + k
                step(k, n, 0, GROUP_END[n - 2] if n >= 2 else 0)
            if between:
                between()
            if count >= 4:
                with eng.Fori(0, (count - 2) // 2) as i:
                    for u in range(2):
                        step(2 + u, GROUP[name] + 2 + u, i, GROUP_END[GROUP[name] + u] + pair * i)
            if count > 2 and count % 2:
                n = GROUP[name] + count - 1
                step(count - 1, n, 0, GROUP_END[n - 2])

        @block.sync
        def _(sp):
            sp.dma_start(a_onehot, a["onehot"]).then_inc(q.table_in, 16)
            sp.dma_start(a_relt, a["table"].rearrange("a (b h) -> (a b) h", h=AH)).then_inc(q.table_in, 16)
            sp.dma_start(vec[:, :], a["vec"]).then_inc(q.consts_in, 16)
            sp.dma_start(consts[:, :], a["consts"]).then_inc(q.consts_in, 16)
            for c in range(DC):
                sp.dma_start(h[:, c, :], a["x_t"][:, c, :]).then_inc(q.x_in, 16)

            def bias_by_distance(n, dram, rows, tail, parts):
                skewed = [[BAND + 1, P], [2 * S, AH]]
                sp.wait_ge(q.g_rowed, (n + 1) * (1 + AH))
                sp.dma_start(bass.AP(tensor=dram.tensor, offset=0, ap=skewed + [[1, S]]), rows).then_inc(q.g_written, 16)
                sp.dma_start(bass.AP(tensor=dram.tensor, offset=S, ap=skewed + [[1, P]]),
                             tail.unsqueeze(1).broadcast_to([P, AH, P])).then_inc(q.g_written, 16)
                sp.wait_ge(q.g_written, 32 * (n + 1))
                for dst, c in parts:
                    band = bass.AP(tensor=dram.tensor, offset=P - 1 + c, ap=[[BAND, P], [2 * S, AH], [1, S - c]])
                    sp.dma_start(dst, band).then_inc(q.g_read, 16)

            def a_bias_by_distance():
                bias_by_distance(0, ab_dram, a_grow, a_neg,
                                 [(a_bias[:, :, OFF[i]:OFF[i] + LEN[i]], S - LEN[i]) for i in range(NQ)])

            def c_bias_by_distance():
                bias_by_distance(1, g_dram, c_bias, neg, [(c_bias, 0)])

            for name, count, blocks, per in STREAM:
                src = a["w_" + name]

                def load(k, n, i, end):
                    wait(sp, q.weights_split, n - 1 + 2 * i if n >= 2 else 0)
                    sp.dma_start(slots[:, n % 2, 0:blocks[k % 2] * P], src[k + 2 * i, :, 0:blocks[k % 2] * P])\
                        .then_inc(landed[n % 2], 16)
                stream(sp, name, count, load, {"a_qkv": a_bias_by_distance, "c_in": c_bias_by_distance}.get(name))
            sp.wait_ge(q.out_stored, 16 * DC)

        @block.tensor
        def _(pe):
            def norm_sums(name):
                for c in range(DC):
                    pe.wait_ge(q.h_squared, DC * NORM[name] + c + 1)
                    mm = pe.matmul(stat[:, :], ones, sq[:, c, :], start=c == 0, stop=c == DC - 1)
                mm.then_inc(q.h_summed, 1)
                if name != "final":
                    pe.wait_ge(q.h_gained, DC * (NORM[name] + 1))

            def weights(name, k, i=0):
                n = GROUP[name] + k
                pe.wait_ge(q.weights_split, n + 1 + i)
                return w_hi[:, n % 2, :], w_lo[:, n % 2, :]

            def tile(t, parity, w, first, rhs):
                wait(pe, q.tile_taken, t - 1)
                for k, (x_hi, x_lo) in enumerate(rhs):
                    hi, lo = (p_[:, (first + k) * P:(first + k + 1) * P] for p_ in w)
                    pe.matmul(lin[:, parity, :], hi, x_hi, start=k == 0, stop=False)
                    pe.matmul(lin[:, parity, :], hi, x_lo, start=False, stop=False)
                    mm = pe.matmul(lin[:, parity, :], lo, x_hi, start=False, stop=k == len(rhs) - 1)
                mm.then_inc(q.tile_done, 1)

            def parts(hi, lo, n):
                return [(hi[:, c, :], lo[:, c, :]) for c in range(n)]

            def linear(name, rhs, groups, ready=None):
                def turn_(i, us):
                    for u in us:
                        if ready:
                            pe.wait_ge(*ready[u])
                        w = weights(name, u, 2 * i)
                        t = TILE[name] + u
                        tile(t + 2 * i, t % 2, w, 0, rhs[u])
                assert PER[name] == (1, 1)
                with pe.Fori(0, groups // 2) as i:
                    turn_(i, (0, 1))
                if groups % 2:
                    turn_(groups // 2, (0,))

            def ple(n):
                name = f"ple{n}"
                pe.wait_ge(q.p_split, 2 * (n + 1))
                with pe.Fori(0, DC // 2) as i:
                    for u in range(2):
                        w = weights(name, u, 2 * i)
                        t = TILE[name] + 2 * u
                        tile(t + 4 * i, t % 2, w, 0, gs)
                        tile(t + 1 + 4 * i, (t + 1) % 2, w, DC, parts(p_hi, p_lo, 2))

            gs = parts(g_hi, g_lo, DC)

            def ffn_products(n):
                linear(f"ffn{n}_in", (gs, gs), 2 * FC)
                hidden, half = parts(f_hi, f_lo, FC), FC // 2
                linear(f"ffn{n}_out", (hidden[:half], hidden[half:]), 2 * DC,
                       [(q.f_through, FC * n + half), (q.f_through, FC * n + FC)])

            def output_products(name, n, rhs, halves):
                for k in range(len(rhs)):
                    pe.wait_ge(q.out_split, n + k + 1)
                linear(name, (rhs[:len(rhs) // 2], rhs[len(rhs) // 2:]) if halves else (rhs, rhs), (1 + halves) * DC)

            def ffn(n):
                norm_sums(f"ffn{n}")
                ffn_products(n)

            def turn_weights(src, i, dst_bank):
                for j in range(i + 1):
                    mm = pe.transpose(dst_bank[:, j * P:(j + 1) * P], src[:, j * P:(j + 1) * P], ident)
                return mm

            pe.wait_ge(q.table_in, 48)
            for hd in range(AH):
                b = (scores[:, 0, :], scores[:, 1, :], turn[:, 0, :], turn[:, 1, :])[hd % 4]
                if hd >= 4:
                    pe.wait_ge(q.g_rowed, hd - 2)
                pe.matmul(b, a_relt[:, hd:hd + 1].broadcast_to([BUCKETS, P]), a_onehot, start=True, stop=True)\
                    .then_inc(q.g_made, 1)
            pe.wait_ge(q.consts_in, 32)

            norm_sums("attn0")

            def a_step(s, par, proj, attn, tail):
                def lin_(j):
                    if proj:
                        w = weights("a_qkv", 3 * par + j, 3 * (s - par))
                        tile(TILE["a_qkv"] + 3 * s + j, (TILE["a_qkv"] + 3 * par + j) % 2, w, 0, gs)

                def score(i):
                    if attn:
                        hd = s - 1
                        if i == 0:
                            pe.wait_ge(q.a_normed, 2 * hd + 2)
                        wait(pe, q.a_biased, 4 * hd + i)
                        for c in range(2):
                            rows = slice(64 * c, 64 * c + 64)
                            mm = pe.matmul(scores[:, c, 0:LEN[i]], a_qk[rows, 1 - par, 0, i * P:(i + 1) * P],
                                           a_qk[rows, 1 - par, 1, 0:LEN[i]], start=True, stop=True)
                        mm.then_inc(q.a_scored, 1)

                def sums(j):
                    if proj:
                        pe.wait_ge(q.a_squared, 2 * s + j + 1)
                        wait(pe, q.a_logged, 2 * s + j)
                        if j == 0:
                            wait(pe, q.a_ologged, s - 1 if tail else 0)
                        pe.matmul(stat[:, :], ones64, a_sq[:, j, :], start=True, stop=True).then_inc(q.a_summed, 1)

                if proj:
                    lin_(0)
                if tail:
                    pe.wait_ge(q.a_osquared, s - 1)
                    pe.wait_ge(q.a_logged, 2 * s if proj or attn else 2 * AH)
                    pe.matmul(stat[:, :], ones, a_sq[:, 2, :], start=True, stop=True).then_inc(q.a_osummed, 1)
                score(0)
                lin_(1)
                score(1)
                sums(0)
                lin_(2)
                score(2)
                sums(1)
                score(3)
                if proj:
                    pe.wait_ge(q.tile_taken, TILE["a_qkv"] + 3 * s + 3)
                    wait(pe, q.a_otaken, s - 1)
                    for j in range(NQ):
                        mm = pe.transpose(obank[:, j * P:(j + 1) * P], a_raw[:, 2, j * P:(j + 1) * P], ident)
                    mm.then_inc(q.a_vturned, 1)
                if attn:
                    hd = s - 1
                    for i in range(NQ):
                        pe.wait_ge(q.a_weights, 4 * hd + i + 1)
                        wait(pe, q.a_tcopied, 4 * hd + i - 1)
                        turn_weights(a_sc[:, i, 0, :], i, turn[:, i % 2, :]).then_inc(q.a_turned, 1)
                    pe.wait_ge(q.a_vcopied, s + 1 if proj else AH)
                    pe.wait_ge(q.a_tcopied, 4 * hd + 4)
                    for j in range(NQ):
                        mm = pe.matmul(obank[:, j * P:S], a_v[:, 1 - par, j, :], a_pt[:, j, j * P:S],
                                       start=j == 0, stop=j == NQ - 1)
                    mm.then_inc(q.a_pv, 1)

            a_steps(pe, a_step)
            output_products("a_wo", 0, gs, 0)
            end_stage(pe, 2)
            ffn(0)
            end_stage(pe, 3)
            norm_sums("ple0")
            ple(0)
            end_stage(pe, 4)

            norm_sums("attn1")
            pe.wait_ge(q.h_gained2, DC)
            for name, n, rhs in (("b_dkv", 3, parts(b_g2_hi, b_g2_lo, DC)), ("b_dq", 4, gs)):
                for k in range(n):
                    t = TILE[name] + k
                    tile(t, t % 2, weights(name, k), 0, rhs)
            for n, (tiles, m) in enumerate((((0, 1), ones), ((2,), ones64), ((3, 4, 5, 6), ones))):
                pe.wait_ge(q.bd_squared, tiles[-1] + 1)
                wait(pe, q.bd_logged, n)
                for t in tiles:
                    mm = pe.matmul(stat[:, :], m, b_dsq[:, t, :], start=t == tiles[0], stop=t == tiles[-1])
                mm.then_inc(q.bd_summed, 1)
            pe.wait_ge(q.bd_normed, 7)
            pe.matmul(obank[:, :], rot, b_rt[:, 0, :], start=True, stop=True).then_inc(q.bd_rotated, 1)
            end_stage(pe, 5)

            def b_step(s, par, proj, attn):
                cq, ck = parts(b_cq_hi, b_cq_lo, 4), parts(b_ckv_hi, b_ckv_lo, 2)
                at_ = (0, 4, 8, 0, 2, 4, 6)

                def lin_(j):
                    if proj:
                        t = TILE["b_pair"] + 7 * par + j
                        w = weights("b_pair", int(j >= 3), 2 * s)
                        tile(TILE["b_pair"] + 7 * s + j, t % 2, w, at_[j], cq if j < 3 else ck)

                def score(x, i):
                    if attn:
                        n = 8 * (s - 1) + 4 * x + i
                        if x == 0 and i == 0:
                            pe.wait_ge(q.b_normed, 5 * s)
                            pe.wait_ge(q.b_rope, s)
                        wait(pe, q.b_biased, n - 1)
                        qb = slice(i * P, (i + 1) * P)
                        rows = slice(64 * x, 64 * x + 64)
                        pe.matmul(scores[:, i % 2, 0:LEN[i]], b_qn[:, 1 - par, x, qb], b_kn[:, 1 - par, x, 0:LEN[i]],
                                  start=True, stop=False)
                        pe.matmul(scores[:, i % 2, 0:LEN[i]], b_qp[rows, 1 - par, qb], b_kp[rows, 0:LEN[i]],
                                  start=False, stop=True).then_inc(q.b_scored, 1)

                def sums(j):
                    if proj:
                        pe.wait_ge(q.b_squared, 5 * s + j + 1)
                        wait(pe, q.b_logged, 5 * s + j)
                        pe.matmul(stat[:, :], ones64 if j == 2 else ones, b_sq[:, j, :], start=True, stop=True)\
                            .then_inc(q.b_summed, 1)

                lin_(0); score(0, 0); lin_(1); score(0, 1); lin_(2); sums(0); score(0, 2); lin_(3); sums(1)
                score(0, 3); lin_(4); sums(2); score(1, 0); lin_(5); sums(3); score(1, 1); lin_(6); sums(4)
                score(1, 2)
                if proj:
                    pe.wait_ge(q.b_normed, 5 * s + 3)
                    wait(pe, q.b_otaken, 2 * s - 2)
                    wait(pe, q.b_vcopied, 2 * s)
                    pe.matmul(obank[:, :], rot, b_rt[:, 0, :], start=True, stop=True).then_inc(q.b_rotated, 1)
                score(1, 3)
                if proj:
                    for x in range(2):
                        pe.wait_ge(q.tile_taken, TILE["b_pair"] + 7 * s + 6 + x)
                        if x == 0:
                            pe.wait_ge(q.b_rope, s + 1)
                        else:
                            pe.wait_ge(q.b_vcopied, 2 * s + 1)
                        for j in range(NQ):
                            mm = pe.transpose(obank[:, j * P:(j + 1) * P], b_raw[:, 5 + x, j * P:(j + 1) * P], ident)
                        mm.then_inc(q.b_vturned, 1)
                if attn:
                    for x in range(2):
                        n = 8 * (s - 1) + 4 * x
                        for i in range(NQ):
                            pe.wait_ge(q.b_weights, n + i + 1)
                            wait(pe, q.b_tcopied, n + i - 1)
                            turn_weights(b_sc[:, x, i, :], i, turn[:, i % 2, :]).then_inc(q.b_turned, 1)
                        pe.wait_ge(q.b_tcopied, n + 4)
                        if x == 0:
                            pe.wait_ge(q.b_vcopied, 2 * s + 2 if proj else 2 * B_PAIRS)
                            wait(pe, q.b_otaken, 2 * s - 2)
                        else:
                            pe.wait_ge(q.b_otaken, 2 * s - 1)
                        for j in range(NQ):
                            mm = pe.matmul(obank[:, j * P:S], b_v[:, 1 - par, x, j * P:(j + 1) * P], b_pt[:, j, j * P:S],
                                           start=j == 0, stop=j == NQ - 1)
                        mm.then_inc(q.b_pv, 1)

            b_steps(pe, b_step)
            output_products("b_wo", DC, parts(b_o_hi, b_o_lo, BH), 1)
            end_stage(pe, 6)
            ffn(1)
            end_stage(pe, 7)
            norm_sums("ple1")
            ple(1)
            end_stage(pe, 8)
            pe.wait_ge(q.extra_in, 16 * 4)
            for hd in range(CH):
                b = (scores[:, 0, :], scores[:, 1, :], turn[:, 0, :], turn[:, 1, :])[hd % 4]
                if hd >= 4:
                    pe.wait_ge(q.g_rowed, G_ROWED + hd - 2)
                pe.matmul(b, relt[:, hd:hd + 1].broadcast_to([BUCKETS, P]), onehot, start=True, stop=True)\
                    .then_inc(q.g_made, 1)
            norm_sums("mix2")
            linear("c_in", (gs, gs), 23)
            end_stage(pe, 9)

            for k in range(8):
                w = weights("c_cmp", k)
                pe.wait_ge(q.zp_made, 16)
                t = TILE["c_cmp"] + k
                pe.wait_ge(q.tile_taken, t - 1)
                for c in range(8):
                    for x in range(2):
                        mm = pe.matmul(lin[:, t % 2, 0:2 * NCMP], w[x][:, c * P:(c + 1) * P].bitcast(F32),
                                       c_zp[:, k // 4, 8 * (k % 2) + c, :], start=c == 0 and x == 0,
                                       stop=c == 7 and x == 1)
                mm.then_inc(q.tile_done, 1)
            for k in range(NQ):
                mm = pe.transpose(stat[:, k * P:(k + 1) * P], c_z[:, 22, k * P:(k + 1) * P], ident)
            mm.then_inc(q.gates_turned, 1)
            for x in range(2):
                for j in range(NQ):
                    mm = pe.transpose(turn[:, x, j * P:(j + 1) * P], c_z[:, 6 + x, j * P:(j + 1) * P], ident)
                mm.then_inc(q.c_vturned, 1)
            pe.wait_ge(q.hid_act, 4)
            for x in range(2):
                for c in range(2):
                    mm = pe.matmul(obank[64 * x:64 * x + 64, 0:NCMP], w2c[:, c, :],
                                   c_hid[:, c, x * NCMP:(x + 1) * NCMP], start=c == 0, stop=c == 1)
            mm.then_inc(q.kc_made, 1)
            pe.wait_ge(q.kc_copied, 1)
            for x in range(2):
                for c in range(2):
                    mm = pe.matmul(obank[0:NCMP, x * CD:(x + 1) * CD], c_hid[:, 2 + c, x * NCMP:(x + 1) * NCMP],
                                   w2c[:, 2 + c, :], start=c == 0, stop=c == 1)
            mm.then_inc(q.kc_made, 1)
            pe.wait_ge(q.kc_copied, 3)
            for kv in range(2):
                for t in range(4):
                    for i in range(NQ):
                        hd = 4 * kv + t
                        at_ = (t * NQ + i) * NCMP
                        mm = pe.matmul(scores[:, kv, at_:at_ + NCMP], c_z[64 * kv:64 * kv + 64, t, i * P:(i + 1) * P],
                                       c_kc[64 * kv:64 * kv + 64, 0:NCMP], start=True, stop=True)
                mm.then_inc(q.cc_scored, 1)
            for hd in range(CH):
                pe.wait_ge(q.cc_scaled, 1)
                pe.wait_ge(q.c_vcopied, 2)
                wait(pe, q.cc_copied, hd - 1)
                for i in range(NQ):
                    mm = pe.transpose(turn[0:NCMP, hd % 2, i * P:(i + 1) * P], c_cs[:, hd, i, :], ident)
                mm.then_inc(q.cc_turned, 1)
            end_stage(pe, 10)

            for s in range(CH + 1):
                for i in range(NQ):
                    if s < CH:
                        rows = slice(64 * (s // 4), 64 * (s // 4) + 64)
                        wait(pe, q.c_biased, 4 * s + i)
                        for x in range(2):
                            mm = pe.matmul(scores[:, x, 0:LEN[i]], c_z[rows, s % 4, i * P:(i + 1) * P],
                                           c_z[rows, 4 + x, 0:LEN[i]], start=True, stop=True)
                        mm.then_inc(q.c_scored, 1)
                    if s > 0:
                        n = 4 * (s - 1) + i
                        pe.wait_ge(q.c_weights, 2 * n + 2)
                        for x in range(2):
                            wait(pe, q.c_tcopied, 2 * n - 1 + x)
                            turn_weights(c_sc[:, i, x, :], i, turn[:, x, :]).then_inc(q.c_turned, 1)
                if s > 0:
                    hd = s - 1
                    out_rows = slice(64 * (hd % 2), 64 * (hd % 2) + 64)
                    kv = hd // 4
                    pe.wait_ge(q.c_tcopied, 8 * hd + 8)
                    wait(pe, q.c_otaken, hd // 2)
                    for j in range(NQ):
                        for x in range(2):
                            pe.matmul(obank[out_rows, j * P:S], c_v[:, x, j, kv * CD:(kv + 1) * CD],
                                      c_pt[:, x, j, j * P:S], start=j == 0 and x == 0, stop=False)
                    pe.matmul(obank[out_rows, :], c_vc[0:NCMP, kv, :], c_ct[0:NCMP, hd, :],
                              start=False, stop=True).then_inc(q.c_pv, 1)
            end_stage(pe, 11)

            pe.matmul(stat[:, :], walpha[32:48, :], c_z[32:48, 22, :], start=True, stop=True).then_inc(q.gl_alpha, 1)
            pe.wait_ge(q.gl_prod, 3)
            for hd in range(GH):
                rows = slice(GK * hd, GK * hd + GK)
                b = (scores[:, 0, :], scores[:, 1, :], turn[:, 0, :], turn[:, 1, :])[hd]
                for n in range(NCH):
                    ch = slice(n * GCH, (n + 1) * GCH)
                    mm = pe.matmul(b[64 * (n % 2):64 * (n % 2) + 64, (n // 2) * GCH:(n // 2 + 1) * GCH],
                                   gl_kt[rows, ch], gl_qt[rows, ch], start=True, stop=True)
                mm.then_inc(q.gl_att, 1)
            for j in range(NQ):
                mm = pe.transpose(obank[:, j * P:(j + 1) * P], gl_kd[:, j * P:(j + 1) * P], ident)
            mm.then_inc(q.gl_kdt, 1)
            for x in range(2):
                for j in range(NQ):
                    mm = pe.transpose(lin[:, x, j * P:(j + 1) * P], c_z[:, 18 + x, j * P:(j + 1) * P], ident)
                mm.then_inc(q.gl_kdt, 1)
            pe.wait_ge(q.gl_kdc, 3)
            pe.wait_ge(q.gl_attc, 4)
            for n in range(NCH):
                rows = slice(64 * (n % 2), 64 * (n % 2) + 64)
                b = (scores[:, 0, :], scores[:, 1, :])[n % 2]
                if n >= 2:
                    pe.wait_ge(q.gl_uc, 4 * (n - 1))
                mm = pe.matmul(b[:, 0:2 * P], gl_kdt[rows, n // 2, :], gl_vt[rows, n // 2, :], start=True, stop=True)
                mm.then_inc(q.gl_u, 1)
            pe.wait_ge(q.gl_mask, 2)
            for x in range(2):
                for odd in range(2):
                    rows = slice(64 * odd, 64 * odd + 64)
                    b = (lin[:, 0, :], lin[:, 1, :], turn[:, 0, :], turn[:, 1, :])[2 * x + odd]
                    for y in range(2):
                        for n2 in range(NCH // 2):
                            mm = pe.matmul(b[64 * y:64 * y + 64, n2 * GCH:(n2 + 1) * GCH],
                                           gl_vt[rows, n2, (2 * x + y) * GV:(2 * x + y + 1) * GV],
                                           gl_am[rows, 2 * x + y, n2, :], start=True, stop=True)
                    mm.then_inc(q.gl_out, 1)
            pe.wait_ge(q.gl_bd, 4)
            for x in range(2):
                b = (stat, obank)[x]
                for n in range(NCH):
                    ch = slice(n * GCH, (n + 1) * GCH)
                    mm = pe.matmul(b[:, ch], gl_bds[:, n, x * P:(x + 1) * P], gl_qt[:, ch], start=True, stop=True)
                mm.then_inc(q.gl_out, 1)
            for x in range(2):
                pe.wait_ge(q.gl_sq, x + 1)
                pe.wait_ge(q.gl_sum, 2)
                wait(pe, q.gl_log, x)
                pe.matmul(stat[:, :], ones64, gl_s[:, x, :], start=True, stop=True).then_inc(q.gl_ss, 1)
            pe.wait_ge(q.gl_log, 2)
            pe.wait_ge(q.conv_step, 2 * CW)
            for x in range(2):
                mm = pe.matmul(stat[:, :], ones, c_acc[:, x, :], start=x == 0, stop=x == 1)
            mm.then_inc(q.ln_summed, 1)
            pe.wait_ge(q.ln_sq, 2)
            for x in range(2):
                mm = pe.matmul(obank[:, :], ones, gl_s[:, x, :], start=x == 0, stop=x == 1)
            mm.then_inc(q.ln_summed, 1)
            end_stage(pe, 12)
            output_products("c_out", DC + BH, gs, 0)
            end_stage(pe, 13)
            norm_sums("ffn2")
            ffn_products(2)
            end_stage(pe, 14)
            norm_sums("ple2")
            ple(2)
            end_stage(pe, 15)
            norm_sums("final")


        @block.vector
        def _(ve):
            rounded = [0]

            def gains(name, hi=g_hi, lo=g_lo, signal=None):
                for c in range(DC):
                    rounded[0] += 1
                    ve.wait_ge(q.h_rounded, rounded[0])
                    ve.scalar_tensor_tensor(out=lo[:, c, :], in0=h[:, c, :], scalar=v1(name, c), in1=hi[:, c, :].bitcast(F32),
                                            op0=ALU.mult, op1=ALU.subtract).then_inc(signal or q.h_gained, 1)

            def out_lows(n, src, hi, lo, chunks):
                for k in chunks:
                    ve.wait_ge(q.out_rounded, n + k + 1)
                    ve.tensor_tensor(lo[:, k, :], src[:, k, :], hi[:, k, :].bitcast(F32), ALU.subtract)\
                        .then_inc(q.out_split, 1)

            def residual(name):
                t = TILE[name]
                if name in ("ffn0_out", "ffn1_out", "ffn2_out", "b_wo"):
                    with ve.Fori(0, DC) as i:
                        for u in range(2):
                            ve.wait_ge(q.tile_done, 2 * i + t + u + 1)
                            wait(ve, q.tile_taken, 2 * i + t + u)
                            ve.tensor_tensor(h[:, i, :], lin[:, (t + u) % 2, :], h[:, i, :], ALU.add)\
                                .then_inc(q.tile_taken, 1)
                    return
                with ve.Fori(0, DC // 2) as i:
                    for u in range(2):
                        ve.wait_ge(q.tile_done, 2 * i + t + u + 1)
                        ve.tensor_tensor(h[:, 2 * i + u, :], lin[:, (t + u) % 2, :], h[:, 2 * i + u, :], ALU.add)\
                            .then_inc(q.tile_taken, 1)

            def take(t, par, dst):
                ve.wait_ge(q.tile_done, t + 1)
                ve.tensor_tensor(dst, lin[:, par, :], r[:, :], ALU.mult).then_inc(q.tile_taken, 1)

            def bias_of_any_positions():
                def built(ins, value):
                    ins.then_inc(q.bias_built, 1)
                    ve.wait_ge(q.bias_built, value)

                ve.wait_ge(q.table_in, 48)
                built(ve.tensor_tensor(a_diff[:, AH:], a_tab[:, AH:], a_tab[:, 0:(BUCKETS - 1) * AH], ALU.subtract), 1)
                for i in range(NQ):
                    ve.tensor_scalar(a_dist[:, OFF[i]:OFF[i] + LEN[i]], posf[:, 0:LEN[i]], -1.0, posq[:, i:i + 1],
                                     ALU.mult, ALU.add).then_inc(q.bias_built, 1)
                    for hd in range(AH):
                        ve.tensor_scalar(a_bias[:, hd, OFF[i]:OFF[i] + LEN[i]], maskt[:, S - LEN[i]:S],
                                         a_tab[:, hd:hd + 1], None, ALU.add).then_inc(q.bias_built, 1)
                base = 1 + NQ * (1 + AH)
                with ve.Fori(0, BUCKETS - 1) as b:
                    ve.wait_ge(q.bias_built, base + (1 + AH) * b)
                    ve.tensor_scalar(a_mask, a_dist, vec[:, bass.ds(VEC["t5_start"] + b, 1)], None, ALU.is_ge)\
                        .then_inc(q.bias_built, 1)
                    ve.wait_ge(q.bias_built, base + 1 + (1 + AH) * b)
                    for hd in range(AH):
                        ve.scalar_tensor_tensor(out=a_bias[:, hd, :], in0=a_mask, scalar=a_diff[:, bass.ds(AH * b + AH + hd, 1)],
                                                in1=a_bias[:, hd, :], op0=ALU.mult, op1=ALU.add).then_inc(q.bias_built, 1)
                ve.wait_ge(q.bias_built, base + (1 + AH) * (BUCKETS - 1))

            def hidden(n, i, u, k):
                at_ = 2 * FC * n + 4 * i + 2 * u
                ve.tensor_tensor(f_c[:, k, :], f_c[:, k, :], f_sg[:, u, :], ALU.mult).then_inc(q.f_split, 1)
                ve.wait_ge(q.f_split, at_ + 1)
                ve.tensor_copy(f_hi[:, 2 * i + u, :], f_c[:, k, :]).then_inc(q.f_split, 1)
                ve.wait_ge(q.f_split, at_ + 2)
                ve.tensor_tensor(f_lo[:, 2 * i + u, :], f_c[:, k, :], f_hi[:, 2 * i + u, :].bitcast(F32), ALU.subtract)\
                    .then_inc(q.f_through, 1)

            def conv_ffn(n):
                gains(f"ffn{n}")
                ve.wait_ge(q.r_ready, NORM[f"ffn{n}"] + 1)
                t0, f0 = TILE[f"ffn{n}_in"], 2 * FC * n

                def pair(i, u):
                    for j in range(2):
                        k = 2 * u + j
                        ve.wait_ge(q.tile_done, t0 + k + 1 + 4 * i)
                        wait(ve, q.f_first, f0 + 4 * i + k - 3)
                        ve.tensor_tensor(f_u[:, k, 2:S + 2], lin[:, (t0 + k) % 2, :], r[:, :], ALU.mult)\
                            .then_inc(q.tile_taken, 1)
                    for j in range(2):
                        k = 2 * u + j
                        w = VEC[f"conv{n}"] + 4 * k + 16 * i
                        ve.wait_ge(q.f_first, f0 + k + 1 + 4 * i)
                        ve.scalar_tensor_tensor(out=f_c[:, k, :], in0=f_u[:, k, 1:S + 1], scalar=vec[:, bass.ds(w + 1, 1)],
                                                in1=f_c[:, k, :], op0=ALU.mult, op1=ALU.add).then_inc(q.f_conv, 1)
                        ve.wait_ge(q.f_conv, 2 * f0 + 2 * k + 1 + 8 * i)
                        ve.scalar_tensor_tensor(out=f_c[:, k, :], in0=f_u[:, k, 0:S], scalar=vec[:, bass.ds(w, 1)],
                                                in1=f_c[:, k, :], op0=ALU.mult, op1=ALU.add).then_inc(q.f_conv, 1)
                    ve.wait_ge(q.f_silu, FC * n + u + 1 + 2 * i)
                    ve.wait_ge(q.f_conv, 2 * f0 + 4 * u + 4 + 8 * i)
                    hidden(n, i, u, 2 * u)

                ve.memset(f_u[:, :, 0:2], 0.0).then_inc(q.setup_step, 1)
                ve.wait_ge(q.setup_step, SETUP + n + 1)
                pair(0, 0)
                pair(0, 1)
                with ve.Fori(1, FC // 2) as i:
                    pair(i, 0)
                    pair(i, 1)
                residual(f"ffn{n}_out")

            def ple(n):
                gains(f"ple{n}")
                ve.wait_ge(q.p_in, 16 * (n + 1))
                ve.tensor_copy(p_hi[:, :, :], p_in_t[:, :, :]).then_inc(q.p_split, 1)
                ve.wait_ge(q.p_split, 2 * n + 1)
                ve.tensor_tensor(p_lo[:, :, :], p_in_t[:, :, :], p_hi[:, :, :].bitcast(F32), ALU.subtract).then_inc(q.p_split, 1)
                ve.wait_ge(q.r_ready, NORM[f"ple{n}"] + 1)
                t0, g0 = TILE[f"ple{n}"], DC * n

                def one(i, j):
                    b = j % 2
                    ve.wait_ge(q.tile_done, t0 + 2 * j + 1 + 8 * i)
                    ve.tensor_tensor(p_gp[:, b, :], lin[:, (t0 + 2 * j) % 2, :], r[:, :], ALU.mult)\
                        .then_inc(q.tile_taken, 1)
                    ve.wait_ge(q.tile_done, t0 + 2 * j + 2 + 8 * i)
                    ve.wait_ge(q.ple_sigmoid, g0 + j + 1 + 4 * i)
                    ve.tensor_tensor(p_t[:, b, :], lin[:, (t0 + 2 * j + 1) % 2, :], p_sg[:, b, :], ALU.mult)\
                        .then_inc(q.tile_taken, 1)
                    ve.wait_ge(q.tile_taken, t0 + 2 * j + 2 + 8 * i)
                    ve.tensor_tensor(h[:, 4 * i + j, :], h[:, 4 * i + j, :], p_t[:, b, :], ALU.add)\
                        .then_inc(q.residual_added, 1)
                with ve.Fori(0, 2) as i:
                    for j in range(4):
                        one(i, j)

            steps = [0]

            def did(ins):
                steps[0] += 1
                ins.then_inc(q.setup_step, 1)
                ve.wait_ge(q.setup_step, steps[0])

            ve.memset(a_neg, NEG).then_inc(q.g_rowed, 1)
            did(ve.memset(eps[:, :], EPS))
            for hd in range(AH):
                ve.wait_ge(q.g_made, hd + 1)
                b = (scores[:, 0, :], scores[:, 1, :], turn[:, 0, :], turn[:, 1, :])[hd % 4]
                ve.tensor_copy(a_grow[:, hd, :], b).then_inc(q.g_rowed, 1)
            ve.wait_ge(q.consts_in, 32)
            ve.wait_ge(q.x_in, 16 * DC)
            gains("attn0")
            ve.wait_ge(q.positions_in, 16 * (NQ + 1))
            did(ve.tensor_copy(posf, pos_i))
            did(ve.tensor_copy(posq, posq_i[:, :]))
            did(ve.tensor_tensor(a_step_ok, posf[:, 1:S], posf[:, 0:S - 1], ALU.subtract))
            did(ve.tensor_scalar(a_step_ok, a_step_ok, 1.0, None, ALU.is_equal))
            did(ve.tensor_reduce(regular[:, 0:1], a_step_ok, AX.X, ALU.min))
            did(ve.tensor_copy(regular_i[:, :], regular[:, 0:1]))
            ve.wait_ge(q.lam_in, 16)
            for x in range(2):
                did(ve.tensor_tensor(a_lam[:, 4, :], a_lam[:, 2 * x, :], a_lam[:, 2 * x + 1, :], ALU.mult))
                did(ve.tensor_reduce(lamd[:, x:x + 1], a_lam[:, 4, :], AX.X, ALU.add))
            ve.sem_inc(q.lam_dots, 1)
            turn_parts = (6.28125, 0.0019340515136718750, 2 * math.pi - 6.28125 - 0.0019340515136718750)
            ang, k_ = cosb[:, :], a_rawo
            did(ve.tensor_scalar(ang, posf, v1("inv_freq"), None, ALU.mult))
            did(ve.tensor_scalar(k_, ang, 1 / (2 * math.pi), 12582912.0, ALU.mult, ALU.add))
            did(ve.tensor_scalar(k_, k_, 12582912.0, None, ALU.subtract))
            for part in turn_parts:
                did(ve.scalar_tensor_tensor(out=ang, in0=k_, scalar=-part, in1=ang, op0=ALU.mult, op1=ALU.add))
            did(ve.tensor_scalar(sinb[:, :], ang, PI_IN, -PI_IN, ALU.min, ALU.max))
            did(ve.tensor_scalar(ang, ang, math.pi / 2, None, ALU.add))
            did(ve.tensor_scalar(k_, ang, math.pi, -2 * math.pi, ALU.is_gt, ALU.mult))
            did(ve.tensor_tensor(ang, ang, k_, ALU.add))
            did(ve.tensor_scalar(ang, ang, PI_IN, -PI_IN, ALU.min, ALU.max))
            ve.sem_inc(q.angles_ready, 1)
            ve.wait_ge(q.lam_exps, 1)
            did(ve.tensor_tensor(nlam, lame[:, 1:2], lame[:, 0:1], ALU.subtract))
            did(ve.tensor_scalar(nlam, nlam, LAM_INIT, None, ALU.subtract))
            did(ve.tensor_scalar(asub, v1("a_sub"), 1.0 - LAM_INIT, None, ALU.mult))
            SETUP = steps[0]
            ve.wait_ge(q.g_read, 16 * NQ)
            in_a_row = ve.value_load(regular_i[0:1, 0:1])
            with ve.If(in_a_row < 1):
                bias_of_any_positions()
            ve.wait_ge(q.r_ready, 1)

            def a_step(s, par, proj, attn, tail):
                hd = s - 1

                def take_(j):
                    if proj:
                        take(TILE["a_qkv"] + 3 * s + j, (TILE["a_qkv"] + 3 * par + j) % 2, a_raw[:, j, :])

                def biased(i):
                    if attn:
                        n = 4 * hd + i
                        ve.wait_ge(q.a_scored, n + 1)
                        wait(ve, q.a_turned, n - 3)
                        bias = a_bias[:, hd, OFF[i]:OFF[i] + LEN[i]] if isinstance(hd, int) else \
                            a_bias[:, bass.ds(hd, 1), OFF[i]:OFF[i] + LEN[i]].rearrange("p a l -> p (a l)")
                        ve.scalar_tensor_tensor(out=a_sc[:, i, :, 0:LEN[i]], in0=scores[:, :, 0:LEN[i]],
                                                scalar=-(AQK ** -0.5),
                                                in1=bias.unsqueeze(1).broadcast_to([P, 2, LEN[i]]),
                                                op0=ALU.mult, op1=ALU.subtract).then_inc(q.a_biased, 1)
                        ve.wait_ge(q.a_biased, n + 1)
                        ve.tensor_reduce(nmax[:, 2 * i:2 * i + 2], a_sc[:, i, :, 0:LEN[i]], AX.X, ALU.min)\
                            .then_inc(q.a_min, 1)

                def weights_(i):
                    if attn:
                        n = 4 * hd + i
                        d = den[:, 2 * i:2 * i + 2]
                        ve.wait_ge(q.a_exped, 2 * n + 2)
                        ve.reciprocal(d, d).then_inc(q.a_recip, 1)
                        ve.wait_ge(q.a_recip, 2 * n + 1)
                        ve.tensor_tensor(d[:, 1:2], d[:, 1:2], nlam, ALU.mult).then_inc(q.a_recip, 1)
                        ve.tensor_scalar(a_sc[:, i, 0, 0:LEN[i]], a_sc[:, i, 0, 0:LEN[i]], d[:, 0:1], None, ALU.mult)\
                            .then_inc(q.a_scaled, 1)
                        ve.wait_ge(q.a_recip, 2 * n + 2)
                        ve.wait_ge(q.a_scaled, n + 1)
                        ve.scalar_tensor_tensor(out=a_sc[:, i, 0, 0:LEN[i]], in0=a_sc[:, i, 1, 0:LEN[i]],
                                                scalar=d[:, 1:2], in1=a_sc[:, i, 0, 0:LEN[i]], op0=ALU.mult,
                                                op1=ALU.add).then_inc(q.a_weights, 1)

                def normed(j):
                    if proj:
                        ve.wait_ge(q.a_factor, 2 * s + j + 1)
                        ve.scalar_tensor_tensor(out=a_qk[:, par, j, :], in0=a_raw[:, j, :],
                                                scalar=v1("a_q" if j == 0 else "a_k"), in1=a_ri[:, j, :],
                                                op0=ALU.mult, op1=ALU.mult).then_inc(q.a_normed, 1)

                take_(0)
                if tail:
                    ve.wait_ge(q.a_ofactor, s - 1)
                    ve.scalar_tensor_tensor(out=a_o[:, s - 2, :], in0=a_rawo, scalar=asub, in1=a_ri[:, 2, :],
                                            op0=ALU.mult, op1=ALU.mult).then_inc(q.a_onormed, 1)
                biased(0)
                take_(1)
                biased(1)
                weights_(0)
                normed(0)
                take_(2)
                biased(2)
                weights_(1)
                normed(1)
                biased(3)
                weights_(2)
                weights_(3)
                if attn:
                    ve.wait_ge(q.a_pv, s)
                    ve.tensor_copy(a_rawo, obank[:, :]).then_inc(q.a_otaken, 1)

            a_steps(ve, a_step)
            out_lows(0, a_o, g_hi, g_lo, range(DC))
            residual("a_wo")
            end_stage(ve, 2)
            conv_ffn(0)
            end_stage(ve, 3)
            ple(0)
            end_stage(ve, 4)

            gains("kv", b_g2_hi, b_g2_lo, q.h_gained2)
            gains("attn1")
            ve.wait_ge(q.r_ready, NORM["attn1"] + 1)
            t0 = TILE["b_dkv"]
            for j in range(7):
                take(t0 + j, (t0 + j) % 2, b_cr[:, j, :])
            for n, (tiles, vname) in enumerate((((0, 1), "ckv"), ((2,), "k_pe"), ((3, 4, 5, 6), "cq"))):
                ve.wait_ge(q.bd_factor, n + 1)
                for k, j in enumerate(tiles):
                    dst = b_rt[:, 0, :] if n == 1 else b_cr[:, j, :]
                    ve.scalar_tensor_tensor(out=dst, in0=b_cr[:, j, :], scalar=v1(vname, k), in1=b_ri[:, n, :],
                                            op0=ALU.mult, op1=ALU.mult).then_inc(q.bd_normed, 1)
            for k, j in enumerate((0, 1, 3, 4, 5, 6)):
                hi = b_ckv_hi[:, k, :] if k < 2 else b_cq_hi[:, k - 2, :]
                ve.wait_ge(q.bd_normed, j + 1)
                ve.tensor_copy(hi, b_cr[:, j, :]).then_inc(q.bd_rounded, 1)
            for k, j in enumerate((0, 1, 3, 4, 5, 6)):
                hi = b_ckv_hi[:, k, :] if k < 2 else b_cq_hi[:, k - 2, :]
                lo = b_ckv_lo[:, k, :] if k < 2 else b_cq_lo[:, k - 2, :]
                ve.wait_ge(q.bd_rounded, k + 1)
                ve.tensor_tensor(lo, b_cr[:, j, :], hi.bitcast(F32), ALU.subtract)
            ve.wait_ge(q.bd_rotated, 1)
            ve.tensor_tensor(b_rt[:, 1, :], obank[:, :], sinb[:, :], ALU.mult).then_inc(q.bd_terms, 1)
            ve.tensor_tensor(b_rt[:, 2, :], b_rt[:, 0, :], cosb[:, :], ALU.mult).then_inc(q.bd_terms, 1)
            ve.wait_ge(q.bd_terms, 2)
            ve.tensor_tensor(b_kp, b_rt[:, 1, :], b_rt[:, 2, :], ALU.add).then_inc(q.bd_terms, 1)
            end_stage(ve, 5)

            def b_step(s, par, proj, attn):
                def take_(j):
                    if proj:
                        ve.wait_ge(q.tile_done, TILE["b_pair"] + 7 * s + j + 1)
                        ve.tensor_copy(b_raw[:, j, :], lin[:, (TILE["b_pair"] + 7 * par + j) % 2, :])\
                            .then_inc(q.tile_taken, 1)

                def biased(x, i):
                    if attn:
                        n = 8 * (s - 1) + 4 * x + i
                        ve.wait_ge(q.b_scored, n + 1)
                        wait(ve, q.b_turned, n - 7)
                        ve.scalar_tensor_tensor(out=b_sc[:, x, i, 0:LEN[i]], in0=scores[:, i % 2, 0:LEN[i]],
                                                scalar=-((NOPE + ROPE) ** -0.5), in1=maskt[:, S - LEN[i]:S],
                                                op0=ALU.mult, op1=ALU.subtract).then_inc(q.b_biased, 1)
                        ve.wait_ge(q.b_biased, n + 1)
                        ve.tensor_reduce(nmax[:, 4 * x + i:4 * x + i + 1], b_sc[:, x, i, 0:LEN[i]], AX.X, ALU.min)\
                            .then_inc(q.b_min, 1)

                def weights_(x, i):
                    if attn:
                        n = 8 * (s - 1) + 4 * x + i
                        d = den[:, 4 * x + i:4 * x + i + 1]
                        ve.wait_ge(q.b_exped, n + 1)
                        ve.reciprocal(d, d).then_inc(q.b_recip, 1)
                        ve.wait_ge(q.b_recip, n + 1)
                        ve.tensor_scalar(b_sc[:, x, i, 0:LEN[i]], b_sc[:, x, i, 0:LEN[i]], d, None, ALU.mult)\
                            .then_inc(q.b_weights, 1)

                def normed(j):
                    if proj:
                        ve.wait_ge(q.b_factor, 5 * s + j + 1)
                        dst = (b_qn[:, par, 0, :], b_qn[:, par, 1, :], b_rt[:, 0, :], b_kn[:, par, 0, :],
                               b_kn[:, par, 1, :])[j]
                        vname = ("q_nope", "q_nope", "q_pe", "k_nope", "k_nope")[j]
                        ve.scalar_tensor_tensor(out=dst, in0=b_raw[:, j, :], scalar=v1(vname), in1=b_ri[:, j, :],
                                                op0=ALU.mult, op1=ALU.mult).then_inc(q.b_normed, 1)

                take_(0); biased(0, 0); take_(1); biased(0, 1); weights_(0, 0); take_(2); biased(0, 2)
                weights_(0, 1); normed(0); take_(3); biased(0, 3); weights_(0, 2); normed(1); take_(4)
                biased(1, 0); weights_(0, 3); normed(2); take_(5); biased(1, 1); weights_(1, 0); normed(3)
                take_(6); biased(1, 2); weights_(1, 1); normed(4)
                if proj:
                    ve.wait_ge(q.b_rotated, s + 1)
                    ve.tensor_tensor(b_rt[:, 1, :], obank[:, :], sinb[:, :], ALU.mult).then_inc(q.b_terms, 1)
                    ve.tensor_tensor(b_rt[:, 2, :], b_rt[:, 0, :], cosb[:, :], ALU.mult).then_inc(q.b_terms, 1)
                    ve.wait_ge(q.b_terms, 2 * s + 2)
                    ve.tensor_tensor(b_qp[:, par, :], b_rt[:, 1, :], b_rt[:, 2, :], ALU.add).then_inc(q.b_rope, 1)
                biased(1, 3); weights_(1, 2); weights_(1, 3)
                if attn:
                    for x in range(2):
                        ve.wait_ge(q.b_pv, 2 * s - 1 + x)
                        ve.tensor_copy(b_o[:, 2 * (s - 1) + x, :], obank[:, :]).then_inc(q.b_otaken, 1)

            b_steps(ve, b_step)
            out_lows(DC, b_o, b_o_hi, b_o_lo, range(BH))
            residual("b_wo")
            end_stage(ve, 6)
            conv_ffn(1)
            end_stage(ve, 7)
            ple(1)
            end_stage(ve, 8)

            gains("mix2")
            ve.memset(neg, NEG).then_inc(q.g_rowed, 1)
            for hd in range(CH):
                ve.wait_ge(q.g_made, AH + hd + 1)
                b = (scores[:, 0, :], scores[:, 1, :], turn[:, 0, :], turn[:, 1, :])[hd % 4]
                ve.tensor_copy(c_bias[:, hd, :], b).then_inc(q.g_rowed, 1)
            ve.wait_ge(q.r_ready, NORM["mix2"] + 1)
            t0 = TILE["c_in"]
            def c_take(j, jj):
                ve.wait_ge(q.tile_done, t0 + j + 1)
                ve.tensor_tensor(c_z[:, j, :], lin[:, (t0 + jj) % 2, :], r[:, :], ALU.mult).then_inc(q.tile_taken, 1)
            with ve.Fori(0, 11) as i:
                for u in range(2):
                    c_take(2 * i + u, u)
            c_take(22, 22)
            ve.memset(c_hp[:, :, 0:CW - 1], 0.0).then_inc(q.c_glu, 1)
            for x in range(2):
                ve.wait_ge(q.c_sigmoid, x + 1)
                ve.tensor_tensor(c_hp[:, x, CW - 1:], c_z[:, 12 + x, :], c_acc[:, x, :], ALU.mult)\
                    .then_inc(q.c_glu, 1)
            end_stage(ve, 9)

            for k in range(4):
                z = c_z[:, 8 + k, :].rearrange("p (n l) -> p l n", l=CMPS)
                for half in range(2):
                    rows = slice(64 * half, 64 * half + 64)
                    for over in range(2):
                        pos = vec[rows, VEC["cmp_pos"] + 16 * (k // 2) + 8 * over:VEC["cmp_pos"] + 16 * (k // 2) + 8 * over + 8]
                        ins = ve.tensor_tensor(c_zp[rows, k // 2, 8 * over:8 * over + 8, (k % 2) * NCMP:(k % 2 + 1) * NCMP],
                                               z[rows, half::2, over:over + NCMP],
                                               pos.unsqueeze(2).broadcast_to([64, 8, NCMP]), ALU.add)
                        ins.then_inc(q.zp_made, 1)
            for k in range(4):
                t = TILE["c_cmp"] + 2 * k
                ve.wait_ge(q.tile_done, t + 1)
                ve.tensor_copy(c_hid[:, k, :], lin[:, t % 2, 0:2 * NCMP]).then_inc(q.tile_taken, 1)
                ve.wait_ge(q.tile_done, t + 2)
                ve.wait_ge(q.tile_taken, t + 1)
                ve.tensor_tensor(c_hid[:, k, :], lin[:, (t + 1) % 2, 0:2 * NCMP], c_hid[:, k, :], ALU.add)\
                    .then_inc(q.tile_taken, 1)
            ve.memset(c_cb[:, :, :, :], NEG).then_inc(q.cb_made, 1)
            ve.wait_ge(q.cb_made, 1)
            ve.wait_ge(q.g_read, G_READ + 16)
            for i in range(NQ):
                n = min(NCMP, 7 + 8 * i)
                first = S - P - P * i + CMPB - 1
                ve.tensor_copy(c_cb[:, :, i, 0:n], c_bias[:, :, first:first + CMPS * (n - 1) + 1:CMPS]).then_inc(q.cb_made, 1)
            ve.wait_ge(q.cb_made, 1 + NQ)
            ve.wait_ge(q.kc_made, 1)
            ve.tensor_copy(c_kc[:, 0:NCMP], obank[:, 0:NCMP]).then_inc(q.kc_copied, 1)
            ve.wait_ge(q.kc_made, 2)
            for x in range(2):
                ve.tensor_copy(c_vc[0:NCMP, x, :], obank[0:NCMP, x * CD:(x + 1) * CD]).then_inc(q.kc_copied, 1)
            for kv in range(2):
                ve.wait_ge(q.cc_scored, kv + 1)
                ve.scalar_tensor_tensor(
                    out=c_cs[:, 4 * kv:4 * kv + 4, :, :].rearrange("p h i n -> p (h i n)"), in0=scores[:, kv, 0:4 * NQ * NCMP],
                    scalar=-(CD ** -0.5), in1=c_cb[:, 4 * kv:4 * kv + 4, :, :].rearrange("p h i n -> p (h i n)"),
                    op0=ALU.mult, op1=ALU.subtract).then_inc(q.cc_biased, 1)
            ve.wait_ge(q.cc_biased, 2)
            cs3 = c_cs[:, :, :, :].rearrange("p h i n -> p (h i) n")
            ve.tensor_reduce(c_cmin, cs3, AX.X, ALU.min).then_inc(q.cc_reduced, 1)
            ve.wait_ge(q.cc_reduced, 1)
            ve.tensor_tensor(cs3, cs3, c_cmin.unsqueeze(2).broadcast_to([P, CH * NQ, NCMP]), ALU.subtract)\
                .then_inc(q.cc_reduced, 1)
            ve.wait_ge(q.cc_exped, 1)
            ve.tensor_reduce(c_cden, cs3, AX.X, ALU.add).then_inc(q.cc_reduced, 1)
            ve.wait_ge(q.cc_reduced, 3)
            ve.reciprocal(c_cden, c_cden).then_inc(q.cc_recip, 1)
            ve.wait_ge(q.cc_recip, 1)
            ve.wait_ge(q.gates_made, 1)
            d3 = c_cden.rearrange("p (h i) -> p h i", i=NQ)
            ve.tensor_tensor(d3, d3, c_ga[:, :, :].rearrange("p i (h b) -> p h i b", b=3)[:, :, :, 0], ALU.mult)\
                .then_inc(q.cc_recip, 1)
            ve.wait_ge(q.cc_recip, 2)
            ve.tensor_scalar(d3[:, :, 0], d3[:, :, 0], v1("first_block"), None, ALU.mult).then_inc(q.cc_recip, 1)
            ve.wait_ge(q.cc_recip, 3)
            ve.tensor_tensor(cs3, cs3, c_cden.unsqueeze(2).broadcast_to([P, CH * NQ, NCMP]), ALU.mult)\
                .then_inc(q.cc_scaled, 1)
            end_stage(ve, 10)

            def conv_tap(k):
                x, j = k % 2, k // 2
                if j == 0:
                    ve.wait_ge(q.c_glu, 3)
                    ve.tensor_scalar(c_acc[:, x, :], c_hp[:, x, 0:S], v1("dw", CW * x), v1("dw_b", x), ALU.mult,
                                     ALU.add).then_inc(q.conv_step, 1)
                elif j < CW:
                    ve.wait_ge(q.conv_step, k - 1)
                    ve.scalar_tensor_tensor(out=c_acc[:, x, :], in0=c_hp[:, x, j:j + S], scalar=v1("dw", CW * x + j),
                                            in1=c_acc[:, x, :], op0=ALU.mult, op1=ALU.add).then_inc(q.conv_step, 1)

            for s in range(CH):
                def weights_(i):
                    n = 4 * s + i
                    d = den[:, 2 * i:2 * i + 2]
                    ve.wait_ge(q.c_exped, 2 * n + 2)
                    ve.reciprocal(d, d).then_inc(q.c_recip, 1)
                    ve.wait_ge(q.c_recip, n + 1)
                    ve.tensor_tensor(d, d, c_ga[:, i, 3 * s + 1:3 * s + 3], ALU.mult).then_inc(q.c_gated, 1)
                    ve.wait_ge(q.c_gated, n + 1)
                    for x in range(2):
                        ve.tensor_scalar(c_sc[:, i, x, 0:LEN[i]], c_sc[:, i, x, 0:LEN[i]], d[:, x:x + 1], None,
                                         ALU.mult).then_inc(q.c_weights, 1)

                for i in range(NQ):
                    n = 4 * s + i
                    ve.wait_ge(q.c_scored, n + 1)
                    wait(ve, q.c_turned, 2 * n - 6)
                    ve.scalar_tensor_tensor(out=c_sc[:, i, :, 0:LEN[i]], in0=scores[:, :, 0:LEN[i]], scalar=-(CD ** -0.5),
                                            in1=c_bias[:, s:s + 1, S - LEN[i]:S].broadcast_to([P, 2, LEN[i]]),
                                            op0=ALU.mult, op1=ALU.subtract).then_inc(q.c_biased, 1)
                    ve.wait_ge(q.c_biased, n + 1)
                    ve.tensor_reduce(nmax[:, 2 * i:2 * i + 2], c_sc[:, i, :, 0:LEN[i]], AX.X, ALU.min).then_inc(q.c_min, 1)
                    if i:
                        weights_(i - 1)
                    for k in range(2):
                        conv_tap(8 * s + 2 * i + k)
                weights_(3)
                if s % 2 and s >= 3:
                    ve.wait_ge(q.c_pv, s - 1)
                    ve.tensor_copy(low[:, (s - 3) // 2, :], obank[:, :]).then_inc(q.c_otaken, 1)
            ve.wait_ge(q.c_pv, CH)
            ve.tensor_copy(low[:, 3, :], obank[:, :]).then_inc(q.c_otaken, 1)
            end_stage(ve, 11)

            ve.memset(gl_reset, 1.0).then_inc(q.gl_scale, 1)
            ve.wait_ge(q.gl_scale, 1)
            ve.memset(gl_reset.rearrange("p (n c) -> p n c", c=GCH)[:, :, 0:1], 0.0).then_inc(q.gl_scale, 1)
            ve.memset(gl_bds[:, :, :], 0.0).then_inc(q.gl_scale, 1)
            ve.wait_ge(q.gl_ln, 1)
            ve.scalar_tensor_tensor(out=gl_b, in0=gl_e[:, 1, :], scalar=0.0, in1=gl_e[:, 0, :], op0=ALU.min,
                                    op1=ALU.subtract).then_inc(q.gl_la, 1)
            ve.wait_ge(q.gl_la, 1)
            ve.tensor_scalar(gl_e[:, 0, :], gl_b, 1.0 / TAU, None, ALU.mult).then_inc(q.gl_la, 1)
            ve.wait_ge(q.gl_la, 2)
            ve.wait_ge(q.gl_scale, 3)
            ve.tensor_tensor_scan(gl_b, gl_reset, gl_e[:, 0, :], 0.0, ALU.mult, ALU.add).then_inc(q.gl_scan, 1)
            ve.wait_ge(q.gl_scan, 1)
            b3 = gl_b.rearrange("p (n c) -> p n c", c=GCH)
            ve.tensor_tensor(gl_e[:, 0, :].rearrange("p (n c) -> p n c", c=GCH), b3[:, :, GCH - 1:GCH].broadcast_to([P, NCH, GCH]),
                             b3, ALU.subtract).then_inc(q.gl_scan, 1)
            ve.wait_ge(q.gl_exps, 4)
            ve.scalar_tensor_tensor(out=gl_qt, in0=c_z[:, 16, :], scalar=GK ** -0.5, in1=gl_t[:, 0, :], op0=ALU.mult,
                                    op1=ALU.mult).then_inc(q.gl_prod, 1)
            ve.tensor_tensor(gl_kt, c_z[:, 17, :], gl_t[:, 1, :], ALU.mult).then_inc(q.gl_prod, 1)
            ve.tensor_tensor(gl_kd, c_z[:, 17, :], gl_e[:, 1, :], ALU.mult).then_inc(q.gl_prod, 1)
            for hd in range(GH):
                b = (scores[:, 0, :], scores[:, 1, :], turn[:, 0, :], turn[:, 1, :])[hd]
                ve.wait_ge(q.gl_att, hd + 1)
                ve.tensor_copy(gl_am[:, hd, :, :].rearrange("p n c -> p (n c)"), b[:, 0:NCH // 2 * GCH])\
                    .then_inc(q.gl_attc, 1)
            ve.wait_ge(q.gl_kdt, 1)
            ve.tensor_copy(gl_kdt[:, :, :].rearrange("p j c -> p (j c)"), obank[:, :]).then_inc(q.gl_kdc, 1)
            for x in range(2):
                ve.wait_ge(q.gl_kdt, 2 + x)
                ve.tensor_copy(gl_vt[:, :, x * P:(x + 1) * P], lin[:, x, :].rearrange("p (j c) -> p j c", c=P))\
                    .then_inc(q.gl_kdc, 1)
            for n in range(NCH):
                b = (scores[:, 0, :], scores[:, 1, :])[n % 2]
                ve.wait_ge(q.gl_u, n + 1)
                for hd in range(GH):
                    rows = slice(GK * hd, GK * hd + GK)
                    ve.tensor_copy(gl_us[rows, n, :], b[rows, hd * GV:(hd + 1) * GV]).then_inc(q.gl_uc, 1)
            ve.wait_ge(q.gl_uc, 4 * NCH)
            ve.memset(gl_st[:, 0, :], 0.0).then_inc(q.gl_state, 1)
            for n in range(1, NCH):
                ve.wait_ge(q.gl_state, n)
                ve.scalar_tensor_tensor(out=gl_st[:, n, :], in0=gl_st[:, n - 1, :], scalar=gl_dn[:, n - 1:n],
                                        in1=gl_us[:, n - 1, :], op0=ALU.mult, op1=ALU.add).then_inc(q.gl_state, 1)
            ve.wait_ge(q.gl_state, NCH)
            for hd in range(GH):
                rows = slice(GK * hd, GK * hd + GK)
                ve.tensor_copy(gl_bds[rows, :, hd * GV:(hd + 1) * GV], gl_st[rows, :, :]).then_inc(q.gl_bd, 1)
            for x in range(2):
                ve.wait_ge(q.gl_out, 5 + x)
                ve.tensor_copy(gl_o[:, x, :], (stat, obank)[x][:, :]).then_inc(q.gl_sum, 1)
            for x in range(2):
                for odd in range(2):
                    b = (lin[:, 0, :], lin[:, 1, :], turn[:, 0, :], turn[:, 1, :])[2 * x + odd]
                    o4 = gl_o[:, x, :].rearrange("p (n o c) -> p n o c", o=2, c=GCH)[:, :, odd, :]
                    ve.wait_ge(q.gl_sum, x + 1)
                    ve.tensor_tensor(o4, b[:, 0:NCH // 2 * GCH].rearrange("p (n c) -> p n c", c=GCH), o4, ALU.add)\
                        .then_inc(q.gl_add, 1)
            for x in range(2):
                ve.wait_ge(q.gl_fac, x + 1)
                ve.scalar_tensor_tensor(out=gl_t[:, x, :], in0=gl_o[:, x, :], scalar=v1("gla_g", x), in1=gl_e[:, x, :],
                                        op0=ALU.mult, op1=ALU.mult).then_inc(q.gl_norm, 1)
                ve.wait_ge(q.gl_norm, x + 1)
                ve.wait_ge(q.gl_silu, x + 1)
                ve.tensor_tensor(low[:, 6 + x, :], gl_t[:, x, :], c_z[:, 20 + x, :], ALU.mult)
            ve.wait_ge(q.ln_summed, 1)
            for x in range(2):
                ve.scalar_tensor_tensor(out=c_acc[:, x, :], in0=stat[:, :], scalar=-1.0 / CC, in1=c_acc[:, x, :],
                                        op0=ALU.mult, op1=ALU.add).then_inc(q.ln_cent, 1)
            for x in range(2):
                ve.wait_ge(q.ln_logged, 2)
                ve.scalar_tensor_tensor(out=gl_o[:, x, :], in0=c_acc[:, x, :], scalar=v1("ln_g", x), in1=gl_e[:, 2, :],
                                        op0=ALU.mult, op1=ALU.mult).then_inc(q.ln_norm, 1)
            end_stage(ve, 12)
            out_lows(DC + BH, low, g_hi, g_lo, range(DC))
            residual("c_out")
            end_stage(ve, 13)

            gains("ffn2")
            ve.wait_ge(q.r_ready, NORM["ffn2"] + 1)
            t0 = TILE["ffn2_in"]

            def gated(i, u):
                ve.wait_ge(q.tile_done, t0 + 2 * u + 1 + 4 * i)
                ve.tensor_tensor(f_c[:, 2 * u, :], lin[:, (t0 + 2 * u) % 2, :], r[:, :], ALU.mult)\
                    .then_inc(q.tile_taken, 1)
                ve.wait_ge(q.tile_done, t0 + 2 * u + 2 + 4 * i)
                ve.tensor_tensor(f_c[:, 2 * u + 1, :], lin[:, (t0 + 2 * u + 1) % 2, :], r[:, :], ALU.mult)\
                    .then_inc(q.tile_taken, 1)
                ve.wait_ge(q.tile_taken, t0 + 2 * u + 2 + 4 * i)
                ve.wait_ge(q.s_gate, u + 1 + 2 * i)
                hidden(2, i, u, 2 * u + 1)
            with ve.Fori(0, FC // 2) as i:
                gated(i, 0)
                gated(i, 1)
            residual("ffn2_out")
            end_stage(ve, 14)
            ple(2)
            end_stage(ve, 15)
            ve.wait_ge(q.r_ready, NORM["final"] + 1)
            for c in range(DC):
                ve.scalar_tensor_tensor(out=g[:, c, :], in0=h[:, c, :], scalar=v1("final", c), in1=r[:, :],
                                        op0=ALU.mult, op1=ALU.mult).then_inc(q.residual_added, 1)

        @block.scalar
        def _(ac):
            def rounded(vname, c, hi):
                ac.activation(hi[:, c, :], h[:, c, :], ACT.Copy, scale=v1(vname, c)).then_inc(q.h_rounded, 1)

            def out_highs(src, hi, chunks):
                for k in chunks:
                    ac.activation(hi[:, k, :], src[:, k, :], ACT.Copy).then_inc(q.out_rounded, 1)

            def factor(name):
                n = NORM[name]
                for c in range(DC):
                    if name != "final":
                        rounded(name, c, g_hi)
                    ac.activation(sq[:, c, :], h[:, c, :], ACT.Square).then_inc(q.h_squared, 1)
                ac.wait_ge(q.h_summed, n + 1)
                ac.activation(lnr[:, :], stat[:, :], ACT.Ln, bias=eps[:, 0:1], scale=1.0 / D).then_inc(q.r_logged, 1)
                ac.wait_ge(q.r_logged, n + 1)
                ac.activation(r[:, :], lnr[:, :], ACT.Exp, scale=-0.5).then_inc(q.r_ready, 1)

            def inv_sqrt(dst, n, summed, logged, factor_, summed_v, logged_v):
                ac.wait_ge(summed, summed_v)
                ac.activation(dst, stat[:, :], ACT.Ln, bias=eps[:, 0:1], scale=1.0 / n).then_inc(logged, 1)
                ac.wait_ge(logged, logged_v)
                ac.activation(dst, dst, ACT.Exp, scale=-0.5).then_inc(factor_, 1)

            def conv_ffn(n):
                factor(f"ffn{n}")
                t0, f0 = TILE[f"ffn{n}_in"], 2 * FC * n

                def pair(i, u):
                    for j in range(2):
                        k = 2 * u + j
                        w = VEC[f"conv{n}"] + 4 * k + 16 * i
                        ac.wait_ge(q.tile_taken, t0 + k + 1 + 4 * i)
                        wait(ac, q.f_through, FC * n + 2 * i + u - 1)
                        ac.activation(f_c[:, k, :], f_u[:, k, 2:S + 2], ACT.Identity, bias=vec[:, bass.ds(w + 3, 1)],
                                      scale=vec[:, bass.ds(w + 2, 1)]).then_inc(q.f_first, 1)
                    ac.wait_ge(q.f_conv, 2 * f0 + 4 * u + 4 + 8 * i)
                    ac.activation(f_sg[:, u, :], f_c[:, 2 * u + 1, :], ACT.Silu).then_inc(q.f_silu, 1)
                pair(0, 0)
                pair(0, 1)
                with ac.Fori(1, FC // 2) as i:
                    pair(i, 0)
                    pair(i, 1)

            def ple(n):
                factor(f"ple{n}")
                t0, g0 = TILE[f"ple{n}"], DC * n
                with ac.Fori(0, 2) as i:
                    for j in range(4):
                        ac.wait_ge(q.tile_taken, t0 + 2 * j + 1 + 8 * i)
                        ac.activation(p_sg[:, j % 2, :], p_gp[:, j % 2, :], ACT.Sigmoid).then_inc(q.ple_sigmoid, 1)

            def load_p(n):
                ac.dma_start(p_in_t[:, :, :].rearrange("p c s -> p (c s)"), a["p_t"][n]).then_inc(q.p_in, 16)

            ac.dma_start(pos_i, a["positions"].broadcast_to([P, S])).then_inc(q.positions_in, 16)
            for i in range(NQ):
                ac.dma_start(posq_i[:, i:i + 1], a["positions"][0, i * P:(i + 1) * P].rearrange("(p a) -> p a", a=1))\
                    .then_inc(q.positions_in, 16)
            ac.dma_start(a_lam[:, 0:4, :].rearrange("p k d -> p (k d)"), a["lam"].broadcast_to([P, 4 * AQK])).then_inc(q.lam_in, 16)
            ac.dma_start(a_tab, a["table"].broadcast_to([P, BUCKETS * AH])).then_inc(q.table_in, 16)
            ac.dma_start(walpha[32:48, :], a["w_alpha"]).then_inc(q.extra_in, 16)
            ac.dma_start(w2c[:, :, :].rearrange("p c d -> p (c d)"), a["cmp_w2"]).then_inc(q.extra_in, 16)
            load_p(0)
            ac.wait_ge(q.setup_step, 1)
            ac.wait_ge(q.x_in, 16 * DC)
            factor("attn0")
            ac.wait_ge(q.lam_dots, 1)
            ac.activation(lame, lamd, ACT.Exp).then_inc(q.lam_exps, 1)
            ac.wait_ge(q.angles_ready, 1)
            ac.activation(sinb[:, :], sinb[:, :], ACT.Sin)
            ac.activation(cosb[:, :], cosb[:, :], ACT.Sin)

            def a_step(s, par, proj, attn, tail):
                hd = s - 1

                def squared(j):
                    if proj:
                        ac.wait_ge(q.tile_taken, TILE["a_qkv"] + 3 * s + j + 1)
                        ac.activation(a_sq[:, j, :], a_raw[:, j, :], ACT.Square).then_inc(q.a_squared, 1)

                def exps(i):
                    if attn:
                        n = 4 * hd + i
                        ac.wait_ge(q.a_min, n + 1)
                        for x in range(2):
                            e = a_sc[:, i, x, 0:LEN[i]]
                            ac.activation(e, e, ACT.Exp, bias=nmax[:, 2 * i + x:2 * i + x + 1], scale=-1.0,
                                          accum_out=den[:, 2 * i + x:2 * i + x + 1]).then_inc(q.a_exped, 1)

                def factor_(j):
                    if proj:
                        inv_sqrt(a_ri[:, j, :], AQK, q.a_summed, q.a_logged, q.a_factor, 2 * s + j + 1, 2 * s + j + 1)

                if tail:
                    ac.wait_ge(q.a_otaken, s - 1)
                    ac.activation(a_sq[:, 2, :], a_rawo, ACT.Square).then_inc(q.a_osquared, 1)
                squared(0)
                if tail:
                    inv_sqrt(a_ri[:, 2, :], 2 * AQK, q.a_osummed, q.a_ologged, q.a_ofactor, s - 1, s - 1)
                exps(0)
                squared(1)
                exps(1)
                factor_(0)
                exps(2)
                factor_(1)
                exps(3)
                if proj:
                    ac.wait_ge(q.a_vturned, s + 1)
                    ac.activation(a_v[:, par, :, :].rearrange("p j c -> p (j c)"), obank[:, :], ACT.Copy)\
                        .then_inc(q.a_vcopied, 1)
                if attn:
                    for i in range(NQ):
                        ac.wait_ge(q.a_turned, 4 * hd + i + 1)
                        ac.activation(a_pt[:, 0:i + 1, i * P:(i + 1) * P],
                                      turn[:, i % 2, 0:LEN[i]].rearrange("p (j c) -> p j c", c=P), ACT.Copy)\
                            .then_inc(q.a_tcopied, 1)

            a_steps(ac, a_step)
            ac.wait_ge(q.a_onormed, AH)
            out_highs(a_o, g_hi, range(DC))
            end_stage(ac, 2)
            conv_ffn(0)
            end_stage(ac, 3)
            ple(0)
            end_stage(ac, 4)

            load_p(1)
            for c in range(DC):
                rounded("kv", c, b_g2_hi)
            factor("attn1")
            for j in range(7):
                ac.wait_ge(q.tile_taken, TILE["b_dkv"] + j + 1)
                ac.activation(b_dsq[:, j, :], b_cr[:, j, :], ACT.Square).then_inc(q.bd_squared, 1)
            for n, width in enumerate((KVL, ROPE, QL)):
                inv_sqrt(b_ri[:, n, :], width, q.bd_summed, q.bd_logged, q.bd_factor, n + 1, n + 1)
            end_stage(ac, 5)

            def b_step(s, par, proj, attn):
                def squared(j):
                    if proj:
                        ac.wait_ge(q.tile_taken, TILE["b_pair"] + 7 * s + j + 1)
                        ac.activation(b_sq[:, j, :], b_raw[:, j, :], ACT.Square).then_inc(q.b_squared, 1)

                def exps(x, i):
                    if attn:
                        n = 8 * (s - 1) + 4 * x + i
                        ac.wait_ge(q.b_min, n + 1)
                        e = b_sc[:, x, i, 0:LEN[i]]
                        ac.activation(e, e, ACT.Exp, bias=nmax[:, 4 * x + i:4 * x + i + 1], scale=-1.0,
                                      accum_out=den[:, 4 * x + i:4 * x + i + 1]).then_inc(q.b_exped, 1)

                def factor_(j):
                    if proj:
                        inv_sqrt(b_ri[:, j, :], ROPE if j == 2 else NOPE, q.b_summed, q.b_logged, q.b_factor,
                                 5 * s + j + 1, 5 * s + j + 1)

                squared(0); exps(0, 0); squared(1); exps(0, 1); squared(2); factor_(0); exps(0, 2); squared(3)
                factor_(1); exps(0, 3); squared(4); factor_(2); exps(1, 0); factor_(3); exps(1, 1); factor_(4)
                exps(1, 2); exps(1, 3)
                if proj:
                    for x in range(2):
                        ac.wait_ge(q.b_vturned, 2 * s + x + 1)
                        ac.activation(b_v[:, par, x, :], obank[:, :], ACT.Copy).then_inc(q.b_vcopied, 1)
                if attn:
                    for x in range(2):
                        for i in range(NQ):
                            ac.wait_ge(q.b_turned, 8 * (s - 1) + 4 * x + i + 1)
                            if x == 1 and i == 0:
                                ac.wait_ge(q.b_pv, 2 * s - 1)
                            ac.activation(b_pt[:, 0:i + 1, i * P:(i + 1) * P],
                                          turn[:, i % 2, 0:LEN[i]].rearrange("p (j c) -> p j c", c=P), ACT.Copy)\
                                .then_inc(q.b_tcopied, 1)

            b_steps(ac, b_step)
            ac.wait_ge(q.b_otaken, BH)
            out_highs(b_o, b_o_hi, range(BH))
            end_stage(ac, 6)
            conv_ffn(1)
            end_stage(ac, 7)
            ac.dma_start(onehot, a["onehot"]).then_inc(q.extra_in, 16)
            ac.dma_start(relt, a["relt"]).then_inc(q.extra_in, 16)
            ple(1)
            end_stage(ac, 8)

            load_p(2)
            factor("mix2")
            for x in range(2):
                ac.wait_ge(q.tile_taken, TILE["c_in"] + 15 + x)
                ac.activation(c_acc[:, x, :], c_z[:, 14 + x, :], ACT.Sigmoid).then_inc(q.c_sigmoid, 1)
            for x in range(2):
                ac.wait_ge(q.tile_taken, TILE["c_in"] + 21 + x)
                ac.activation(c_z[:, 20 + x, :], c_z[:, 20 + x, :], ACT.Silu).then_inc(q.gl_silu, 1)
            end_stage(ac, 9)

            ac.wait_ge(q.gates_turned, 1)
            ac.activation(c_ga[:, :, :], stat[:, :].rearrange("p (i c) -> p i c", c=P)[:, :, 0:24], ACT.Sigmoid)\
                .then_inc(q.gates_made, 1)
            for x in range(2):
                ac.wait_ge(q.c_vturned, x + 1)
                ac.activation(c_v[:, x, :, :].rearrange("p j c -> p (j c)"), turn[:, x, :], ACT.Copy)\
                    .then_inc(q.c_vcopied, 1)
            for k in range(4):
                ac.wait_ge(q.tile_taken, TILE["c_cmp"] + 2 * k + 2)
                ac.activation(c_hid[:, k, :], c_hid[:, k, :], ACT.Silu, bias=v1("cmp_b1", k)).then_inc(q.hid_act, 1)
            ac.wait_ge(q.cc_reduced, 2)
            cs3 = c_cs[:, :, :, :].rearrange("p h i n -> p (h i) n")
            ac.activation(cs3, cs3, ACT.Exp, scale=-1.0).then_inc(q.cc_exped, 1)
            for hd in range(CH):
                ac.wait_ge(q.cc_turned, hd + 1)
                ac.activation(c_ct[0:NCMP, hd, :], turn[0:NCMP, hd % 2, :], ACT.Copy).then_inc(q.cc_copied, 1)
            end_stage(ac, 10)

            for s in range(CH + 1):
                for i in range(NQ):
                    if s < CH:
                        n = 4 * s + i
                        ac.wait_ge(q.c_min, n + 1)
                        for x in range(2):
                            e = c_sc[:, i, x, 0:LEN[i]]
                            ac.activation(e, e, ACT.Exp, bias=nmax[:, 2 * i + x:2 * i + x + 1], scale=-1.0,
                                          accum_out=den[:, 2 * i + x:2 * i + x + 1]).then_inc(q.c_exped, 1)
                    if s > 0:
                        for x in range(2):
                            ac.wait_ge(q.c_turned, 8 * (s - 1) + 2 * i + x + 1)
                            if i == 0 and x == 0:
                                wait(ac, q.c_pv, s - 1)
                            ac.activation(c_pt[:, x, 0:i + 1, i * P:(i + 1) * P],
                                          turn[:, x, 0:LEN[i]].rearrange("p (j c) -> p j c", c=P), ACT.Copy)\
                                .then_inc(q.c_tcopied, 1)
            end_stage(ac, 11)

            ac.wait_ge(q.gl_alpha, 1)
            ac.activation(gl_e[:, 1, :], stat[:, :], ACT.Identity, bias=v1("b_alpha")).then_inc(q.gl_abs, 1)
            ac.wait_ge(q.gl_abs, 1)
            ac.activation(gl_e[:, 0, :], gl_e[:, 1, :], ACT.Abs).then_inc(q.gl_abs, 1)
            ac.wait_ge(q.gl_abs, 2)
            ac.activation(gl_e[:, 0, :], gl_e[:, 0, :], ACT.Exp, scale=-1.0).then_inc(q.gl_exp, 1)
            ac.wait_ge(q.gl_exp, 1)
            ac.activation(gl_e[:, 0, :], gl_e[:, 0, :], ACT.Ln, bias=ones[:, 0:1]).then_inc(q.gl_ln, 1)
            ac.wait_ge(q.gl_scan, 1)
            ac.activation(gl_t[:, 0, :], gl_b, ACT.Exp).then_inc(q.gl_exps, 1)
            ac.activation(gl_t[:, 1, :], gl_b, ACT.Exp, scale=-1.0).then_inc(q.gl_exps, 1)
            ac.activation(gl_dn, gl_b.rearrange("p (n c) -> p n c", c=GCH)[:, :, GCH - 1], ACT.Exp).then_inc(q.gl_exps, 1)
            ac.wait_ge(q.gl_scan, 2)
            ac.activation(gl_e[:, 1, :], gl_e[:, 0, :], ACT.Exp).then_inc(q.gl_exps, 1)
            for x in range(2):
                ac.wait_ge(q.gl_add, 2 * x + 2)
                ac.activation(gl_s[:, x, :], gl_o[:, x, :], ACT.Square).then_inc(q.gl_sq, 1)
            for x in range(2):
                inv_sqrt(gl_e[:, x, :], GV, q.gl_ss, q.gl_log, q.gl_fac, x + 1, x + 1)
            for x in range(2):
                ac.wait_ge(q.ln_cent, x + 1)
                ac.activation(gl_s[:, x, :], c_acc[:, x, :], ACT.Square).then_inc(q.ln_sq, 1)
            ac.wait_ge(q.ln_summed, 2)
            ac.activation(gl_e[:, 2, :], obank[:, :], ACT.Ln, bias=eps[:, 0:1], scale=1.0 / CC).then_inc(q.ln_logged, 1)
            ac.wait_ge(q.ln_logged, 1)
            ac.activation(gl_e[:, 2, :], gl_e[:, 2, :], ACT.Exp, scale=-0.5).then_inc(q.ln_logged, 1)
            for x in range(2):
                ac.wait_ge(q.ln_norm, x + 1)
                ac.activation(low[:, 4 + x, :], gl_o[:, x, :], ACT.Silu, bias=v1("ln_b", x))
            end_stage(ac, 12)
            out_highs(low, g_hi, range(DC))
            end_stage(ac, 13)

            factor("ffn2")
            t0 = TILE["ffn2_in"]

            def gate(i, u):
                ac.wait_ge(q.tile_taken, t0 + 2 * u + 1 + 4 * i)
                wait(ac, q.f_through, 2 * FC + 2 * i + u - 1)
                ac.activation(f_sg[:, u, :], f_c[:, 2 * u, :], ACT.Silu).then_inc(q.s_gate, 1)
            with ac.Fori(0, FC // 2) as i:
                gate(i, 0)
                gate(i, 1)
            end_stage(ac, 14)
            ple(2)
            end_stage(ac, 15)
            factor("final")
            for c in range(DC):
                ac.wait_ge(q.residual_added, 3 * DC + c + 1)
                ac.dma_start(out[c * P:(c + 1) * P, :], g[:, c, :]).then_inc(q.out_stored, 16)

        @block.gpsimd
        def _(po):
            def causal_within_chunks():
                po.wait_ge(q.weights_split, GROUP["c_out"] + 2)
                po.wait_ge(q.gl_attc, GH)
                for odd in range(2):
                    half = gl_am[64 * odd:64 * odd + 64, :, :, :].rearrange("p h n c -> p (h n) c")
                    po.affine_select(out=half, in_=half, compare_op=ALU.is_ge, fill=0.0, base=0,
                                     pattern=[[0, GH * NCH // 2], [1, GCH]], channel_multiplier=-1).then_inc(q.gl_mask, 1)

            po.wait_ge(q.consts_in, 32)
            for name, count, blocks, per in STREAM:
                def split(k, n, i, end):
                    at_ = slice(0, blocks[k % 2] * P)
                    po.wait_ge(landed[n % 2], 16 * (n // 2 + 1) + 16 * i)
                    wait(po, q.tile_done, end)
                    b3 = [t_[:, n % 2, at_].rearrange("p (b c) -> p b c", c=P) for t_ in (w_hi, slots)]
                    po.tensor_tensor(b3[0], b3[1], ones.unsqueeze(1).broadcast_to([P, blocks[k % 2], P]), ALU.mult).then_inc(q.hi_made, 1)
                    po.wait_ge(q.hi_made, n + 1 + 2 * i)
                    po.tensor_tensor(w_lo[:, n % 2, at_], slots[:, n % 2, at_], w_hi[:, n % 2, at_].bitcast(F32),
                                     ALU.subtract).then_inc(q.weights_split, 1)
                stream(po, name, count, split, causal_within_chunks if name == "c_out" else None)


def _blocks(w):
    k, m = w.shape
    return w.reshape(k // P, P, m // P, P).transpose(2, 1, 0, 3).reshape(m // P, P, k)


def _side_by_side(tiles):
    return tiles.transpose(1, 0, 2).reshape(P, -1)


def _halves(tiles):
    n, _, k = tiles.shape
    return tiles.reshape(n, P, 2, k // 2).transpose(0, 2, 1, 3).reshape(2 * n, P, k // 2)


def _columns(v):
    return np.ascontiguousarray(v.reshape(-1, P).T)


def _consts():
    i = np.arange(P)
    rot = np.zeros((P, P), np.float32)
    low = i % ROPE < ROPE // 2
    rot[i[low] + ROPE // 2, i[low]] = -1.0
    rot[i[~low] - ROPE // 2, i[~low]] = 1.0
    mask = np.where(np.arange(S)[None, :] - (S - P) <= i[:, None], 0.0, NEG)
    return np.concatenate([np.ones((P, P)), i[:, None] // 64 == i[None, :] // 64, np.eye(P), rot, mask], axis=1)\
        .astype(np.float32)


def _onehot():
    starts = np.array([0] + bucket_starts())
    dist = S - 1 - np.arange(S)
    bucket = np.searchsorted(starts, dist, side="right") - 1
    return (np.arange(BUCKETS)[:, None] == bucket[None, :]).astype(np.float32)


def _lay_out(x):
    f = {k: np.asarray(v) for k, v in x.items()}
    a = {}
    a["x_t"] = f["x"][0].T.reshape(DC, P, S).transpose(1, 0, 2)
    p = np.concatenate([f["p"][:, 0], f["p_2"][:, 0]], axis=0)
    a["p_t"] = p.transpose(0, 2, 1).reshape(3, 2, P, S).transpose(0, 2, 1, 3).reshape(3, P, -1)
    a["positions"] = f["positions"].astype(np.int32) if f["positions"].dtype != np.int32 else f["positions"]
    a["table"] = f["rel_bias_table"].reshape(1, -1)
    a["lam"] = np.concatenate([f["a_lam_q1"], f["a_lam_k1"], f["a_lam_q2"], f["a_lam_k2"]], axis=1)
    a["consts"] = _consts()
    a["onehot"] = _onehot()
    a["relt"] = f["rel_bias_2"]
    a["w_alpha"] = f["gla_w_alpha_2"][0]
    a["cmp_w2"] = np.concatenate([f["cmp_w2_k_2"][0].reshape(2, P, CD), f["cmp_w2_v_2"][0].reshape(2, P, CD)])\
        .transpose(1, 0, 2).reshape(P, -1)

    qkv = _blocks(f["a_w_qkv"][0]).reshape(3, AH, P, D).transpose(1, 0, 2, 3).reshape(3 * AH, P, D)
    a["w_a_qkv"] = qkv
    a["w_a_wo"] = _blocks(f["a_w_o"][0])

    def ffn_in(first, second):
        return np.stack([_blocks(first), _blocks(second)], axis=1).reshape(2 * FC, P, D)

    def ple(gate, proj):
        return np.concatenate([_blocks(gate), _blocks(proj)], axis=2)

    for n in range(2):
        w = f["ffn_w_in"][n]
        a[f"w_ffn{n}_in"] = ffn_in(w[:, :FF], w[:, FF:])
        a[f"w_ffn{n}_out"] = _halves(_blocks(f["ffn_w_out"][n]))
        a[f"w_ple{n}"] = ple(f["ple_w_gate"][n], f["ple_w_proj"][n])
    a["w_ffn2_in"] = ffn_in(f["ffn_w_gate_2"][0], f["ffn_w_up_2"][0])
    a["w_ffn2_out"] = _halves(_blocks(f["ffn_w_down_2"][0]))
    a["w_ple2"] = ple(f["ple_w_gate_2"][0], f["ple_w_proj_2"][0])

    dkv = f["w_dkv"]
    a["w_b_dkv"] = _blocks(np.concatenate([dkv, dkv[:, KVL:]], axis=1))
    a["w_b_dq"] = _blocks(f["b_w_dq"][0])
    uq = f["b_w_uq"][0].reshape(QL, B_PAIRS, 2, NOPE + ROPE)
    ukv = f["w_ukv"].reshape(KVL, B_PAIRS, 2, NOPE + P)
    pair = []
    for n in range(B_PAIRS):
        up = np.concatenate([uq[:, n, 0, :NOPE], uq[:, n, 1, :NOPE], uq[:, n, 0, NOPE:], uq[:, n, 1, NOPE:]], axis=1)
        kv = np.concatenate([ukv[:, n, 0, :NOPE], ukv[:, n, 1, :NOPE], ukv[:, n, 0, NOPE:], ukv[:, n, 1, NOPE:]], axis=1)
        pair += [_side_by_side(_blocks(up)), np.pad(_side_by_side(_blocks(kv)), ((0, 0), (0, 4 * P)))]
    a["w_b_pair"] = np.stack(pair)
    a["w_b_wo"] = _halves(_blocks(f["b_w_o"][0]))

    w = f["w_in_2"][0]
    splits = [512, 128, 128, 128, 128, 128, 128, 24, 512, 128, 128, 256, 16, 256]
    nq, kc, vc, ks, vs, kw, vw, ng, cu, gq, gk, gv, ga, gr = np.split(w, np.cumsum(splits)[:-1], axis=1)
    heads = [nq[:, CD * i:CD * (i + 1)] for i in range(CH)]
    cols = [c for t in range(4) for c in (heads[t], heads[t + 4])] + [ks, kw, vs, vw]
    for m in (kc, vc):
        for x in range(CKV):
            cols += [m[:, CD * x:CD * (x + 1)]] * 2
    cols += [cu, gq, gk, gv, gr, ng, np.zeros((D, 8), w.dtype), ga, np.zeros((D, 80), w.dtype)]
    a["w_c_in"] = _blocks(np.concatenate(cols, axis=1))
    a["w_c_cmp"] = _halves(np.concatenate([_blocks(f["cmp_w1_k_2"][0]), _blocks(f["cmp_w1_v_2"][0])]))
    a["w_c_out"] = _blocks(f["w_out_2"][0])

    def twice(v):
        return np.concatenate([v, v]).reshape(P, 1)

    def conv(n):
        t = np.concatenate([f["ffn_conv_w"][n], f["ffn_conv_b"][n][None]])
        t = t.reshape(4, 2, FC, P).transpose(3, 2, 1, 0)
        return t.reshape(P, -1)

    inv = np.exp(np.float32(-math.log(ROPE_BASE)) * np.arange(ROPE // 2, dtype=np.float32) * np.float32(2.0 / ROPE))
    dw = f["conv_w_2"][0]
    vecs = {
        "attn0": _columns(f["attn_norm"][0]), "attn1": _columns(f["attn_norm"][1]), "kv": _columns(f["kv_norm"]),
        "ffn0": _columns(f["ffn_norm"][0]), "ffn1": _columns(f["ffn_norm"][1]),
        "ple0": _columns(f["ple_norm"][0]), "ple1": _columns(f["ple_norm"][1]),
        "mix2": _columns(f["mix_norm_g_2"][0]), "ffn2": _columns(f["ffn_norm_g_2"][0]),
        "ple2": _columns(f["ple_norm_g_2"][0]), "final": _columns(f["final_norm_g_2"]),
        "a_q": twice(f["a_q_norm"][0]), "a_k": twice(f["a_k_norm"][0]), "a_sub": _columns(f["a_sub_norm"][0]),
        "ckv": _columns(f["ckv_norm"]), "cq": _columns(f["b_cq_norm"][0]), "k_nope": _columns(f["k_nope_norm"]),
        "k_pe": twice(f["k_pe_norm"]), "q_nope": _columns(f["b_q_nope_norm"][0]), "q_pe": twice(f["b_q_pe_norm"][0]),
        "inv_freq": np.tile(inv, 4).reshape(P, 1), "conv0": conv(0), "conv1": conv(1),
        "cmp_b1": np.concatenate([_columns(f["cmp_b1_k_2"][0]), _columns(f["cmp_b1_v_2"][0])], axis=1),
        "cmp_pos": np.concatenate([f[n][0].reshape(16, P).T for n in ("cmp_pos_k_2", "cmp_pos_v_2")], axis=1),
        "dw": dw.reshape(CW, 2, P).transpose(2, 1, 0).reshape(P, -1), "dw_b": _columns(f["conv_b_2"][0]),
        "ln_g": _columns(f["conv_ln_g_2"][0]), "ln_b": _columns(f["conv_ln_b_2"][0]),
        "b_alpha": _columns(f["gla_b_alpha_2"][0]), "gla_g": _columns(f["gla_norm_g_2"][0]),
        "t5_start": np.tile(np.array(bucket_starts(), np.float32), (P, 1)),
        "first_block": (np.arange(P) >= CMPB - 1).astype(np.float32).reshape(P, 1),
    }
    for name, n in VEC_COLS:
        assert vecs[name].shape == (P, n), (name, vecs[name].shape)
    a["vec"] = np.concatenate([vecs[name] for name, _ in VEC_COLS], axis=1)
    return {k: np.ascontiguousarray(v) for k, v in a.items()}


def kernel(**inputs):
    import concourse.bacc as bacc
    from concourse.bass_utils import run_bass_kernel_spmd as run

    arrays = {f"in_{k}": v for k, v in _lay_out(inputs).items()}
    nc = bacc.Bacc("TRN2", target_bir_lowering=False, num_devices=1,
                   dynamic_dma_scratch_size=DMA_SCRATCH)
    aps = {k[3:]: nc.dram_tensor(k, v.shape, mybir.dt.from_np(v.dtype), kind="ExternalInput").ap()
           for k, v in arrays.items()}
    out = nc.dram_tensor("out", [D, S], F32, kind="ExternalOutput").ap()
    build_program(nc, aps, out)
    result = run(nc, [arrays], core_ids=[0])
    return result.results[0]["out"].T.reshape(1, S, D)
```

```python
import math
from collections import namedtuple
from contextlib import ExitStack

import concourse.bass as bass
import numpy as np
from concourse import mybir

P = 128
S = 512
D = 1024
DC = D // P
NQ = S // P
FF = 2816
FC = FF // P
EPS = 1e-6
NEG = -1e30
BUCKETS, MAX_EXACT, MAX_DIST = 32, 16, 128
AH, AQK = 8, 64
LAM_INIT = 0.8 - 0.6 * math.exp(0.0)
BH, NOPE, ROPE = 16, 128, 64
QL, KVL = 512, 256
ROPE_BASE = 10000.0
CH, CKV, CD = 8, 2, 64
CMPB, CMPS, HID = 32, 16, 256
NCMP = S // CMPS - CMPB // CMPS + 1
CC, CW = 256, 31
GH, GK, GV, GCH, TAU = 4, 32, 64, 64, 16.0
NCH = S // GCH
SLOT = 12 * P
LEN = [(i + 1) * P for i in range(NQ)]
OFF = [sum(LEN[:i]) for i in range(NQ)]
CAUSAL = sum(LEN)
B_PAIRS = BH // 2

F32 = mybir.dt.float32
F32R = mybir.dt.float32r
I32 = mybir.dt.int32
ALU = mybir.AluOpType
ACT = mybir.ActivationFunctionType
AX = mybir.AxisListType

STREAM = [
    ("a_qkv", 3 * AH, (DC, DC), (1, 1)), ("a_wo", DC, (DC, DC), (1, 1)),
    ("ffn0_in", 2 * FC, (DC, DC), (1, 1)), ("ffn0_out", 2 * DC, (FC // 2, FC // 2), (1, 1)),
    ("ple0", DC, (DC + 2, DC + 2), (2, 2)),
    ("b_dkv", 3, (DC, DC), (1, 1)), ("b_dq", 4, (DC, DC), (1, 1)), ("b_pair", 2 * B_PAIRS, (12, 8), (3, 4)),
    ("b_wo", 2 * DC, (BH // 2, BH // 2), (1, 1)),
    ("ffn1_in", 2 * FC, (DC, DC), (1, 1)), ("ffn1_out", 2 * DC, (FC // 2, FC // 2), (1, 1)),
    ("ple1", DC, (DC + 2, DC + 2), (2, 2)),
    ("c_in", 23, (DC, DC), (1, 1)), ("c_cmp", 8, (8, 8), (1, 1)), ("c_out", DC, (DC, DC), (1, 1)),
    ("ffn2_in", 2 * FC, (DC, DC), (1, 1)), ("ffn2_out", 2 * DC, (FC // 2, FC // 2), (1, 1)),
    ("ple2", DC, (DC + 2, DC + 2), (2, 2)),
]
GROUP, TILE, PER = {}, {}, {}
GROUP_END = []
_g = _t = 0
for _n, _c, _b, _per in STREAM:
    GROUP[_n], TILE[_n], PER[_n] = _g, _t, _per
    _g += _c
    for _k in range(_c):
        _t += _per[_k % 2]
        GROUP_END.append(_t)
NORM = {n: i for i, n in enumerate(
    ["attn0", "ffn0", "ple0", "attn1", "ffn1", "ple1", "mix2", "ffn2", "ple2", "final"])}
RESIDUALS = ["a_wo", "ffn0_out", "b_wo", "ffn1_out", "c_out", "ffn2_out"]

SIGNALS = """
consts_in x_in positions_in lam_in table_in p_in extra_in stage_end h_squared squares_added h_rounded h_gained h_gained2 h_summed
r_logged r_ready hi_made weights_split out_rounded out_split p_split tile_done tile_taken residual_added out_stored setup_step lam_dots lam_exps bias_built
angles_ready f_first f_conv f_silu f_split f_through s_gate ple_sigmoid a_squared a_summed a_logged
a_factor a_normed a_vturned a_vcopied a_scored a_biased a_min a_exped a_recip a_scaled a_weights a_turned
a_tcopied a_pv a_otaken a_osquared a_osummed a_ologged a_ofactor a_onormed bd_squared bd_summed bd_logged
bd_factor bd_normed bd_rounded bd_rotated bd_terms b_squared b_summed b_logged b_factor b_normed b_rotated b_terms
b_rope b_vturned b_vcopied b_scored b_biased b_min b_exped b_recip b_weights b_turned b_tcopied b_pv
b_otaken g_made g_rowed g_written g_read  c_sigmoid c_glu conv_step zp_made hid_act kc_made
kc_copied c_vturned c_vcopied gates_turned gates_made cb_made cc_scored cc_biased cc_reduced cc_exped
 cc_recip cc_scaled cc_turned cc_copied c_scored c_biased c_min c_exped c_recip c_gated c_weights
c_turned c_tcopied c_pv c_otaken gl_alpha gl_abs gl_exp gl_ln gl_la gl_scale gl_scan gl_exps
gl_prod gl_att gl_attc gl_mask gl_kdt gl_kdc gl_u gl_uc gl_state gl_bd gl_out gl_sum gl_add gl_sq gl_ss
gl_log gl_fac gl_norm gl_silu ln_summed ln_cent ln_sq ln_logged ln_norm
""".split()
Signals = namedtuple("Signals", SIGNALS)

VEC_COLS = [("attn0", DC), ("attn1", DC), ("kv", DC), ("ffn0", DC), ("ffn1", DC), ("ple0", DC), ("ple1", DC),
            ("mix2", DC), ("ffn2", DC), ("ple2", DC), ("final", DC), ("a_q", 1), ("a_k", 1), ("a_sub", 1),
            ("ckv", 2), ("cq", 4), ("k_nope", 1), ("k_pe", 1), ("q_nope", 1), ("q_pe", 1), ("inv_freq", 1),
            ("conv0", 8 * FC), ("conv1", 8 * FC), ("cmp_b1", 4), ("cmp_pos", 32), ("dw", 2 * CW), ("dw_b", 2),
            ("ln_g", 2), ("ln_b", 2), ("b_alpha", 1), ("gla_g", 2), ("first_block", 1),
            ("t5_start", BUCKETS - 1)]
VEC = {}
NVEC = 0
for _n, _c in VEC_COLS:
    VEC[_n] = NVEC
    NVEC += _c
ARENA = 29824
DMA_SCRATCH, SBUF_BYTES = 1024, 229344
G_READ = 16 * NQ
PI_IN = 3.1415925
BAND = CH * 2 * S


def bucket_starts():
    ratio = MAX_DIST / MAX_EXACT
    return [b if b <= MAX_EXACT else math.ceil(MAX_EXACT * ratio ** ((b - MAX_EXACT) / (BUCKETS - MAX_EXACT)))
            for b in range(1, BUCKETS)]


def wait(eng, sem, value):
    if not (isinstance(value, int) and value <= 0):
        eng.wait_ge(sem, value)


def a_steps(eng, step, before_last=None):
    step(0, 0, True, False, False)
    step(1, 1, True, True, False)
    with eng.Fori(0, (AH - 2) // 2) as i:
        for par in range(2):
            step(2 * i + 2 + par, par, True, True, True)
    step(AH, 0, False, True, True)
    if before_last:
        before_last()
    step(AH + 1, 1, False, False, True)


def b_steps(eng, step):
    step(0, 0, True, False)
    step(1, 1, True, True)
    with eng.Fori(0, (B_PAIRS - 2) // 2) as i:
        for par in range(2):
            step(2 * i + 2 + par, par, True, True)
    step(B_PAIRS, 0, False, True)


def build_program(nc, a, out):
    with ExitStack() as ctx:
        top = [DMA_SCRATCH]

        def sb(name, *shape, dt=F32, rounded=None):
            kw = {"offset": top[0]}
            main = nc.alloc_sbuf_tensor_at(name, list(shape), dt, **kw)
            both = (main, nc.alloc_sbuf_tensor_at(rounded, list(shape), F32R, **kw)) if rounded else main
            top[0] += -(-4 * int(np.prod(shape[1:])) // 32) * 32
            assert top[0] <= SBUF_BYTES, top[0]
            return both

        def sem(name):
            return ctx.enter_context(nc.semaphore(name))

        lin = ctx.enter_context(nc.psum_tensor("lin", [P, 2, 512], F32))
        scores = ctx.enter_context(nc.psum_tensor("scores", [P, 2, 512], F32))
        stat = ctx.enter_context(nc.psum_tensor("stat", [P, 512], F32))
        turn = ctx.enter_context(nc.psum_tensor("turn", [P, 2, 512], F32))
        obank = ctx.enter_context(nc.psum_tensor("obank", [P, 512], F32))

        h = sb("h", P, DC, S)
        g, g_hi = sb("g", P, DC, S, rounded="g_hi")
        low, g_lo = sb("low", P, DC, S, rounded="g_lo")
        slots = sb("slots", P, 2, SLOT)
        w_hi = nc.alloc_sbuf_tensor_at("w_hi", [P, 2, SLOT], F32R, offset=top[0]); top[0] += 8 * SLOT
        w_lo = nc.alloc_sbuf_tensor_at("w_lo", [P, 2, SLOT], F32R, offset=top[0]); top[0] += 8 * SLOT
        r = sb("r", P, S)
        lnr = sb("lnr", P, S)
        vec = sb("vec", P, NVEC)
        consts = sb("consts", P, 8 * P)
        ones, ones64, ident, rot = (consts[:, k * P:(k + 1) * P] for k in range(4))
        maskt = consts[:, 4 * P:8 * P]
        eps = sb("eps", P, 1)
        small = sb("small", P, 64)
        p_in_t = sb("p_in_t", P, 2, S)
        arena_at = top[0]
        arena = sb("arena", P, ARENA)

        def area_r(name, at, *shape):
            assert at + int(np.prod(shape)) <= ARENA, (at, shape)
            return nc.alloc_sbuf_tensor_at(name, [P, *shape], F32R, offset=arena_at + 4 * at)

        def area(at, *shape):
            n = int(np.prod(shape))
            assert at + n <= ARENA, (at, shape)
            v = arena[:, at:at + n]
            names = "abcd"[:len(shape)]
            if len(shape) == 1:
                return v
            return v.rearrange(f"p ({' '.join(names)}) -> p {' '.join(names)}", **dict(zip(names[:-1], shape[:-1])))

        def v1(name, j=0, n=1):
            c = VEC[name] + j
            return vec[:, c:c + n]

        sq_last, sq_sum = area(ARENA - 2 * S - 128, S), area(ARENA - S - 128, S)
        at = DC * S
        a_bias = area(at, AH, CAUSAL); at += AH * CAUSAL
        a_raw = area(at, 3, S); at += 3 * S
        a_sq = a_ri = area(at, 3, S); at += 3 * S
        a_rawo = area(at, S); at += S
        a_qk = area(at, 2, 2, S); at += 4 * S
        a_v = area(at, 2, NQ, P); at += 2 * S
        a_sc = area(at, NQ, 2, S); a_dist = area(at, CAUSAL); a_mask = area(at + CAUSAL, CAUSAL); a_rows = area(at, S + P)[0:AH, :]; at += 8 * S
        a_pt = area(at, NQ, S)
        pos_i = area(at, S).bitcast(I32); at += S
        posf = area(at, S); at += S
        a_tab = area(at, BUCKETS * AH); at += BUCKETS * AH
        a_diff = area(at, BUCKETS * AH); at += BUCKETS * AH
        a_lam = area(at, 5, AQK); at += 5 * AQK
        a_step_ok = a_rawo[:, 0:S - 1]
        a_onehot, a_relt = a_v[0:BUCKETS, 0, :, :].rearrange("p j c -> p (j c)"), a_v[0:BUCKETS, 1, 0, 0:AH]
        a_o = area(0, DC, S)
        assert at + P <= ARENA - 2 * S - 128
        regular = sb("regular", P, 2)
        regular_i = sb("regular_i", P, 1, dt=I32)
        posq_i = sb("posq_i", P, NQ, dt=I32)
        cosb = sb("cosb", P, S)
        sinb = sb("sinb", P, S)
        posq = small[:, 0:4]
        nlam, asub, lamd, lame = small[:, 4:5], small[:, 5:6], small[:, 6:8], small[:, 8:10]
        nmax = small[:, 16:32]
        den = small[:, 32:48]
        f_hi = area_r("f_hi", 0, FC, S)
        f_lo = area_r("f_lo", FC * S, FC, S)
        f_u = area(2 * FC * S, 4, S + 2)
        f_c = area(2 * FC * S + 4 * (S + 2), 4, S)
        f_sg = area(2 * FC * S + 4 * (S + 2) + 4 * S, 2, S)
        p_gp = area(2 * DC * S, 2, S)
        p_sg = area(2 * DC * S + 2 * S, 2, S)
        p_t = area(2 * DC * S + 4 * S, 2, S)
        p_hi = area_r("p_hi", 2 * DC * S + 6 * S, 2, S)
        p_lo = area_r("p_lo", 2 * DC * S + 8 * S, 2, S)
        at = DC * S
        b_g2_hi = area_r("b_g2_hi", at, DC, S); b_o = area(0, BH, S); at += DC * S
        b_o_hi = area_r("b_o_hi", at, BH, S); b_o_lo = area_r("b_o_lo", at + BH * S, BH, S)
        b_sc = g[:, :, :].rearrange("p (x i) s -> p x i s", x=2)
        b_cr = area(at, 7, S); b_raw = b_cr; at += 7 * S
        b_sq = b_ri = area(at, 5, S); at += 5 * S
        b_ckv_hi = area_r("b_ckv_hi", at, 2, S); at += 2 * S
        b_cq_hi = area_r("b_cq_hi", at, 4, S); at += 4 * S
        b_kp = area(at, S); at += S
        b_dsq = area(at, 7, S)
        b_qn = area(at, 2, 2, S); at += 4 * S
        b_kn = area(at, 2, 2, S); at += 4 * S
        b_qp = area(at, 2, S); at += 2 * S
        b_rt = area(at, 3, S); at += 3 * S
        b_g2_lo = area_r("b_g2_lo", at, DC, S)
        b_ckv_lo = area_r("b_ckv_lo", at, 2, S); at += 2 * S
        b_cq_lo = area_r("b_cq_lo", at, 4, S); at += 4 * S
        b_v = low[:, 0:4, :].rearrange("p (a b) s -> p a b s", a=2)
        b_pt = low[:, 4:8, :]
        at = 0
        c_sc = area(at, NQ, 2, S); c_mix_hi = area_r("c_mix_hi", at, DC, S); c_gl = at; at += 8 * S
        c_z = area(at, 23, S); at += 23 * S
        c_ct = c_z[:, 8:16, :]
        c_hp = area(at, 2, S + CW - 1); at += 2 * (S + CW - 1)
        c_acc = area(at, 2, S); at += 2 * S
        c_bias = area(at, CH, S); at += CH * S
        c_rows = c_bias[0:CH, 0:2, :].rearrange("p h s -> p (h s)")[:, 0:S + P]
        c_cb = area(at, CH, NQ, NCMP); at += CH * NQ * NCMP
        c_pt = area(at, 2, NQ, S); c_zp = area(at, 2, 16, 2 * NCMP)
        c_pts = (c_pt, g[:, :, :].rearrange("p (x j) s -> p x j s", x=2))
        turns = (turn, lin)
        onehot = area(at + 6 * S, S)[0:BUCKETS, :]
        relt = area(at + 7 * S, CH)[0:BUCKETS, :]; at += 8 * S
        c_v = area(at, 2, NQ, P); at += 2 * S
        c_ga = area(at, NQ, 24); at += NQ * 24
        c_kc = area(at, 32); at += 32
        c_vc = area(at, 2, CD); at += 2 * CD
        c_hid = area(at, 4, 2 * NCMP); at += 4 * 2 * NCMP
        c_cs = area(at, CH, NQ, NCMP); at += CH * NQ * NCMP
        c_cden = area(at, CH * NQ); at += CH * NQ
        c_cmin = area(at, CH * NQ); at += CH * NQ
        c_small_end = at
        at = c_gl
        gl_x, gl_l, gl_b, gl_reset = (low[:, 4 + k, :] for k in range(4))
        gl_qt = area(at, S); at += S
        gl_kt = area(at, S); at += S
        gl_kd = area(at, S); at += S
        gl_t = area(at, 2, S); at += 2 * S
        gl_s = area(at, 2, S); at += 2 * S
        at = DC * S + 23 * S + 2 * (S + CW - 1) + 2 * S
        gl_am = area(at, GH, NCH // 2, GCH); at += GH * NCH // 2 * GCH
        gl_kdt = area(at, NQ, P); at += S
        gl_vt = area(at, NQ, 2 * P); at += 2 * S
        gl_us = area(at, NCH, GV); at += NCH * GV
        gl_st = area(at, NCH, GV); at += NCH * GV
        gl_bds = area(at, NCH, 2 * P); at += NCH * 2 * P
        gl_o = area(at, 2, S); at += 2 * S
        gl_e = area(at, 3, S); at += 3 * S
        gl_dn = small[:, 48:48 + NCH]
        w2c = sb("w2c", P, 4, CD)
        walpha = sb("walpha", P, P)

        landed = [sem("weights_landed_in_slot0"), sem("weights_landed_in_slot1")]

        q = Signals(*(sem(name) for name in SIGNALS))

        a_row_dram = nc.dram_tensor("a_bias_rows", [AH, S + P], F32, kind="Internal").ap()
        c_row_dram = nc.dram_tensor("c_bias_rows", [CH, S + P], F32, kind="Internal").ap()
        ab_dram = nc.dram_tensor("a_bias_by_distance", [P + 1, BAND], F32, kind="Internal").ap()
        g_dram = nc.dram_tensor("bias_by_distance", [P + 1, BAND], F32, kind="Internal").ap()
        block = ctx.enter_context(nc.Block())

        def end_stage(eng, n):
            eng.drain().then_inc(q.stage_end, 1)
            eng.wait_ge(q.stage_end, 3 * (n - 1))

        def stream(eng, name, count, step, between=None):
            pair = sum(PER[name])
            for k in range(min(2, count)):
                n = GROUP[name] + k
                step(k, n, 0, GROUP_END[n - 2] if n >= 2 else 0)
            if between:
                between()
            if count >= 4:
                with eng.Fori(0, (count - 2) // 2) as i:
                    for u in range(2):
                        step(2 + u, GROUP[name] + 2 + u, i, GROUP_END[GROUP[name] + u] + pair * i)
            if count > 2 and count % 2:
                n = GROUP[name] + count - 1
                step(count - 1, n, 0, GROUP_END[n - 2])

        @block.sync
        def _(sp):
            sp.dma_start(a_onehot, a["onehot"]).then_inc(q.table_in, 16)
            sp.dma_start(a_relt, a["table"].rearrange("a (b h) -> (a b) h", h=AH)).then_inc(q.table_in, 16)
            sp.dma_start(vec[:, :], a["vec"]).then_inc(q.consts_in, 16)
            sp.dma_start(consts[:, :], a["consts"]).then_inc(q.consts_in, 16)

            def load_x():
                for c in range(DC):
                    sp.dma_start(h[:, c, :], a["x_t"][:, c, :]).then_inc(q.x_in, 16)

            def bias_by_distance(n, row_dram, dram, rows, parts):
                sp.wait_ge(q.g_rowed, n + 1)
                sp.dma_start(row_dram, rows).then_inc(q.g_written, 16)
                sp.wait_ge(q.g_written, 32 * n + 16)
                sp.dma_start(bass.AP(tensor=dram.tensor, offset=0, ap=[[BAND + 1, P], [2 * S, AH], [1, S + P]]),
                             bass.AP(tensor=row_dram.tensor, offset=0, ap=[[0, P], [S + P, AH], [1, S + P]]))\
                    .then_inc(q.g_written, 16)
                sp.wait_ge(q.g_written, 32 * (n + 1))
                for dst, c in parts:
                    band = bass.AP(tensor=dram.tensor, offset=P - 1 + c, ap=[[BAND, P], [2 * S, AH], [1, S - c]])
                    sp.dma_start(dst, band).then_inc(q.g_read, 16)

            def a_bias_by_distance():
                bias_by_distance(0, a_row_dram, ab_dram, a_rows,
                                 [(a_bias[:, :, OFF[i]:OFF[i] + LEN[i]], S - LEN[i]) for i in range(NQ)])

            def c_bias_by_distance():
                bias_by_distance(1, c_row_dram, g_dram, c_rows, [(c_bias, 0)])

            for name, count, blocks, per in STREAM:
                src = a["w_" + name]

                def load(k, n, i, end):
                    wait(sp, q.weights_split, n - 1 + 2 * i if n >= 2 else 0)
                    sp.dma_start(slots[:, n % 2, 0:blocks[k % 2] * P], src[k + 2 * i, :, 0:blocks[k % 2] * P])\
                        .then_inc(landed[n % 2], 16)
                    if n == 0 and name == "a_qkv":
                        load_x()
                stream(sp, name, count, load, {"a_qkv": a_bias_by_distance, "c_in": c_bias_by_distance}.get(name))
            sp.wait_ge(q.out_stored, 16 * DC)

        @block.tensor
        def _(pe):
            def norm_sums(name):
                pe.wait_ge(q.squares_added, (DC - 1) * (NORM[name] + 1))
                pe.matmul(stat[:, :], ones, sq_sum, start=True, stop=True).then_inc(q.h_summed, 1)

            def weights(name, k, i=0):
                n = GROUP[name] + k
                pe.wait_ge(q.weights_split, n + 1 + i)
                return w_hi[:, n % 2, :], w_lo[:, n % 2, :]

            def tile(t, parity, w, first, rhs):
                wait(pe, q.tile_taken, t - 1)
                for k, (x_hi, x_lo) in enumerate(rhs):
                    hi, lo = (p_[:, (first + k) * P:(first + k + 1) * P] for p_ in w)
                    pe.matmul(lin[:, parity, :], hi, x_hi, start=k == 0, stop=False)
                    pe.matmul(lin[:, parity, :], hi, x_lo, start=False, stop=False)
                    mm = pe.matmul(lin[:, parity, :], lo, x_hi, start=False, stop=k == len(rhs) - 1)
                mm.then_inc(q.tile_done, 1)

            def parts(hi, lo, n):
                return [(hi[:, c, :], lo[:, c, :]) for c in range(n)]

            def first_tile(norm, name, rhs, gained=None):
                w, t = weights(name, 0), TILE[name]
                gained, n = gained or (q.h_gained, DC * NORM[norm] if norm else 0)
                wait(pe, q.tile_taken, t - 1)
                for c, (x_hi, x_lo) in enumerate(rhs):
                    hi, lo = (p_[:, c * P:(c + 1) * P] for p_ in w)
                    pe.wait_ge(gained, n + c + 1)
                    pe.matmul(lin[:, t % 2, :], hi, x_hi, start=c == 0, stop=False)
                    pe.matmul(lin[:, t % 2, :], hi, x_lo, start=False, stop=False)
                    mm = pe.matmul(lin[:, t % 2, :], lo, x_hi, start=False, stop=c == DC - 1)
                mm.then_inc(q.tile_done, 1)
                if norm:
                    norm_sums(norm)

            def linear(name, rhs, groups, ready=None, norm=None, first=True):
                def turn_(i, us):
                    for u in us:
                        if ready:
                            pe.wait_ge(*ready[u])
                        w = weights(name, u, 2 * i)
                        t = TILE[name] + u
                        tile(t + 2 * i, t % 2, w, 0, rhs[u])
                assert PER[name] == (1, 1)
                if norm:
                    first_tile(norm, name, rhs[0])
                if norm or not first:
                    turn_(0, (1,))
                with pe.Fori(1 if norm or not first else 0, groups // 2) as i:
                    turn_(i, (0, 1))
                if groups % 2:
                    turn_(groups // 2, (0,))

            def c_bias_rows():
                pe.wait_ge(q.extra_in, 16 * 4)
                pe.matmul(scores[0:CH, 0, :], relt, onehot, start=True, stop=True).then_inc(q.g_made, 1)

            def ple(n):
                name = f"ple{n}"

                def gate_and_projection(u, i, gate=True):
                    w = weights(name, u, 2 * i)
                    t = TILE[name] + 2 * u
                    if gate:
                        tile(t + 4 * i, t % 2, w, 0, gs)
                    tile(t + 1 + 4 * i, (t + 1) % 2, w, DC, parts(p_hi, p_lo, 2))
                first_tile(name, name, gs)
                pe.wait_ge(q.p_split, 2 * (n + 1))
                gate_and_projection(0, 0, False)
                gate_and_projection(1, 0)
                if n == 1:
                    c_bias_rows()
                with pe.Fori(1, DC // 2) as i:
                    gate_and_projection(0, i)
                    gate_and_projection(1, i)

            gs = parts(g_hi, g_lo, DC)

            def ffn_products(n):
                linear(f"ffn{n}_in", (gs, gs), 2 * FC, norm=f"ffn{n}")
                hidden, half = parts(f_hi, f_lo, FC), FC // 2
                linear(f"ffn{n}_out", (hidden[:half], hidden[half:]), 2 * DC,
                       [(q.f_through, FC * n + half), (q.f_through, FC * n + FC)])

            def output_products(name, n, rhs, halves):
                pe.wait_ge(q.tile_taken, TILE[name] - 1)
                first_tile(None, name, rhs[:DC], (q.out_split, n))
                linear(name, (rhs[:DC], rhs[DC:]) if halves else (rhs, rhs), (1 + halves) * DC,
                       [(q.out_split, n + len(rhs))] * 2, first=False)

            def ffn(n):
                ffn_products(n)

            def turn_weights(src, i, dst_bank):
                for j in range(i + 1):
                    mm = pe.transpose(dst_bank[:, j * P:(j + 1) * P], src[:, j * P:(j + 1) * P], ident)
                return mm

            pe.wait_ge(q.table_in, 32)
            pe.matmul(scores[0:AH, 0, :], a_relt, a_onehot, start=True, stop=True).then_inc(q.g_made, 1)
            pe.wait_ge(q.consts_in, 32)


            def a_step(s, par, proj, attn, tail):
                def lin_(j):
                    if isinstance(s, int) and s == 0 and j == 0:
                        first_tile("attn0", "a_qkv", gs)
                    elif proj:
                        w = weights("a_qkv", 3 * par + j, 3 * (s - par))
                        tile(TILE["a_qkv"] + 3 * s + j, (TILE["a_qkv"] + 3 * par + j) % 2, w, 0, gs)

                def score(k):
                    if attn:
                        hd, i = s - 1, NQ - 1 - k
                        if k == 0:
                            pe.wait_ge(q.a_normed, 2 * hd + 2)
                        wait(pe, q.a_biased, 4 * hd + k)
                        for c in range(2):
                            rows = slice(64 * c, 64 * c + 64)
                            mm = pe.matmul(scores[:, c, 0:LEN[i]], a_qk[rows, 1 - par, 0, i * P:(i + 1) * P],
                                           a_qk[rows, 1 - par, 1, 0:LEN[i]], start=True, stop=True)
                        mm.then_inc(q.a_scored, 1)

                def sums(j):
                    if proj:
                        pe.wait_ge(q.a_squared, 2 * s + j + 1)
                        wait(pe, q.a_logged, 2 * s + j)
                        if j == 0:
                            wait(pe, q.a_ologged, s - 1 if tail else 0)
                        pe.matmul(stat[:, :], ones64, a_sq[:, j, :], start=True, stop=True).then_inc(q.a_summed, 1)

                score(0)
                if proj:
                    lin_(0)
                if tail:
                    pe.wait_ge(q.a_osquared, s - 1)
                    pe.wait_ge(q.a_logged, 2 * s if proj or attn else 2 * AH)
                    pe.matmul(stat[:, :], ones, a_sq[:, 2, :], start=True, stop=True).then_inc(q.a_osummed, 1)
                score(1)
                lin_(1)
                score(2)
                sums(0)
                score(3)
                sums(1)
                lin_(2)
                if proj:
                    pe.wait_ge(q.tile_taken, TILE["a_qkv"] + 3 * s + 3)
                    wait(pe, q.a_otaken, s - 1)
                    for j in range(NQ):
                        mm = pe.transpose(obank[:, j * P:(j + 1) * P], a_raw[:, 2, j * P:(j + 1) * P], ident)
                    mm.then_inc(q.a_vturned, 1)
                if attn:
                    hd = s - 1
                    for k in range(NQ):
                        i = NQ - 1 - k
                        pe.wait_ge(q.a_weights, 4 * hd + k + 1)
                        wait(pe, q.a_tcopied, 4 * hd + k - 1)
                        turn_weights(a_sc[:, i, 0, :], i, turn[:, k % 2, :]).then_inc(q.a_turned, 1)
                    pe.wait_ge(q.a_vcopied, s + 1 if proj else AH)
                    pe.wait_ge(q.a_tcopied, 4 * hd + 4)
                    for j in range(NQ):
                        mm = pe.matmul(obank[:, j * P:S], a_v[:, 1 - par, j, :], a_pt[:, j, j * P:S],
                                       start=j == 0, stop=j == NQ - 1)
                    mm.then_inc(q.a_pv, 1)

            a_steps(pe, a_step)
            output_products("a_wo", 0, gs, 0)
            end_stage(pe, 2)
            ffn(0)
            end_stage(pe, 3)
            ple(0)
            end_stage(pe, 4)

            def down_sums(n):
                tiles, m = (((0, 1), ones), ((2,), ones64), ((3, 4, 5, 6), ones))[n]
                pe.wait_ge(q.bd_squared, tiles[-1] + 1)
                wait(pe, q.bd_logged, n)
                for t in tiles:
                    mm = pe.matmul(stat[:, :], m, b_dsq[:, t, :], start=t == tiles[0], stop=t == tiles[-1])
                mm.then_inc(q.bd_summed, 1)

            for name, n, rhs in (("b_dkv", 3, parts(b_g2_hi, b_g2_lo, DC)), ("b_dq", 4, gs)):
                for k in range(n):
                    t = TILE[name] + k
                    if t == TILE["b_dkv"]:
                        first_tile("attn1", name, rhs, (q.h_gained2, 0))
                    else:
                        if t == TILE["b_dq"]:
                            pe.wait_ge(q.h_gained, DC * (NORM["attn1"] + 1))
                        tile(t, t % 2, weights(name, k), 0, rhs)
                    if name == "b_dq" and k:
                        down_sums(k - 1)
            pe.wait_ge(q.bd_normed, 7)
            pe.matmul(obank[:, :], rot, b_rt[:, 0, :], start=True, stop=True).then_inc(q.bd_rotated, 1)
            end_stage(pe, 5)

            def b_step(s, par, proj, attn):
                cq, ck = parts(b_cq_hi, b_cq_lo, 4), parts(b_ckv_hi, b_ckv_lo, 2)
                at_ = (0, 4, 8, 0, 2, 4, 6)

                def lin_(j):
                    if proj:
                        t = TILE["b_pair"] + 7 * par + j
                        w = weights("b_pair", int(j >= 3), 2 * s)
                        tile(TILE["b_pair"] + 7 * s + j, t % 2, w, at_[j], cq if j < 3 else ck)

                def score(x, k):
                    if attn:
                        n, i = 8 * (s - 1) + 4 * x + k, NQ - 1 - k
                        if x == 0 and k == 0:
                            pe.wait_ge(q.b_normed, 5 * s)
                            pe.wait_ge(q.b_rope, s)
                        wait(pe, q.b_biased, n - 1)
                        qb = slice(i * P, (i + 1) * P)
                        rows = slice(64 * x, 64 * x + 64)
                        pe.matmul(scores[:, k % 2, 0:LEN[i]], b_qn[:, 1 - par, x, qb], b_kn[:, 1 - par, x, 0:LEN[i]],
                                  start=True, stop=False)
                        pe.matmul(scores[:, k % 2, 0:LEN[i]], b_qp[rows, 1 - par, qb], b_kp[rows, 0:LEN[i]],
                                  start=False, stop=True).then_inc(q.b_scored, 1)

                def turn_(x, *ks):
                    if attn:
                        for k in ks:
                            n, i = 8 * (s - 1) + 4 * x + k, NQ - 1 - k
                            pe.wait_ge(q.b_weights, n + 1)
                            wait(pe, q.b_tcopied, n - 1)
                            turn_weights(b_sc[:, x, i, :], i, turn[:, k % 2, :]).then_inc(q.b_turned, 1)

                def product(x):
                    if attn:
                        pe.wait_ge(q.b_tcopied, 8 * (s - 1) + 4 * x + 4)
                        if x == 0:
                            pe.wait_ge(q.b_vcopied, 2 * s)
                            wait(pe, q.b_otaken, 2 * s - 2)
                        else:
                            pe.wait_ge(q.b_vcopied, 2 * s + 2 if proj else 2 * B_PAIRS)
                            pe.wait_ge(q.b_otaken, 2 * s - 1)
                        for j in range(NQ):
                            mm = pe.matmul(obank[:, j * P:S], b_v[:, 1 - par, x, j * P:(j + 1) * P], b_pt[:, j, j * P:S],
                                           start=j == 0, stop=j == NQ - 1)
                        mm.then_inc(q.b_pv, 1)

                def turn_values(x):
                    if proj:
                        pe.wait_ge(q.tile_taken, TILE["b_pair"] + 7 * s + 6 + x)
                        if x == 0:
                            pe.wait_ge(q.b_rope, s + 1)
                        else:
                            pe.wait_ge(q.b_vcopied, 2 * s + 1)
                        for j in range(NQ):
                            mm = pe.transpose(obank[:, j * P:(j + 1) * P], b_raw[:, 5 + x, j * P:(j + 1) * P], ident)
                        mm.then_inc(q.b_vturned, 1)

                def sums(j):
                    if proj:
                        pe.wait_ge(q.b_squared, 5 * s + j + 1)
                        wait(pe, q.b_logged, 5 * s + j)
                        pe.matmul(stat[:, :], ones64 if j == 2 else ones, b_sq[:, j, :], start=True, stop=True)\
                            .then_inc(q.b_summed, 1)

                lin_(0); score(0, 0); lin_(1); score(0, 1); lin_(2); sums(0); score(0, 2); lin_(3); sums(1)
                score(0, 3); lin_(4); sums(2); score(1, 0); turn_(0, 0, 1); lin_(5); sums(3); score(1, 1)
                turn_(0, 2, 3); lin_(6); sums(4); score(1, 2); product(0)
                if proj:
                    pe.wait_ge(q.b_normed, 5 * s + 3)
                    if attn:
                        pe.wait_ge(q.b_otaken, 2 * s - 1)
                    wait(pe, q.b_vcopied, 2 * s)
                    pe.matmul(obank[:, :], rot, b_rt[:, 0, :], start=True, stop=True).then_inc(q.b_rotated, 1)
                score(1, 3); turn_values(0); turn_(1, 0); turn_values(1); turn_(1, 1, 2, 3); product(1)

            b_steps(pe, b_step)
            output_products("b_wo", DC, parts(b_o_hi, b_o_lo, BH), 1)
            end_stage(pe, 6)
            ffn(1)
            end_stage(pe, 7)
            ple(1)
            end_stage(pe, 8)
            mix = parts(c_mix_hi, g_lo, DC)
            linear("c_in", (mix, mix), 23, norm="mix2")
            end_stage(pe, 9)

            pe.wait_ge(q.extra_in, 16 * 4)
            pe.matmul(scores[:, 1, :], walpha[32:48, :], c_z[32:48, 22, :], start=True, stop=True).then_inc(q.gl_alpha, 1)
            for k in range(NQ):
                mm = pe.transpose(stat[:, k * P:(k + 1) * P], c_z[:, 22, k * P:(k + 1) * P], ident)
            mm.then_inc(q.gates_turned, 1)
            for x in range(2):
                for j in range(NQ):
                    mm = pe.transpose(turn[:, x, j * P:(j + 1) * P], c_z[:, 6 + x, j * P:(j + 1) * P], ident)
                mm.then_inc(q.c_vturned, 1)
            for k in range(8):
                w = weights("c_cmp", k)
                pe.wait_ge(q.zp_made, 16)
                t = TILE["c_cmp"] + k
                pe.wait_ge(q.tile_taken, t - 1)
                for c in range(8):
                    for x in range(2):
                        mm = pe.matmul(lin[:, t % 2, 0:2 * NCMP], w[x][:, c * P:(c + 1) * P].bitcast(F32),
                                       c_zp[:, k // 4, 8 * (k % 2) + c, :], start=c == 0 and x == 0,
                                       stop=c == 7 and x == 1)
                mm.then_inc(q.tile_done, 1)
            pe.wait_ge(q.hid_act, 4)
            for x in range(2):
                for c in range(2):
                    mm = pe.matmul(obank[64 * x:64 * x + 64, 0:NCMP], w2c[:, c, :],
                                   c_hid[:, c, x * NCMP:(x + 1) * NCMP], start=c == 0, stop=c == 1)
            mm.then_inc(q.kc_made, 1)
            pe.wait_ge(q.kc_copied, 1)
            for x in range(2):
                for c in range(2):
                    mm = pe.matmul(obank[0:NCMP, x * CD:(x + 1) * CD], c_hid[:, 2 + c, x * NCMP:(x + 1) * NCMP],
                                   w2c[:, 2 + c, :], start=c == 0, stop=c == 1)
            mm.then_inc(q.kc_made, 1)
            pe.wait_ge(q.kc_copied, 3)
            end_stage(pe, 10)
            pe.wait_ge(q.gl_abs, 1)
            for kv in range(2):
                for t in range(4):
                    for i in range(NQ):
                        hd = 4 * kv + t
                        at_ = (t * NQ + i) * NCMP
                        mm = pe.matmul(scores[:, kv, at_:at_ + NCMP], c_z[64 * kv:64 * kv + 64, t, i * P:(i + 1) * P],
                                       c_kc[64 * kv:64 * kv + 64, 0:NCMP], start=True, stop=True)
                mm.then_inc(q.cc_scored, 1)
            def c_out_product(hd, j):
                out_rows = slice(64 * (hd % 2), 64 * (hd % 2) + 64)
                kv = hd // 4
                if j == 0:
                    pe.wait_ge(q.c_tcopied, 8 * hd + 8)
                    wait(pe, q.c_otaken, hd // 2)
                for x in range(2):
                    pe.matmul(obank[out_rows, j * P:S], c_v[:, x, j, kv * CD:(kv + 1) * CD],
                              c_pts[hd % 2][:, x, j, j * P:S], start=j == 0 and x == 0, stop=False)
                if j == NQ - 1:
                    pe.matmul(obank[out_rows, :], c_vc[0:NCMP, kv, :], c_ct[0:NCMP, hd, :],
                              start=False, stop=True).then_inc(q.c_pv, 1)

            def cc_turn(hd):
                pe.wait_ge(q.cc_scaled, 1)
                pe.wait_ge(q.c_vcopied, 2)
                wait(pe, q.cc_copied, hd - 1)
                for i in range(NQ):
                    mm = pe.transpose(turn[0:NCMP, hd % 2, i * P:(i + 1) * P], c_cs[:, hd, i, :], ident)
                mm.then_inc(q.cc_turned, 1)

            pe.wait_ge(q.cc_biased, 2)
            for s in range(CH + 2):
                for k in range(NQ):
                    i = NQ - 1 - k
                    if s < CH:
                        rows = slice(64 * (s // 4), 64 * (s // 4) + 64)
                        wait(pe, q.c_biased, 4 * s + k)
                        for x in range(2):
                            mm = pe.matmul(scores[:, x, 0:LEN[i]], c_z[rows, s % 4, i * P:(i + 1) * P],
                                           c_z[rows, 4 + x, 0:LEN[i]], start=True, stop=True)
                        mm.then_inc(q.c_scored, 1)
                    if s == 0:
                        cc_turn(2 * k)
                        cc_turn(2 * k + 1)
                    if s == 1 and k == 0:
                        pe.wait_ge(q.cc_copied, CH)
                    if s > 1:
                        c_out_product(s - 2, k)
                    if 0 < s <= CH:
                        n = 4 * (s - 1) + k
                        pe.wait_ge(q.c_weights, 2 * n + 2)
                        for x in range(2):
                            wait(pe, q.c_tcopied, 2 * n - 3 + x)
                            turn_weights(c_sc[:, i, x, :], i, turns[n % 2][:, x, :]).then_inc(q.c_turned, 1)
            end_stage(pe, 11)

            pe.wait_ge(q.conv_step, 2 * CW)
            for x in range(2):
                mm = pe.matmul(stat[:, :], ones, c_acc[:, x, :], start=x == 0, stop=x == 1)
            mm.then_inc(q.ln_summed, 1)
            pe.wait_ge(q.gl_prod, 3)
            for hd in range(GH):
                rows = slice(GK * hd, GK * hd + GK)
                b = (scores[:, 0, :], scores[:, 1, :], turn[:, 0, :], turn[:, 1, :])[hd]
                for n in range(NCH):
                    ch = slice(n * GCH, (n + 1) * GCH)
                    mm = pe.matmul(b[64 * (n % 2):64 * (n % 2) + 64, (n // 2) * GCH:(n // 2 + 1) * GCH],
                                   gl_kt[rows, ch], gl_qt[rows, ch], start=True, stop=True)
                mm.then_inc(q.gl_att, 1)
            for j in range(NQ):
                mm = pe.transpose(obank[:, j * P:(j + 1) * P], gl_kd[:, j * P:(j + 1) * P], ident)
            mm.then_inc(q.gl_kdt, 1)
            for x in range(2):
                for j in range(NQ):
                    mm = pe.transpose(lin[:, x, j * P:(j + 1) * P], c_z[:, 18 + x, j * P:(j + 1) * P], ident)
                mm.then_inc(q.gl_kdt, 1)
            pe.wait_ge(q.ln_sq, 2)
            for x in range(2):
                mm = pe.matmul(stat[:, :], ones, gl_s[:, x, :], start=x == 0, stop=x == 1)
            mm.then_inc(q.ln_summed, 1)
            pe.wait_ge(q.gl_kdc, 3)
            pe.wait_ge(q.gl_attc, 4)
            for n in range(NCH):
                rows = slice(64 * (n % 2), 64 * (n % 2) + 64)
                b = (scores[:, 0, :], scores[:, 1, :])[n % 2]
                if n >= 2:
                    pe.wait_ge(q.gl_uc, 4 * (n - 1))
                mm = pe.matmul(b[:, 0:2 * P], gl_kdt[rows, n // 2, :], gl_vt[rows, n // 2, :], start=True, stop=True)
                mm.then_inc(q.gl_u, 1)
            pe.wait_ge(q.gl_mask, 2)
            for x in range(2):
                for odd in range(2):
                    rows = slice(64 * odd, 64 * odd + 64)
                    b = (lin[:, 0, :], lin[:, 1, :], turn[:, 0, :], turn[:, 1, :])[2 * x + odd]
                    for y in range(2):
                        for n2 in range(NCH // 2):
                            mm = pe.matmul(b[64 * y:64 * y + 64, n2 * GCH:(n2 + 1) * GCH],
                                           gl_vt[rows, n2, (2 * x + y) * GV:(2 * x + y + 1) * GV],
                                           gl_am[rows, 2 * x + y, n2, :], start=True, stop=True)
                    mm.then_inc(q.gl_out, 1)
            pe.wait_ge(q.gl_bd, 4)
            pe.wait_ge(q.ln_logged, 1)
            for x in range(2):
                b = (stat, obank)[x]
                for n in range(NCH):
                    ch = slice(n * GCH, (n + 1) * GCH)
                    mm = pe.matmul(b[:, ch], gl_bds[:, n, x * P:(x + 1) * P], gl_qt[:, ch], start=True, stop=True)
                mm.then_inc(q.gl_out, 1)
            for x in range(2):
                pe.wait_ge(q.gl_sq, x + 1)
                pe.wait_ge(q.gl_sum, 2)
                wait(pe, q.gl_log, x)
                pe.matmul(stat[:, :], ones64, gl_s[:, x, :], start=True, stop=True).then_inc(q.gl_ss, 1)
            end_stage(pe, 12)
            output_products("c_out", DC + BH, gs, 0)
            end_stage(pe, 13)
            ffn_products(2)
            end_stage(pe, 14)
            ple(2)
            end_stage(pe, 15)
            norm_sums("final")


        @block.vector
        def _(ve):
            rounded = [0]

            def rounding(hi, gain, c):
                ve.tensor_scalar(hi[:, c, :], h[:, c, :], vec[:, bass.ds(VEC[gain] + c, 1)], None, ALU.mult)\
                    .then_inc(q.h_rounded, 1)

            def remainder(hi, lo, gain, c, n, signal):
                ve.wait_ge(q.h_rounded, n + c + 1)
                ve.scalar_tensor_tensor(out=lo[:, c, :], in0=h[:, c, :], scalar=vec[:, bass.ds(VEC[gain] + c, 1)],
                                        in1=hi[:, c, :].bitcast(F32), op0=ALU.mult, op1=ALU.subtract)\
                    .then_inc(signal, 1)

            def gains(name):
                for c in range(DC):
                    rounding(g_hi, name, c)
                    remainder(g_hi, g_lo, name, c, rounded[0], q.h_gained)
                rounded[0] += DC

            def add_square(norm, c):
                n = NORM[norm]
                ve.wait_ge(q.h_squared, DC * n + c + 1)
                wait(ve, q.squares_added, (DC - 1) * n + c - 1)
                ve.tensor_tensor(sq_sum, sq_sum, sq_last, ALU.add).then_inc(q.squares_added, 1)

            def chunks(step, norm, gain=None, hi=None, lo=None, signal=None):
                n = rounded[0]

                def one(i, k):
                    c = 2 * i + k
                    done = step(i, k)
                    if gain:
                        ve.wait_ge(*done)
                        rounding(hi, gain, c)
                    if not (isinstance(c, int) and c < 2):
                        add_square(norm, c - 1)
                    if lo:
                        remainder(hi, lo, gain, c, n, signal)
                one(0, 0)
                one(0, 1)
                if norm == "mix2":
                    c_bias_rows()
                with ve.Fori(1, DC // 2) as i:
                    one(i, 0)
                    one(i, 1)
                rounded[0] += DC if gain else 0

            def out_lows(n, src, hi, lo, chunks):
                for k in chunks:
                    ve.wait_ge(q.out_rounded, n + k + 1)
                    ve.tensor_tensor(lo[:, k, :], src[:, k, :], hi[:, k, :].bitcast(F32), ALU.subtract)\
                        .then_inc(q.out_split, 1)

            def residual(name, norm, *gain):
                t, halves = TILE[name], name in ("ffn0_out", "ffn1_out", "ffn2_out", "b_wo")

                def add(i, k):
                    for u in range(1 + halves):
                        j = 2 * k + u if halves else k
                        at_ = t + (4 if halves else 2) * i + j
                        ve.wait_ge(q.tile_done, at_ + 1)
                        if u:
                            ve.wait_ge(q.tile_taken, at_)
                        ve.tensor_tensor(h[:, 2 * i + k, :], lin[:, (t + j) % 2, :], h[:, 2 * i + k, :], ALU.add)\
                            .then_inc(q.tile_taken, 1)
                    return q.tile_taken, at_ + 1
                chunks(add, norm, *gain)

            def take(t, par, dst):
                ve.wait_ge(q.tile_done, t + 1)
                ve.tensor_tensor(dst, lin[:, par, :], r[:, :], ALU.mult).then_inc(q.tile_taken, 1)

            def bias_of_any_positions():
                def built(ins, value):
                    ins.then_inc(q.bias_built, 1)
                    ve.wait_ge(q.bias_built, value)

                built(ve.tensor_tensor(a_diff[:, AH:], a_tab[:, AH:], a_tab[:, 0:(BUCKETS - 1) * AH], ALU.subtract), 1)
                for i in range(NQ):
                    ve.tensor_scalar(a_dist[:, OFF[i]:OFF[i] + LEN[i]], posf[:, 0:LEN[i]], -1.0, posq[:, i:i + 1],
                                     ALU.mult, ALU.add).then_inc(q.bias_built, 1)
                    for hd in range(AH):
                        ve.tensor_scalar(a_bias[:, hd, OFF[i]:OFF[i] + LEN[i]], maskt[:, S - LEN[i]:S],
                                         a_tab[:, hd:hd + 1], None, ALU.add).then_inc(q.bias_built, 1)
                base = 1 + NQ * (1 + AH)
                with ve.Fori(0, BUCKETS - 1) as b:
                    ve.wait_ge(q.bias_built, base + (1 + AH) * b)
                    ve.tensor_scalar(a_mask, a_dist, vec[:, bass.ds(VEC["t5_start"] + b, 1)], None, ALU.is_ge)\
                        .then_inc(q.bias_built, 1)
                    ve.wait_ge(q.bias_built, base + 1 + (1 + AH) * b)
                    for hd in range(AH):
                        ve.scalar_tensor_tensor(out=a_bias[:, hd, :], in0=a_mask, scalar=a_diff[:, bass.ds(AH * b + AH + hd, 1)],
                                                in1=a_bias[:, hd, :], op0=ALU.mult, op1=ALU.add).then_inc(q.bias_built, 1)
                ve.wait_ge(q.bias_built, base + (1 + AH) * (BUCKETS - 1))

            def hidden(n, i, u, k):
                at_ = 2 * FC * n + 4 * i + 2 * u
                ve.tensor_tensor(f_c[:, k, :], f_c[:, k, :], f_sg[:, u, :], ALU.mult).then_inc(q.f_split, 1)
                ve.wait_ge(q.f_split, at_ + 1)
                ve.tensor_copy(f_hi[:, 2 * i + u, :], f_c[:, k, :]).then_inc(q.f_split, 1)
                ve.wait_ge(q.f_split, at_ + 2)
                ve.tensor_tensor(f_lo[:, 2 * i + u, :], f_c[:, k, :], f_hi[:, 2 * i + u, :].bitcast(F32), ALU.subtract)\
                    .then_inc(q.f_through, 1)

            def conv_ffn(n):
                if n == 0:
                    gains("ffn0")
                ve.wait_ge(q.r_ready, NORM[f"ffn{n}"] + 1)
                t0, f0 = TILE[f"ffn{n}_in"], 2 * FC * n

                def pair(i, u):
                    for j in range(2):
                        k = 2 * u + j
                        ve.wait_ge(q.tile_done, t0 + k + 1 + 4 * i)
                        wait(ve, q.f_first, f0 + 4 * i + k - 3)
                        ve.tensor_tensor(f_u[:, k, 2:S + 2], lin[:, (t0 + k) % 2, :], r[:, :], ALU.mult)\
                            .then_inc(q.tile_taken, 1)
                    for j in range(2):
                        k = 2 * u + j
                        w = VEC[f"conv{n}"] + 4 * k + 16 * i
                        ve.wait_ge(q.f_first, f0 + k + 1 + 4 * i)
                        ve.scalar_tensor_tensor(out=f_c[:, k, :], in0=f_u[:, k, 1:S + 1], scalar=vec[:, bass.ds(w + 1, 1)],
                                                in1=f_c[:, k, :], op0=ALU.mult, op1=ALU.add).then_inc(q.f_conv, 1)
                        ve.wait_ge(q.f_conv, 2 * f0 + 2 * k + 1 + 8 * i)
                        ve.scalar_tensor_tensor(out=f_c[:, k, :], in0=f_u[:, k, 0:S], scalar=vec[:, bass.ds(w, 1)],
                                                in1=f_c[:, k, :], op0=ALU.mult, op1=ALU.add).then_inc(q.f_conv, 1)
                    ve.wait_ge(q.f_silu, FC * n + u + 1 + 2 * i)
                    ve.wait_ge(q.f_conv, 2 * f0 + 4 * u + 4 + 8 * i)
                    hidden(n, i, u, 2 * u)

                ve.memset(f_u[:, :, 0:2], 0.0).then_inc(q.setup_step, 1)
                ve.wait_ge(q.setup_step, steps[0] + n + 1)
                pair(0, 0)
                pair(0, 1)
                with ve.Fori(1, FC // 2) as i:
                    pair(i, 0)
                    pair(i, 1)
                residual(f"ffn{n}_out", f"ple{n}", f"ple{n}", g_hi, g_lo, q.h_gained)

            def c_bias_rows():
                ve.memset(c_rows[:, S:], NEG).then_inc(q.setup_step, 1)
                ve.wait_ge(q.setup_step, steps[0] + 3)
                ve.wait_ge(q.g_made, 2)
                ve.tensor_copy(c_rows[:, 0:S], scores[0:CH, 0, :]).then_inc(q.g_rowed, 1)

            def ple(n, norm, *gain):
                ve.wait_ge(q.p_in, 16 * (n + 1))
                ve.tensor_copy(p_hi[:, :, :], p_in_t[:, :, :]).then_inc(q.p_split, 1)
                ve.wait_ge(q.p_split, 2 * n + 1)
                ve.tensor_tensor(p_lo[:, :, :], p_in_t[:, :, :], p_hi[:, :, :].bitcast(F32), ALU.subtract).then_inc(q.p_split, 1)
                ve.wait_ge(q.r_ready, NORM[f"ple{n}"] + 1)
                t0, g0 = TILE[f"ple{n}"], DC * n

                def one(i, j):
                    b = j
                    ve.wait_ge(q.tile_done, t0 + 2 * j + 1 + 4 * i)
                    ve.tensor_tensor(p_gp[:, b, :], lin[:, (t0 + 2 * j) % 2, :], r[:, :], ALU.mult)\
                        .then_inc(q.tile_taken, 1)
                    ve.wait_ge(q.tile_done, t0 + 2 * j + 2 + 4 * i)
                    ve.wait_ge(q.ple_sigmoid, g0 + j + 1 + 2 * i)
                    ve.tensor_tensor(p_t[:, b, :], lin[:, (t0 + 2 * j + 1) % 2, :], p_sg[:, b, :], ALU.mult)\
                        .then_inc(q.tile_taken, 1)
                    ve.wait_ge(q.tile_taken, t0 + 2 * j + 2 + 4 * i)
                    ve.tensor_tensor(h[:, 2 * i + j, :], h[:, 2 * i + j, :], p_t[:, b, :], ALU.add)\
                        .then_inc(q.residual_added, 1)
                    return q.residual_added, g0 + j + 1 + 2 * i
                chunks(one, norm, *gain)

            steps = [0]

            def did(ins):
                steps[0] += 1
                ins.then_inc(q.setup_step, 1)
                ve.wait_ge(q.setup_step, steps[0])

            did(ve.memset(a_rows[:, S:], NEG))
            did(ve.memset(eps[:, :], EPS))
            ve.wait_ge(q.g_made, 1)
            ve.tensor_copy(a_rows[:, 0:S], scores[0:AH, 0, :]).then_inc(q.g_rowed, 1)
            ve.wait_ge(q.consts_in, 32)
            ve.wait_ge(q.x_in, 16 * DC)
            for c in range(DC):
                rounding(g_hi, "attn0", c)
                if c:
                    add_square("attn0", c)
                remainder(g_hi, g_lo, "attn0", c, 0, q.h_gained)
            rounded[0] += DC
            def regularity_and_lam():
                ve.wait_ge(q.positions_in, 16 * (NQ + 2))
                did(ve.tensor_copy(posf, pos_i))
                did(ve.tensor_copy(posq, posq_i[:, :]))
                did(ve.tensor_tensor(a_step_ok, posf[:, 1:S], posf[:, 0:S - 1], ALU.subtract))
                did(ve.tensor_scalar(a_step_ok, a_step_ok, 1.0, None, ALU.is_equal))
                did(ve.tensor_reduce(regular[:, 0:1], a_step_ok, AX.X, ALU.min))
                did(ve.tensor_copy(regular_i[:, :], regular[:, 0:1]))
                ve.wait_ge(q.lam_in, 16)
                for x in range(2):
                    did(ve.tensor_tensor(a_lam[:, 4, :], a_lam[:, 2 * x, :], a_lam[:, 2 * x + 1, :], ALU.mult))
                    did(ve.tensor_reduce(lamd[:, x:x + 1], a_lam[:, 4, :], AX.X, ALU.add))
                ve.sem_inc(q.lam_dots, 1)

            def angles():
                turn_parts = (6.28125, 0.0019340515136718750, 2 * math.pi - 6.28125 - 0.0019340515136718750)
                ang, k_ = cosb[:, :], a_rawo
                did(ve.tensor_scalar(ang, posf, v1("inv_freq"), None, ALU.mult))
                did(ve.tensor_scalar(k_, ang, 1 / (2 * math.pi), 12582912.0, ALU.mult, ALU.add))
                did(ve.tensor_scalar(k_, k_, 12582912.0, None, ALU.subtract))
                for part in turn_parts:
                    did(ve.scalar_tensor_tensor(out=ang, in0=k_, scalar=-part, in1=ang, op0=ALU.mult, op1=ALU.add))
                did(ve.tensor_scalar(sinb[:, :], ang, PI_IN, -PI_IN, ALU.min, ALU.max))
                did(ve.tensor_scalar(ang, ang, math.pi / 2, None, ALU.add))
                did(ve.tensor_scalar(k_, ang, math.pi, -2 * math.pi, ALU.is_gt, ALU.mult))
                did(ve.tensor_tensor(ang, ang, k_, ALU.add))
                did(ve.tensor_scalar(ang, ang, PI_IN, -PI_IN, ALU.min, ALU.max))
                ve.sem_inc(q.angles_ready, 1)

            def lam_and_bias():
                ve.wait_ge(q.lam_exps, 1)
                did(ve.tensor_tensor(nlam, lame[:, 1:2], lame[:, 0:1], ALU.subtract))
                did(ve.tensor_scalar(nlam, nlam, LAM_INIT, None, ALU.subtract))
                did(ve.tensor_scalar(asub, v1("a_sub"), 1.0 - LAM_INIT, None, ALU.mult))
                ve.wait_ge(q.g_read, 16 * NQ)
                in_a_row = ve.value_load(regular_i[0:1, 0:1])
                with ve.If(in_a_row < 1):
                    bias_of_any_positions()

            ve.wait_ge(q.r_ready, 1)

            def a_step(s, par, proj, attn, tail):
                hd = s - 1

                def take_(j):
                    if proj:
                        take(TILE["a_qkv"] + 3 * s + j, (TILE["a_qkv"] + 3 * par + j) % 2, a_raw[:, j, :])

                def biased(k):
                    if attn:
                        n, i = 4 * hd + k, NQ - 1 - k
                        ve.wait_ge(q.a_scored, n + 1)
                        wait(ve, q.a_turned, n - 3)
                        bias = a_bias[:, hd, OFF[i]:OFF[i] + LEN[i]] if isinstance(hd, int) else \
                            a_bias[:, bass.ds(hd, 1), OFF[i]:OFF[i] + LEN[i]].rearrange("p a l -> p (a l)")
                        ve.scalar_tensor_tensor(out=a_sc[:, i, :, 0:LEN[i]], in0=scores[:, :, 0:LEN[i]],
                                                scalar=-(AQK ** -0.5),
                                                in1=bias.unsqueeze(1).broadcast_to([P, 2, LEN[i]]),
                                                op0=ALU.mult, op1=ALU.subtract).then_inc(q.a_biased, 1)
                        ve.wait_ge(q.a_biased, n + 1)
                        ve.tensor_reduce(nmax[:, 2 * i:2 * i + 2], a_sc[:, i, :, 0:LEN[i]], AX.X, ALU.min)\
                            .then_inc(q.a_min, 1)

                def weights_(k):
                    if attn:
                        n, i = 4 * hd + k, NQ - 1 - k
                        d = den[:, 2 * i:2 * i + 2]
                        ve.wait_ge(q.a_exped, 2 * n + 2)
                        ve.reciprocal(d, d).then_inc(q.a_recip, 1)
                        ve.wait_ge(q.a_recip, 2 * n + 1)
                        ve.tensor_tensor(d[:, 1:2], d[:, 1:2], nlam, ALU.mult).then_inc(q.a_recip, 1)
                        ve.tensor_scalar(a_sc[:, i, 0, 0:LEN[i]], a_sc[:, i, 0, 0:LEN[i]], d[:, 0:1], None, ALU.mult)\
                            .then_inc(q.a_scaled, 1)
                        ve.wait_ge(q.a_recip, 2 * n + 2)
                        ve.wait_ge(q.a_scaled, n + 1)
                        ve.scalar_tensor_tensor(out=a_sc[:, i, 0, 0:LEN[i]], in0=a_sc[:, i, 1, 0:LEN[i]],
                                                scalar=d[:, 1:2], in1=a_sc[:, i, 0, 0:LEN[i]], op0=ALU.mult,
                                                op1=ALU.add).then_inc(q.a_weights, 1)

                def normed(j):
                    if proj:
                        ve.wait_ge(q.a_factor, 2 * s + j + 1)
                        ve.scalar_tensor_tensor(out=a_qk[:, par, j, :], in0=a_raw[:, j, :],
                                                scalar=v1("a_q" if j == 0 else "a_k"), in1=a_ri[:, j, :],
                                                op0=ALU.mult, op1=ALU.mult).then_inc(q.a_normed, 1)

                biased(0)
                take_(0)
                if isinstance(s, int) and s == 0:
                    regularity_and_lam()
                if tail:
                    ve.wait_ge(q.a_ofactor, s - 1)
                    ve.scalar_tensor_tensor(out=a_o[:, s - 2, :], in0=a_rawo, scalar=asub, in1=a_ri[:, 2, :],
                                            op0=ALU.mult, op1=ALU.mult).then_inc(q.a_onormed, 1)
                biased(1)
                weights_(0)
                take_(1)
                if isinstance(s, int) and s == 0:
                    angles()
                biased(2)
                weights_(1)
                biased(3)
                normed(0)
                weights_(2)
                weights_(3)
                normed(1)
                take_(2)
                if isinstance(s, int) and s == 0:
                    lam_and_bias()
                if attn:
                    ve.wait_ge(q.a_pv, s)
                    ve.tensor_copy(a_rawo, obank[:, :]).then_inc(q.a_otaken, 1)

            a_steps(ve, a_step, lambda: out_lows(0, a_o, g_hi, g_lo, range(AH - 1)))
            out_lows(0, a_o, g_hi, g_lo, (AH - 1,))
            residual("a_wo", "ffn0")
            end_stage(ve, 2)
            add_square("ffn0", DC - 1)
            conv_ffn(0)
            end_stage(ve, 3)
            add_square("ple0", DC - 1)
            ple(0, "attn1", "kv", b_g2_hi, b_g2_lo, q.h_gained2)
            end_stage(ve, 4)
            add_square("attn1", DC - 1)

            gains("attn1")
            ve.wait_ge(q.r_ready, NORM["attn1"] + 1)
            t0 = TILE["b_dkv"]
            for j in range(7):
                take(t0 + j, (t0 + j) % 2, b_cr[:, j, :])
            for n, (tiles, vname) in enumerate((((0, 1), "ckv"), ((2,), "k_pe"), ((3, 4, 5, 6), "cq"))):
                ve.wait_ge(q.bd_factor, n + 1)
                for k, j in enumerate(tiles):
                    dst = b_rt[:, 0, :] if n == 1 else b_cr[:, j, :]
                    ve.scalar_tensor_tensor(out=dst, in0=b_cr[:, j, :], scalar=v1(vname, k), in1=b_ri[:, n, :],
                                            op0=ALU.mult, op1=ALU.mult).then_inc(q.bd_normed, 1)
            for k, j in enumerate((0, 1, 3, 4, 5, 6)):
                hi = b_ckv_hi[:, k, :] if k < 2 else b_cq_hi[:, k - 2, :]
                ve.wait_ge(q.bd_normed, j + 1)
                ve.tensor_copy(hi, b_cr[:, j, :]).then_inc(q.bd_rounded, 1)
            for k, j in enumerate((0, 1, 3, 4, 5, 6)):
                hi = b_ckv_hi[:, k, :] if k < 2 else b_cq_hi[:, k - 2, :]
                lo = b_ckv_lo[:, k, :] if k < 2 else b_cq_lo[:, k - 2, :]
                ve.wait_ge(q.bd_rounded, k + 1)
                ve.tensor_tensor(lo, b_cr[:, j, :], hi.bitcast(F32), ALU.subtract)
            ve.wait_ge(q.bd_rotated, 1)
            ve.tensor_tensor(b_rt[:, 1, :], obank[:, :], sinb[:, :], ALU.mult).then_inc(q.bd_terms, 1)
            ve.tensor_tensor(b_rt[:, 2, :], b_rt[:, 0, :], cosb[:, :], ALU.mult).then_inc(q.bd_terms, 1)
            ve.wait_ge(q.bd_terms, 2)
            ve.tensor_tensor(b_kp, b_rt[:, 1, :], b_rt[:, 2, :], ALU.add).then_inc(q.bd_terms, 1)
            end_stage(ve, 5)

            def b_step(s, par, proj, attn):
                def take_(j):
                    if proj:
                        ve.wait_ge(q.tile_done, TILE["b_pair"] + 7 * s + j + 1)
                        ve.tensor_copy(b_raw[:, j, :], lin[:, (TILE["b_pair"] + 7 * par + j) % 2, :])\
                            .then_inc(q.tile_taken, 1)

                def biased(x, k):
                    if attn:
                        n, i = 8 * (s - 1) + 4 * x + k, NQ - 1 - k
                        ve.wait_ge(q.b_scored, n + 1)
                        wait(ve, q.b_turned, n - 7)
                        ve.scalar_tensor_tensor(out=b_sc[:, x, i, 0:LEN[i]], in0=scores[:, k % 2, 0:LEN[i]],
                                                scalar=-((NOPE + ROPE) ** -0.5), in1=maskt[:, S - LEN[i]:S],
                                                op0=ALU.mult, op1=ALU.subtract).then_inc(q.b_biased, 1)
                        ve.wait_ge(q.b_biased, n + 1)
                        ve.tensor_reduce(nmax[:, 4 * x + i:4 * x + i + 1], b_sc[:, x, i, 0:LEN[i]], AX.X, ALU.min)\
                            .then_inc(q.b_min, 1)

                def weights_(x, k):
                    if attn:
                        n, i = 8 * (s - 1) + 4 * x + k, NQ - 1 - k
                        d = den[:, 4 * x + i:4 * x + i + 1]
                        ve.wait_ge(q.b_exped, n + 1)
                        ve.reciprocal(d, d).then_inc(q.b_recip, 1)
                        ve.wait_ge(q.b_recip, n + 1)
                        ve.tensor_scalar(b_sc[:, x, i, 0:LEN[i]], b_sc[:, x, i, 0:LEN[i]], d, None, ALU.mult)\
                            .then_inc(q.b_weights, 1)

                def normed(j):
                    if proj:
                        ve.wait_ge(q.b_factor, 5 * s + j + 1)
                        dst = (b_qn[:, par, 0, :], b_qn[:, par, 1, :], b_rt[:, 0, :], b_kn[:, par, 0, :],
                               b_kn[:, par, 1, :])[j]
                        vname = ("q_nope", "q_nope", "q_pe", "k_nope", "k_nope")[j]
                        ve.scalar_tensor_tensor(out=dst, in0=b_raw[:, j, :], scalar=v1(vname), in1=b_ri[:, j, :],
                                                op0=ALU.mult, op1=ALU.mult).then_inc(q.b_normed, 1)

                def output(x):
                    if attn:
                        ve.wait_ge(q.b_pv, 2 * s - 1 + x)
                        ve.tensor_copy(b_o[:, 2 * (s - 1) + x, :], obank[:, :]).then_inc(q.b_otaken, 1)

                take_(0); biased(0, 0); take_(1); biased(0, 1); weights_(0, 0); take_(2); biased(0, 2)
                weights_(0, 1); normed(0); take_(3); biased(0, 3); weights_(0, 2); normed(1); take_(4)
                biased(1, 0); weights_(0, 3); normed(2); take_(5); biased(1, 1); weights_(1, 0); normed(3)
                take_(6); biased(1, 2); weights_(1, 1); normed(4); output(0)
                if proj:
                    ve.wait_ge(q.b_rotated, s + 1)
                    ve.tensor_tensor(b_rt[:, 1, :], obank[:, :], sinb[:, :], ALU.mult).then_inc(q.b_terms, 1)
                    ve.tensor_tensor(b_rt[:, 2, :], b_rt[:, 0, :], cosb[:, :], ALU.mult).then_inc(q.b_terms, 1)
                    ve.wait_ge(q.b_terms, 2 * s + 2)
                    ve.tensor_tensor(b_qp[:, par, :], b_rt[:, 1, :], b_rt[:, 2, :], ALU.add).then_inc(q.b_rope, 1)
                biased(1, 3); weights_(1, 2); weights_(1, 3); output(1)

            b_steps(ve, b_step)
            out_lows(DC, b_o, b_o_hi, b_o_lo, range(BH))
            residual("b_wo", "ffn1", "ffn1", g_hi, g_lo, q.h_gained)
            end_stage(ve, 6)
            add_square("ffn1", DC - 1)
            conv_ffn(1)
            end_stage(ve, 7)
            add_square("ple1", DC - 1)
            mix_n = rounded[0]
            ple(1, "mix2", "mix2", c_mix_hi)
            end_stage(ve, 8)
            add_square("mix2", DC - 1)

            for c in range(DC):
                remainder(c_mix_hi, g_lo, "mix2", c, mix_n, q.h_gained)
            ve.wait_ge(q.r_ready, NORM["mix2"] + 1)
            t0 = TILE["c_in"]
            def c_take(j, jj):
                ve.wait_ge(q.tile_done, t0 + j + 1)
                ve.tensor_tensor(c_z[:, j, :], lin[:, (t0 + jj) % 2, :], r[:, :], ALU.mult).then_inc(q.tile_taken, 1)
            with ve.Fori(0, 11) as i:
                for u in range(2):
                    c_take(2 * i + u, u)
            c_take(22, 22)
            ve.memset(c_hp[:, :, 0:CW - 1], 0.0).then_inc(q.c_glu, 1)
            for x in range(2):
                ve.wait_ge(q.c_sigmoid, x + 1)
                ve.tensor_tensor(c_hp[:, x, CW - 1:], c_z[:, 12 + x, :], c_acc[:, x, :], ALU.mult)\
                    .then_inc(q.c_glu, 1)
            end_stage(ve, 9)

            for k in range(4):
                z = c_z[:, 8 + k, :].rearrange("p (n l) -> p l n", l=CMPS)
                for half in range(2):
                    rows = slice(64 * half, 64 * half + 64)
                    for over in range(2):
                        pos = vec[rows, VEC["cmp_pos"] + 16 * (k // 2) + 8 * over:VEC["cmp_pos"] + 16 * (k // 2) + 8 * over + 8]
                        ins = ve.tensor_tensor(c_zp[rows, k // 2, 8 * over:8 * over + 8, (k % 2) * NCMP:(k % 2 + 1) * NCMP],
                                               z[rows, half::2, over:over + NCMP],
                                               pos.unsqueeze(2).broadcast_to([64, 8, NCMP]), ALU.add)
                        ins.then_inc(q.zp_made, 1)
            for k in range(4):
                t = TILE["c_cmp"] + 2 * k
                ve.wait_ge(q.tile_done, t + 1)
                ve.tensor_copy(c_hid[:, k, :], lin[:, t % 2, 0:2 * NCMP]).then_inc(q.tile_taken, 1)
                ve.wait_ge(q.tile_done, t + 2)
                ve.wait_ge(q.tile_taken, t + 1)
                ve.tensor_tensor(c_hid[:, k, :], lin[:, (t + 1) % 2, 0:2 * NCMP], c_hid[:, k, :], ALU.add)\
                    .then_inc(q.tile_taken, 1)
            ve.memset(gl_reset, 1.0).then_inc(q.gl_scale, 1)
            ve.wait_ge(q.gl_scale, 1)
            ve.memset(gl_reset.rearrange("p (n c) -> p n c", c=GCH)[:, :, 0:1], 0.0).then_inc(q.gl_scale, 1)
            ve.wait_ge(q.gl_ln, 1)
            ve.scalar_tensor_tensor(out=gl_b, in0=gl_x, scalar=0.0, in1=gl_l, op0=ALU.min, op1=ALU.subtract)\
                .then_inc(q.gl_la, 1)
            ve.wait_ge(q.gl_la, 1)
            ve.tensor_scalar(gl_l, gl_b, 1.0 / TAU, None, ALU.mult).then_inc(q.gl_la, 1)
            ve.wait_ge(q.gl_la, 2)
            ve.wait_ge(q.gl_scale, 2)
            ve.tensor_tensor_scan(gl_b, gl_reset, gl_l, 0.0, ALU.mult, ALU.add).then_inc(q.gl_scan, 1)
            ve.wait_ge(q.gl_scan, 1)
            b3 = gl_b.rearrange("p (n c) -> p n c", c=GCH)
            ve.tensor_tensor(gl_l.rearrange("p (n c) -> p n c", c=GCH), b3[:, :, GCH - 1:GCH].broadcast_to([P, NCH, GCH]),
                             b3, ALU.subtract).then_inc(q.gl_scan, 1)
            ve.memset(c_cb[:, :, :, :], NEG).then_inc(q.cb_made, 1)
            ve.wait_ge(q.cb_made, 1)
            ve.wait_ge(q.g_read, G_READ + 16)
            for i in range(NQ):
                n = min(NCMP, 7 + 8 * i)
                first = S - P - P * i + CMPB - 1
                ve.tensor_copy(c_cb[:, :, i, 0:n], c_bias[:, :, first:first + CMPS * (n - 1) + 1:CMPS]).then_inc(q.cb_made, 1)
            ve.wait_ge(q.cb_made, 1 + NQ)
            ve.wait_ge(q.kc_made, 1)
            ve.tensor_copy(c_kc[:, 0:NCMP], obank[:, 0:NCMP]).then_inc(q.kc_copied, 1)
            ve.wait_ge(q.kc_made, 2)
            for x in range(2):
                ve.tensor_copy(c_vc[0:NCMP, x, :], obank[0:NCMP, x * CD:(x + 1) * CD]).then_inc(q.kc_copied, 1)
            end_stage(ve, 10)
            for kv in range(2):
                ve.wait_ge(q.cc_scored, kv + 1)
                ve.scalar_tensor_tensor(
                    out=c_cs[:, 4 * kv:4 * kv + 4, :, :].rearrange("p h i n -> p (h i n)"), in0=scores[:, kv, 0:4 * NQ * NCMP],
                    scalar=-(CD ** -0.5), in1=c_cb[:, 4 * kv:4 * kv + 4, :, :].rearrange("p h i n -> p (h i n)"),
                    op0=ALU.mult, op1=ALU.subtract).then_inc(q.cc_biased, 1)
            ve.wait_ge(q.cc_biased, 2)
            cs3 = c_cs[:, :, :, :].rearrange("p h i n -> p (h i) n")
            ve.tensor_reduce(c_cmin, cs3, AX.X, ALU.min).then_inc(q.cc_reduced, 1)
            ve.wait_ge(q.cc_reduced, 1)
            ve.tensor_tensor(cs3, cs3, c_cmin.unsqueeze(2).broadcast_to([P, CH * NQ, NCMP]), ALU.subtract)\
                .then_inc(q.cc_reduced, 1)
            ve.wait_ge(q.cc_exped, 1)
            ve.tensor_reduce(c_cden, cs3, AX.X, ALU.add).then_inc(q.cc_reduced, 1)
            ve.wait_ge(q.cc_reduced, 3)
            ve.reciprocal(c_cden, c_cden).then_inc(q.cc_recip, 1)
            ve.wait_ge(q.cc_recip, 1)
            ve.wait_ge(q.gates_made, 1)
            d3 = c_cden.rearrange("p (h i) -> p h i", i=NQ)
            ve.tensor_tensor(d3, d3, c_ga[:, :, :].rearrange("p i (h b) -> p h i b", b=3)[:, :, :, 0], ALU.mult)\
                .then_inc(q.cc_recip, 1)
            ve.wait_ge(q.cc_recip, 2)
            ve.tensor_scalar(d3[:, :, 0], d3[:, :, 0], v1("first_block"), None, ALU.mult).then_inc(q.cc_recip, 1)
            ve.wait_ge(q.cc_recip, 3)
            ve.tensor_tensor(cs3, cs3, c_cden.unsqueeze(2).broadcast_to([P, CH * NQ, NCMP]), ALU.mult)\
                .then_inc(q.cc_scaled, 1)

            def conv_tap(k):
                x, j = k % 2, k // 2
                if j == 0:
                    ve.wait_ge(q.c_glu, 3)
                    ve.tensor_scalar(c_acc[:, x, :], c_hp[:, x, 0:S], v1("dw", CW * x), v1("dw_b", x), ALU.mult,
                                     ALU.add).then_inc(q.conv_step, 1)
                elif j < CW:
                    ve.wait_ge(q.conv_step, k - 1)
                    ve.scalar_tensor_tensor(out=c_acc[:, x, :], in0=c_hp[:, x, j:j + S], scalar=v1("dw", CW * x + j),
                                            in1=c_acc[:, x, :], op0=ALU.mult, op1=ALU.add).then_inc(q.conv_step, 1)

            def c_output(pair_):
                ve.wait_ge(q.c_pv, 2 * pair_ + 2)
                ve.tensor_copy(low[:, pair_, :], obank[:, :]).then_inc(q.c_otaken, 1)

            def weights_(n):
                s, i = n // 4, NQ - 1 - n % 4
                d = den[:, 2 * i:2 * i + 2]
                ve.wait_ge(q.c_exped, 2 * n + 2)
                ve.reciprocal(d, d).then_inc(q.c_recip, 1)
                ve.wait_ge(q.c_recip, n + 1)
                ve.tensor_tensor(d, d, c_ga[:, i, 3 * s + 1:3 * s + 3], ALU.mult).then_inc(q.c_gated, 1)
                ve.wait_ge(q.c_gated, n + 1)
                for x in range(2):
                    ve.tensor_scalar(c_sc[:, i, x, 0:LEN[i]], c_sc[:, i, x, 0:LEN[i]], d[:, x:x + 1], None,
                                     ALU.mult).then_inc(q.c_weights, 1)

            for s in range(CH):
                if s in (4, 6):
                    c_output((s - 4) // 2)
                for k in range(NQ):
                    n, i = 4 * s + k, NQ - 1 - k
                    ve.wait_ge(q.c_scored, n + 1)
                    wait(ve, q.c_turned, 2 * n - 6)
                    ve.scalar_tensor_tensor(out=c_sc[:, i, :, 0:LEN[i]], in0=scores[:, :, 0:LEN[i]], scalar=-(CD ** -0.5),
                                            in1=c_bias[:, s:s + 1, S - LEN[i]:S].broadcast_to([P, 2, LEN[i]]),
                                            op0=ALU.mult, op1=ALU.subtract).then_inc(q.c_biased, 1)
                    ve.wait_ge(q.c_biased, n + 1)
                    ve.tensor_reduce(nmax[:, 2 * i:2 * i + 2], c_sc[:, i, :, 0:LEN[i]], AX.X, ALU.min).then_inc(q.c_min, 1)
                    if n:
                        weights_(n - 1)
                    for j in range(2):
                        conv_tap(2 * n + j)
            weights_(4 * CH - 1)
            for pair_ in (2, 3):
                c_output(pair_)
            end_stage(ve, 11)

            ve.memset(gl_bds[:, :, :], 0.0).then_inc(q.gl_scale, 1)
            ve.wait_ge(q.gl_scale, 3)
            ve.wait_ge(q.ln_summed, 1)
            for x in range(2):
                ve.scalar_tensor_tensor(out=c_acc[:, x, :], in0=stat[:, :], scalar=-1.0 / CC, in1=c_acc[:, x, :],
                                        op0=ALU.mult, op1=ALU.add).then_inc(q.ln_cent, 1)
            ve.wait_ge(q.gl_exps, 4)
            ve.scalar_tensor_tensor(out=gl_qt, in0=c_z[:, 16, :], scalar=GK ** -0.5, in1=gl_t[:, 0, :], op0=ALU.mult,
                                    op1=ALU.mult).then_inc(q.gl_prod, 1)
            ve.tensor_tensor(gl_kt, c_z[:, 17, :], gl_t[:, 1, :], ALU.mult).then_inc(q.gl_prod, 1)
            ve.tensor_tensor(gl_kd, c_z[:, 17, :], gl_e[:, 1, :], ALU.mult).then_inc(q.gl_prod, 1)
            for hd in range(GH):
                b = (scores[:, 0, :], scores[:, 1, :], turn[:, 0, :], turn[:, 1, :])[hd]
                ve.wait_ge(q.gl_att, hd + 1)
                ve.tensor_copy(gl_am[:, hd, :, :].rearrange("p n c -> p (n c)"), b[:, 0:NCH // 2 * GCH])\
                    .then_inc(q.gl_attc, 1)
            ve.wait_ge(q.gl_kdt, 1)
            ve.tensor_copy(gl_kdt[:, :, :].rearrange("p j c -> p (j c)"), obank[:, :]).then_inc(q.gl_kdc, 1)
            for x in range(2):
                ve.wait_ge(q.gl_kdt, 2 + x)
                ve.tensor_copy(gl_vt[:, :, x * P:(x + 1) * P], lin[:, x, :].rearrange("p (j c) -> p j c", c=P))\
                    .then_inc(q.gl_kdc, 1)
            for x in range(2):
                ve.wait_ge(q.ln_logged, 2)
                ve.scalar_tensor_tensor(out=c_acc[:, x, :], in0=c_acc[:, x, :], scalar=v1("ln_g", x), in1=gl_e[:, 2, :],
                                        op0=ALU.mult, op1=ALU.mult).then_inc(q.ln_norm, 1)
            for n in range(NCH):
                b = (scores[:, 0, :], scores[:, 1, :])[n % 2]
                ve.wait_ge(q.gl_u, n + 1)
                for hd in range(GH):
                    rows = slice(GK * hd, GK * hd + GK)
                    ve.tensor_copy(gl_us[rows, n, :], b[rows, hd * GV:(hd + 1) * GV]).then_inc(q.gl_uc, 1)
            ve.wait_ge(q.gl_uc, 4 * NCH)
            ve.memset(gl_st[:, 0, :], 0.0).then_inc(q.gl_state, 1)
            for n in range(1, NCH):
                ve.wait_ge(q.gl_state, n)
                ve.scalar_tensor_tensor(out=gl_st[:, n, :], in0=gl_st[:, n - 1, :], scalar=gl_dn[:, n - 1:n],
                                        in1=gl_us[:, n - 1, :], op0=ALU.mult, op1=ALU.add).then_inc(q.gl_state, 1)
            ve.wait_ge(q.gl_state, NCH)
            for hd in range(GH):
                rows = slice(GK * hd, GK * hd + GK)
                ve.tensor_copy(gl_bds[rows, :, hd * GV:(hd + 1) * GV], gl_st[rows, :, :]).then_inc(q.gl_bd, 1)
            for x in range(2):
                ve.wait_ge(q.gl_out, 5 + x)
                ve.tensor_copy(gl_o[:, x, :], (stat, obank)[x][:, :]).then_inc(q.gl_sum, 1)
            for x in range(2):
                for odd in range(2):
                    b = (lin[:, 0, :], lin[:, 1, :], turn[:, 0, :], turn[:, 1, :])[2 * x + odd]
                    o4 = gl_o[:, x, :].rearrange("p (n o c) -> p n o c", o=2, c=GCH)[:, :, odd, :]
                    ve.wait_ge(q.gl_sum, x + 1)
                    ve.tensor_tensor(o4, b[:, 0:NCH // 2 * GCH].rearrange("p (n c) -> p n c", c=GCH), o4, ALU.add)\
                        .then_inc(q.gl_add, 1)
            for x in range(2):
                ve.wait_ge(q.gl_fac, x + 1)
                ve.scalar_tensor_tensor(out=gl_t[:, x, :], in0=gl_o[:, x, :], scalar=v1("gla_g", x), in1=gl_e[:, x, :],
                                        op0=ALU.mult, op1=ALU.mult).then_inc(q.gl_norm, 1)
                ve.wait_ge(q.gl_norm, x + 1)
                ve.wait_ge(q.gl_silu, x + 1)
                ve.tensor_tensor(low[:, 6 + x, :], gl_t[:, x, :], c_z[:, 20 + x, :], ALU.mult)
            end_stage(ve, 12)
            out_lows(DC + BH, low, g_hi, g_lo, range(DC))
            residual("c_out", "ffn2")
            end_stage(ve, 13)
            add_square("ffn2", DC - 1)

            gains("ffn2")
            ve.wait_ge(q.r_ready, NORM["ffn2"] + 1)
            t0 = TILE["ffn2_in"]

            def gated(i, u):
                ve.wait_ge(q.tile_done, t0 + 2 * u + 1 + 4 * i)
                ve.tensor_tensor(f_c[:, 2 * u, :], lin[:, (t0 + 2 * u) % 2, :], r[:, :], ALU.mult)\
                    .then_inc(q.tile_taken, 1)
                ve.wait_ge(q.tile_done, t0 + 2 * u + 2 + 4 * i)
                ve.tensor_tensor(f_c[:, 2 * u + 1, :], lin[:, (t0 + 2 * u + 1) % 2, :], r[:, :], ALU.mult)\
                    .then_inc(q.tile_taken, 1)
                ve.wait_ge(q.tile_taken, t0 + 2 * u + 2 + 4 * i)
                ve.wait_ge(q.s_gate, u + 1 + 2 * i)
                hidden(2, i, u, 2 * u + 1)
            with ve.Fori(0, FC // 2) as i:
                gated(i, 0)
                gated(i, 1)
            residual("ffn2_out", "ple2", "ple2", g_hi, g_lo, q.h_gained)
            end_stage(ve, 14)
            add_square("ple2", DC - 1)
            ple(2, "final")
            end_stage(ve, 15)
            add_square("final", DC - 1)
            ve.wait_ge(q.r_ready, NORM["final"] + 1)
            for c in range(DC):
                ve.scalar_tensor_tensor(out=g[:, c, :], in0=h[:, c, :], scalar=v1("final", c), in1=r[:, :],
                                        op0=ALU.mult, op1=ALU.mult).then_inc(q.residual_added, 1)

        @block.scalar
        def _(ac):
            def out_highs(src, hi, chunks):
                for k in chunks:
                    ac.activation(hi[:, k, :], src[:, k, :], ACT.Copy).then_inc(q.out_rounded, 1)

            def square(norm, c, sem_, value):
                n = NORM[norm]
                ac.wait_ge(sem_, value)
                if isinstance(c, int) and c == 0:
                    dst = sq_sum
                else:
                    dst = sq_last
                    wait(ac, q.squares_added, (DC - 1) * n + c - 1)
                ac.activation(dst, h[:, c, :], ACT.Square).then_inc(q.h_squared, 1)

            def residual_squares(name, norm, stage):
                per = 2 if name in ("ffn0_out", "ffn1_out", "ffn2_out", "b_wo") else 1
                t = TILE[name] + per
                square(norm, 0, q.tile_taken, t)
                with ac.Fori(1, DC - 1) as c:
                    square(norm, c, q.tile_taken, t + per * c)
                end_stage(ac, stage)
                square(norm, DC - 1, q.tile_taken, t + per * (DC - 1))

            def factor(name):
                n = NORM[name]
                ac.wait_ge(q.h_summed, n + 1)
                ac.activation(lnr[:, :], stat[:, :], ACT.Ln, bias=eps[:, 0:1], scale=1.0 / D).then_inc(q.r_logged, 1)
                ac.wait_ge(q.r_logged, n + 1)
                ac.activation(r[:, :], lnr[:, :], ACT.Exp, scale=-0.5).then_inc(q.r_ready, 1)

            def inv_sqrt(dst, n, summed, logged, factor_, summed_v, logged_v):
                ac.wait_ge(summed, summed_v)
                ac.activation(dst, stat[:, :], ACT.Ln, bias=eps[:, 0:1], scale=1.0 / n).then_inc(logged, 1)
                ac.wait_ge(logged, logged_v)
                ac.activation(dst, dst, ACT.Exp, scale=-0.5).then_inc(factor_, 1)

            def conv_ffn(n):
                factor(f"ffn{n}")
                t0, f0 = TILE[f"ffn{n}_in"], 2 * FC * n

                def pair(i, u):
                    for j in range(2):
                        k = 2 * u + j
                        w = VEC[f"conv{n}"] + 4 * k + 16 * i
                        ac.wait_ge(q.tile_taken, t0 + k + 1 + 4 * i)
                        wait(ac, q.f_through, FC * n + 2 * i + u - 1)
                        ac.activation(f_c[:, k, :], f_u[:, k, 2:S + 2], ACT.Identity, bias=vec[:, bass.ds(w + 3, 1)],
                                      scale=vec[:, bass.ds(w + 2, 1)]).then_inc(q.f_first, 1)
                    ac.wait_ge(q.f_conv, 2 * f0 + 4 * u + 4 + 8 * i)
                    ac.activation(f_sg[:, u, :], f_c[:, 2 * u + 1, :], ACT.Silu).then_inc(q.f_silu, 1)
                pair(0, 0)
                pair(0, 1)
                with ac.Fori(1, FC // 2) as i:
                    pair(i, 0)
                    pair(i, 1)

            def ple(n, norm, stage):
                factor(f"ple{n}")
                t0, g0 = TILE[f"ple{n}"], DC * n

                def sigmoid(i, j):
                    ac.wait_ge(q.tile_taken, t0 + 2 * j + 1 + 4 * i)
                    ac.activation(p_sg[:, j, :], p_gp[:, j, :], ACT.Sigmoid).then_inc(q.ple_sigmoid, 1)
                sigmoid(0, 0)
                sigmoid(0, 1)
                square(norm, 0, q.residual_added, g0 + 1)
                with ac.Fori(1, DC // 2) as i:
                    for j in range(2):
                        sigmoid(i, j)
                        square(norm, 2 * i + j - 1, q.residual_added, g0 + 2 * i + j)
                end_stage(ac, stage)
                square(norm, DC - 1, q.residual_added, g0 + DC)

            def load_p(n):
                ac.dma_start(p_in_t[:, :, :].rearrange("p c s -> p (c s)"), a["p_t"][n]).then_inc(q.p_in, 16)

            ac.dma_start(pos_i, a["positions"].broadcast_to([P, S])).then_inc(q.positions_in, 16)
            for i in range(NQ):
                ac.dma_start(posq_i[:, i:i + 1], a["positions"][0, i * P:(i + 1) * P].rearrange("(p a) -> p a", a=1))\
                    .then_inc(q.positions_in, 16)
            ac.dma_start(a_lam[:, 0:4, :].rearrange("p k d -> p (k d)"), a["lam"].broadcast_to([P, 4 * AQK])).then_inc(q.lam_in, 16)
            ac.dma_start(a_tab, a["table"].broadcast_to([P, BUCKETS * AH])).then_inc(q.positions_in, 16)
            ac.dma_start(walpha[32:48, :], a["w_alpha"]).then_inc(q.extra_in, 16)
            ac.dma_start(w2c[:, :, :].rearrange("p c d -> p (c d)"), a["cmp_w2"]).then_inc(q.extra_in, 16)
            load_p(0)
            ac.wait_ge(q.setup_step, 2)
            ac.wait_ge(q.x_in, 16 * DC)
            for c in range(DC):
                square("attn0", c, q.x_in, 16 * DC)
            factor("attn0")

            def a_step(s, par, proj, attn, tail):
                hd = s - 1

                def squared(j):
                    if proj:
                        ac.wait_ge(q.tile_taken, TILE["a_qkv"] + 3 * s + j + 1)
                        ac.activation(a_sq[:, j, :], a_raw[:, j, :], ACT.Square).then_inc(q.a_squared, 1)

                def exps(k):
                    if attn:
                        n, i = 4 * hd + k, NQ - 1 - k
                        ac.wait_ge(q.a_min, n + 1)
                        for x in range(2):
                            e = a_sc[:, i, x, 0:LEN[i]]
                            ac.activation(e, e, ACT.Exp, bias=nmax[:, 2 * i + x:2 * i + x + 1], scale=-1.0,
                                          accum_out=den[:, 2 * i + x:2 * i + x + 1]).then_inc(q.a_exped, 1)

                def factor_(j):
                    if proj:
                        inv_sqrt(a_ri[:, j, :], AQK, q.a_summed, q.a_logged, q.a_factor, 2 * s + j + 1, 2 * s + j + 1)

                if tail:
                    ac.wait_ge(q.a_otaken, s - 1)
                    ac.activation(a_sq[:, 2, :], a_rawo, ACT.Square).then_inc(q.a_osquared, 1)
                exps(0)
                squared(0)
                if tail:
                    inv_sqrt(a_ri[:, 2, :], 2 * AQK, q.a_osummed, q.a_ologged, q.a_ofactor, s - 1, s - 1)
                exps(1)
                squared(1)
                exps(2)
                factor_(0)
                exps(3)
                factor_(1)
                if proj:
                    ac.wait_ge(q.a_vturned, s + 1)
                    ac.activation(a_v[:, par, :, :].rearrange("p j c -> p (j c)"), obank[:, :], ACT.Copy)\
                        .then_inc(q.a_vcopied, 1)
                if isinstance(s, int) and s == 0:
                    ac.wait_ge(q.lam_dots, 1)
                    ac.activation(lame, lamd, ACT.Exp).then_inc(q.lam_exps, 1)
                    ac.wait_ge(q.angles_ready, 1)
                    ac.activation(sinb[:, :], sinb[:, :], ACT.Sin)
                    ac.activation(cosb[:, :], cosb[:, :], ACT.Sin)
                    ac.preload_act_table_set("natural_log_exp_and_others")
                if attn:
                    for k in range(NQ):
                        i = NQ - 1 - k
                        ac.wait_ge(q.a_turned, 4 * hd + k + 1)
                        ac.activation(a_pt[:, 0:i + 1, i * P:(i + 1) * P],
                                      turn[:, k % 2, 0:LEN[i]].rearrange("p (j c) -> p j c", c=P), ACT.Copy)\
                            .then_inc(q.a_tcopied, 1)

            ac.preload_act_table_set("natural_log_exp_and_others")
            def early_highs():
                ac.wait_ge(q.a_onormed, AH - 1)
                out_highs(a_o, g_hi, range(AH - 1))

            a_steps(ac, a_step, early_highs)
            ac.wait_ge(q.a_onormed, AH)
            out_highs(a_o, g_hi, (AH - 1,))
            residual_squares("a_wo", "ffn0", 2)
            conv_ffn(0)
            residual_squares("ffn0_out", "ple0", 3)
            ple(0, "attn1", 4)

            load_p(1)
            factor("attn1")
            ac.preload_act_table_set("natural_log_exp_and_others")
            for j in range(7):
                ac.wait_ge(q.tile_taken, TILE["b_dkv"] + j + 1)
                ac.activation(b_dsq[:, j, :], b_cr[:, j, :], ACT.Square).then_inc(q.bd_squared, 1)
                n = j - 4
                if n >= 0:
                    inv_sqrt(b_ri[:, n, :], (KVL, ROPE, QL)[n], q.bd_summed, q.bd_logged, q.bd_factor, n + 1, n + 1)
            end_stage(ac, 5)

            def b_step(s, par, proj, attn):
                def squared(j):
                    if proj:
                        ac.wait_ge(q.tile_taken, TILE["b_pair"] + 7 * s + j + 1)
                        ac.activation(b_sq[:, j, :], b_raw[:, j, :], ACT.Square).then_inc(q.b_squared, 1)

                def exps(x, k):
                    if attn:
                        n, i = 8 * (s - 1) + 4 * x + k, NQ - 1 - k
                        ac.wait_ge(q.b_min, n + 1)
                        e = b_sc[:, x, i, 0:LEN[i]]
                        ac.activation(e, e, ACT.Exp, bias=nmax[:, 4 * x + i:4 * x + i + 1], scale=-1.0,
                                      accum_out=den[:, 4 * x + i:4 * x + i + 1]).then_inc(q.b_exped, 1)
                        first = 2 * (4 * x + k)
                        if not proj and first < BH - 2:
                            ac.wait_ge(q.b_otaken, first + 2)
                            out_highs(b_o, b_o_hi, (first, first + 1))

                def factor_(j):
                    if proj:
                        inv_sqrt(b_ri[:, j, :], ROPE if j == 2 else NOPE, q.b_summed, q.b_logged, q.b_factor,
                                 5 * s + j + 1, 5 * s + j + 1)

                def turned(x, *ks):
                    if attn:
                        for k in ks:
                            i = NQ - 1 - k
                            ac.wait_ge(q.b_turned, 8 * (s - 1) + 4 * x + k + 1)
                            if x == 1 and k == 0:
                                ac.wait_ge(q.b_pv, 2 * s - 1)
                            ac.activation(b_pt[:, 0:i + 1, i * P:(i + 1) * P],
                                          turn[:, k % 2, 0:LEN[i]].rearrange("p (j c) -> p j c", c=P), ACT.Copy)\
                                .then_inc(q.b_tcopied, 1)

                def values(x):
                    if proj:
                        ac.wait_ge(q.b_vturned, 2 * s + x + 1)
                        ac.activation(b_v[:, par, x, :], obank[:, :], ACT.Copy).then_inc(q.b_vcopied, 1)

                squared(0); exps(0, 0); squared(1); exps(0, 1); squared(2); factor_(0); exps(0, 2); squared(3)
                factor_(1); exps(0, 3); squared(4); factor_(2); exps(1, 0); turned(0, 0, 1); factor_(3)
                exps(1, 1); turned(0, 2, 3); factor_(4); exps(1, 2); exps(1, 3)
                values(0); turned(1, 0); values(1); turned(1, 1, 2, 3)

            ac.preload_act_table_set("natural_log_exp_and_others")
            b_steps(ac, b_step)
            ac.wait_ge(q.b_otaken, BH)
            out_highs(b_o, b_o_hi, (BH - 2, BH - 1))
            residual_squares("b_wo", "ffn1", 6)
            conv_ffn(1)
            residual_squares("ffn1_out", "ple1", 7)
            ac.dma_start(onehot, a["onehot"]).then_inc(q.extra_in, 16)
            ac.dma_start(relt, a["relt"]).then_inc(q.extra_in, 16)
            ple(1, "mix2", 8)

            load_p(2)
            factor("mix2")
            for x in range(2):
                ac.wait_ge(q.tile_taken, TILE["c_in"] + 15 + x)
                ac.activation(c_acc[:, x, :], c_z[:, 14 + x, :], ACT.Sigmoid).then_inc(q.c_sigmoid, 1)
            for x in range(2):
                ac.wait_ge(q.tile_taken, TILE["c_in"] + 21 + x)
                ac.activation(c_z[:, 20 + x, :], c_z[:, 20 + x, :], ACT.Silu).then_inc(q.gl_silu, 1)
            end_stage(ac, 9)

            ac.wait_ge(q.gates_turned, 1)
            ac.activation(c_ga[:, :, :], stat[:, :].rearrange("p (i c) -> p i c", c=P)[:, :, 0:24], ACT.Sigmoid)\
                .then_inc(q.gates_made, 1)
            for x in range(2):
                ac.wait_ge(q.c_vturned, x + 1)
                ac.activation(c_v[:, x, :, :].rearrange("p j c -> p (j c)"), turn[:, x, :], ACT.Copy)\
                    .then_inc(q.c_vcopied, 1)
            ac.wait_ge(q.gl_alpha, 1)
            ac.activation(gl_x, scores[:, 1, :], ACT.Identity, bias=v1("b_alpha")).then_inc(q.gl_abs, 1)
            ac.wait_ge(q.gl_abs, 1)
            ac.activation(gl_l, gl_x, ACT.Abs).then_inc(q.gl_abs, 1)
            ac.wait_ge(q.gl_abs, 2)
            ac.activation(gl_l, gl_l, ACT.Exp, scale=-1.0).then_inc(q.gl_exp, 1)
            ac.wait_ge(q.gl_exp, 1)
            ac.activation(gl_l, gl_l, ACT.Ln, bias=ones[:, 0:1]).then_inc(q.gl_ln, 1)
            for k in range(4):
                ac.wait_ge(q.tile_taken, TILE["c_cmp"] + 2 * k + 2)
                ac.activation(c_hid[:, k, :], c_hid[:, k, :], ACT.Silu, bias=v1("cmp_b1", k)).then_inc(q.hid_act, 1)
            end_stage(ac, 10)
            ac.wait_ge(q.cc_reduced, 2)
            cs3 = c_cs[:, :, :, :].rearrange("p h i n -> p (h i) n")
            ac.activation(cs3, cs3, ACT.Exp, scale=-1.0).then_inc(q.cc_exped, 1)

            for s in range(CH + 1):
                for k in range(NQ):
                    i = NQ - 1 - k
                    if s < CH:
                        n = 4 * s + k
                        ac.wait_ge(q.c_min, n + 1)
                        for x in range(2):
                            e = c_sc[:, i, x, 0:LEN[i]]
                            ac.activation(e, e, ACT.Exp, bias=nmax[:, 2 * i + x:2 * i + x + 1], scale=-1.0,
                                          accum_out=den[:, 2 * i + x:2 * i + x + 1]).then_inc(q.c_exped, 1)
                    if s == 0:
                        for hd in (2 * k, 2 * k + 1):
                            ac.wait_ge(q.cc_turned, hd + 1)
                            ac.activation(c_ct[0:NCMP, hd, :], turn[0:NCMP, hd % 2, :], ACT.Copy).then_inc(q.cc_copied, 1)
                    if s > 0:
                        for x in range(2):
                            ac.wait_ge(q.c_turned, 8 * (s - 1) + 2 * k + x + 1)
                            if k == 0 and x == 0:
                                wait(ac, q.c_pv, s - 2)
                            ac.activation(c_pts[(s - 1) % 2][:, x, 0:i + 1, i * P:(i + 1) * P],
                                          turns[k % 2][:, x, 0:LEN[i]].rearrange("p (j c) -> p j c", c=P), ACT.Copy)\
                                .then_inc(q.c_tcopied, 1)
            end_stage(ac, 11)

            ac.preload_act_table_set("natural_log_exp_and_others")
            ac.wait_ge(q.gl_scan, 1)
            ac.activation(gl_t[:, 0, :], gl_b, ACT.Exp).then_inc(q.gl_exps, 1)
            ac.activation(gl_t[:, 1, :], gl_b, ACT.Exp, scale=-1.0).then_inc(q.gl_exps, 1)
            ac.activation(gl_dn, gl_b.rearrange("p (n c) -> p n c", c=GCH)[:, :, GCH - 1], ACT.Exp).then_inc(q.gl_exps, 1)
            ac.wait_ge(q.gl_scan, 2)
            ac.activation(gl_e[:, 1, :], gl_l, ACT.Exp).then_inc(q.gl_exps, 1)
            for x in range(2):
                ac.wait_ge(q.ln_cent, x + 1)
                ac.activation(gl_s[:, x, :], c_acc[:, x, :], ACT.Square).then_inc(q.ln_sq, 1)
            out_highs(low, g_hi, range(NQ))
            ac.wait_ge(q.ln_summed, 2)
            ac.activation(gl_e[:, 2, :], stat[:, :], ACT.Ln, bias=eps[:, 0:1], scale=1.0 / CC).then_inc(q.ln_logged, 1)
            ac.wait_ge(q.ln_logged, 1)
            ac.activation(gl_e[:, 2, :], gl_e[:, 2, :], ACT.Exp, scale=-0.5).then_inc(q.ln_logged, 1)
            for x in range(2):
                ac.wait_ge(q.gl_add, 2 * x + 2)
                ac.activation(gl_s[:, x, :], gl_o[:, x, :], ACT.Square).then_inc(q.gl_sq, 1)
            for x in range(2):
                inv_sqrt(gl_e[:, x, :], GV, q.gl_ss, q.gl_log, q.gl_fac, x + 1, x + 1)
            for x in range(2):
                ac.wait_ge(q.ln_norm, x + 1)
                ac.activation(low[:, 4 + x, :], c_acc[:, x, :], ACT.Silu, bias=v1("ln_b", x))
            end_stage(ac, 12)
            out_highs(low, g_hi, range(NQ, DC))
            residual_squares("c_out", "ffn2", 13)

            factor("ffn2")
            t0 = TILE["ffn2_in"]

            def gate(i, u):
                ac.wait_ge(q.tile_taken, t0 + 2 * u + 1 + 4 * i)
                wait(ac, q.f_through, 2 * FC + 2 * i + u - 1)
                ac.activation(f_sg[:, u, :], f_c[:, 2 * u, :], ACT.Silu).then_inc(q.s_gate, 1)
            with ac.Fori(0, FC // 2) as i:
                gate(i, 0)
                gate(i, 1)
            residual_squares("ffn2_out", "ple2", 14)
            ple(2, "final", 15)
            factor("final")
            for c in range(DC):
                ac.wait_ge(q.residual_added, 3 * DC + c + 1)
                ac.dma_start(out[c * P:(c + 1) * P, :], g[:, c, :]).then_inc(q.out_stored, 16)

        @block.gpsimd
        def _(po):
            def causal_within_chunks():
                po.wait_ge(q.weights_split, GROUP["c_out"] + 2)
                po.wait_ge(q.gl_attc, GH)
                for odd in range(2):
                    half = gl_am[64 * odd:64 * odd + 64, :, :, :].rearrange("p h n c -> p (h n) c")
                    po.affine_select(out=half, in_=half, compare_op=ALU.is_ge, fill=0.0, base=0,
                                     pattern=[[0, GH * NCH // 2], [1, GCH]], channel_multiplier=-1).then_inc(q.gl_mask, 1)

            po.wait_ge(q.consts_in, 32)
            for name, count, blocks, per in STREAM:
                def split(k, n, i, end):
                    at_ = slice(0, blocks[k % 2] * P)
                    po.wait_ge(landed[n % 2], 16 * (n // 2 + 1) + 16 * i)
                    wait(po, q.tile_done, end)
                    b3 = [t_[:, n % 2, at_].rearrange("p (b c) -> p b c", c=P) for t_ in (w_hi, slots)]
                    po.tensor_tensor(b3[0], b3[1], ones.unsqueeze(1).broadcast_to([P, blocks[k % 2], P]), ALU.mult).then_inc(q.hi_made, 1)
                    po.wait_ge(q.hi_made, n + 1 + 2 * i)
                    po.tensor_tensor(w_lo[:, n % 2, at_], slots[:, n % 2, at_], w_hi[:, n % 2, at_].bitcast(F32),
                                     ALU.subtract).then_inc(q.weights_split, 1)
                stream(po, name, count, split, causal_within_chunks if name == "c_out" else None)


def _blocks(w):
    k, m = w.shape
    return w.reshape(k // P, P, m // P, P).transpose(2, 1, 0, 3).reshape(m // P, P, k)


def _side_by_side(tiles):
    return tiles.transpose(1, 0, 2).reshape(P, -1)


def _halves(tiles):
    n, _, k = tiles.shape
    return tiles.reshape(n, P, 2, k // 2).transpose(0, 2, 1, 3).reshape(2 * n, P, k // 2)


def _columns(v):
    return np.ascontiguousarray(v.reshape(-1, P).T)


def _consts():
    i = np.arange(P)
    rot = np.zeros((P, P), np.float32)
    low = i % ROPE < ROPE // 2
    rot[i[low] + ROPE // 2, i[low]] = -1.0
    rot[i[~low] - ROPE // 2, i[~low]] = 1.0
    mask = np.where(np.arange(S)[None, :] - (S - P) <= i[:, None], 0.0, NEG)
    return np.concatenate([np.ones((P, P)), i[:, None] // 64 == i[None, :] // 64, np.eye(P), rot, mask], axis=1)\
        .astype(np.float32)


def _onehot():
    starts = np.array([0] + bucket_starts())
    dist = S - 1 - np.arange(S)
    bucket = np.searchsorted(starts, dist, side="right") - 1
    return (np.arange(BUCKETS)[:, None] == bucket[None, :]).astype(np.float32)


def _lay_out(x):
    f = {k: np.asarray(v) for k, v in x.items()}
    a = {}
    a["x_t"] = f["x"][0].T.reshape(DC, P, S).transpose(1, 0, 2)
    p = np.concatenate([f["p"][:, 0], f["p_2"][:, 0]], axis=0)
    a["p_t"] = p.transpose(0, 2, 1).reshape(3, 2, P, S).transpose(0, 2, 1, 3).reshape(3, P, -1)
    a["positions"] = f["positions"].astype(np.int32) if f["positions"].dtype != np.int32 else f["positions"]
    a["table"] = f["rel_bias_table"].reshape(1, -1)
    a["lam"] = np.concatenate([f["a_lam_q1"], f["a_lam_k1"], f["a_lam_q2"], f["a_lam_k2"]], axis=1)
    a["consts"] = _consts()
    a["onehot"] = _onehot()
    a["relt"] = f["rel_bias_2"]
    a["w_alpha"] = f["gla_w_alpha_2"][0]
    a["cmp_w2"] = np.concatenate([f["cmp_w2_k_2"][0].reshape(2, P, CD), f["cmp_w2_v_2"][0].reshape(2, P, CD)])\
        .transpose(1, 0, 2).reshape(P, -1)

    qkv = _blocks(f["a_w_qkv"][0]).reshape(3, AH, P, D).transpose(1, 0, 2, 3).reshape(3 * AH, P, D)
    a["w_a_qkv"] = qkv
    a["w_a_wo"] = _blocks(f["a_w_o"][0])

    def ffn_in(first, second):
        return np.stack([_blocks(first), _blocks(second)], axis=1).reshape(2 * FC, P, D)

    def ple(gate, proj):
        return np.concatenate([_blocks(gate), _blocks(proj)], axis=2)

    for n in range(2):
        w = f["ffn_w_in"][n]
        a[f"w_ffn{n}_in"] = ffn_in(w[:, :FF], w[:, FF:])
        a[f"w_ffn{n}_out"] = _halves(_blocks(f["ffn_w_out"][n]))
        a[f"w_ple{n}"] = ple(f["ple_w_gate"][n], f["ple_w_proj"][n])
    a["w_ffn2_in"] = ffn_in(f["ffn_w_gate_2"][0], f["ffn_w_up_2"][0])
    a["w_ffn2_out"] = _halves(_blocks(f["ffn_w_down_2"][0]))
    a["w_ple2"] = ple(f["ple_w_gate_2"][0], f["ple_w_proj_2"][0])

    dkv = f["w_dkv"]
    a["w_b_dkv"] = _blocks(np.concatenate([dkv, dkv[:, KVL:]], axis=1))
    a["w_b_dq"] = _blocks(f["b_w_dq"][0])
    uq = f["b_w_uq"][0].reshape(QL, B_PAIRS, 2, NOPE + ROPE)
    ukv = f["w_ukv"].reshape(KVL, B_PAIRS, 2, NOPE + P)
    pair = []
    for n in range(B_PAIRS):
        up = np.concatenate([uq[:, n, 0, :NOPE], uq[:, n, 1, :NOPE], uq[:, n, 0, NOPE:], uq[:, n, 1, NOPE:]], axis=1)
        kv = np.concatenate([ukv[:, n, 0, :NOPE], ukv[:, n, 1, :NOPE], ukv[:, n, 0, NOPE:], ukv[:, n, 1, NOPE:]], axis=1)
        pair += [_side_by_side(_blocks(up)), np.pad(_side_by_side(_blocks(kv)), ((0, 0), (0, 4 * P)))]
    a["w_b_pair"] = np.stack(pair)
    a["w_b_wo"] = _halves(_blocks(f["b_w_o"][0]))

    w = f["w_in_2"][0]
    splits = [512, 128, 128, 128, 128, 128, 128, 24, 512, 128, 128, 256, 16, 256]
    nq, kc, vc, ks, vs, kw, vw, ng, cu, gq, gk, gv, ga, gr = np.split(w, np.cumsum(splits)[:-1], axis=1)
    heads = [nq[:, CD * i:CD * (i + 1)] for i in range(CH)]
    cols = [c for t in range(4) for c in (heads[t], heads[t + 4])] + [ks, kw, vs, vw]
    for m in (kc, vc):
        for x in range(CKV):
            cols += [m[:, CD * x:CD * (x + 1)]] * 2
    cols += [cu, gq, gk, gv, gr, ng, np.zeros((D, 8), w.dtype), ga, np.zeros((D, 80), w.dtype)]
    a["w_c_in"] = _blocks(np.concatenate(cols, axis=1))
    a["w_c_cmp"] = _halves(np.concatenate([_blocks(f["cmp_w1_k_2"][0]), _blocks(f["cmp_w1_v_2"][0])]))
    a["w_c_out"] = _blocks(f["w_out_2"][0])

    def twice(v):
        return np.concatenate([v, v]).reshape(P, 1)

    def conv(n):
        t = np.concatenate([f["ffn_conv_w"][n], f["ffn_conv_b"][n][None]])
        t = t.reshape(4, 2, FC, P).transpose(3, 2, 1, 0)
        return t.reshape(P, -1)

    inv = np.exp(np.float32(-math.log(ROPE_BASE)) * np.arange(ROPE // 2, dtype=np.float32) * np.float32(2.0 / ROPE))
    dw = f["conv_w_2"][0]
    vecs = {
        "attn0": _columns(f["attn_norm"][0]), "attn1": _columns(f["attn_norm"][1]), "kv": _columns(f["kv_norm"]),
        "ffn0": _columns(f["ffn_norm"][0]), "ffn1": _columns(f["ffn_norm"][1]),
        "ple0": _columns(f["ple_norm"][0]), "ple1": _columns(f["ple_norm"][1]),
        "mix2": _columns(f["mix_norm_g_2"][0]), "ffn2": _columns(f["ffn_norm_g_2"][0]),
        "ple2": _columns(f["ple_norm_g_2"][0]), "final": _columns(f["final_norm_g_2"]),
        "a_q": twice(f["a_q_norm"][0]), "a_k": twice(f["a_k_norm"][0]), "a_sub": _columns(f["a_sub_norm"][0]),
        "ckv": _columns(f["ckv_norm"]), "cq": _columns(f["b_cq_norm"][0]), "k_nope": _columns(f["k_nope_norm"]),
        "k_pe": twice(f["k_pe_norm"]), "q_nope": _columns(f["b_q_nope_norm"][0]), "q_pe": twice(f["b_q_pe_norm"][0]),
        "inv_freq": np.tile(inv, 4).reshape(P, 1), "conv0": conv(0), "conv1": conv(1),
        "cmp_b1": np.concatenate([_columns(f["cmp_b1_k_2"][0]), _columns(f["cmp_b1_v_2"][0])], axis=1),
        "cmp_pos": np.concatenate([f[n][0].reshape(16, P).T for n in ("cmp_pos_k_2", "cmp_pos_v_2")], axis=1),
        "dw": dw.reshape(CW, 2, P).transpose(2, 1, 0).reshape(P, -1), "dw_b": _columns(f["conv_b_2"][0]),
        "ln_g": _columns(f["conv_ln_g_2"][0]), "ln_b": _columns(f["conv_ln_b_2"][0]),
        "b_alpha": _columns(f["gla_b_alpha_2"][0]), "gla_g": _columns(f["gla_norm_g_2"][0]),
        "t5_start": np.tile(np.array(bucket_starts(), np.float32), (P, 1)),
        "first_block": (np.arange(P) >= CMPB - 1).astype(np.float32).reshape(P, 1),
    }
    for name, n in VEC_COLS:
        assert vecs[name].shape == (P, n), (name, vecs[name].shape)
    a["vec"] = np.concatenate([vecs[name] for name, _ in VEC_COLS], axis=1)
    return {k: np.ascontiguousarray(v) for k, v in a.items()}


def kernel(**inputs):
    import concourse.bacc as bacc
    from concourse.bass_utils import run_bass_kernel_spmd as run

    arrays = {f"in_{k}": v for k, v in _lay_out(inputs).items()}
    nc = bacc.Bacc("TRN2", target_bir_lowering=False, num_devices=1,
                   dynamic_dma_scratch_size=DMA_SCRATCH)
    aps = {k[3:]: nc.dram_tensor(k, v.shape, mybir.dt.from_np(v.dtype), kind="ExternalInput").ap()
           for k, v in arrays.items()}
    out = nc.dram_tensor("out", [D, S], F32, kind="ExternalOutput").ap()
    build_program(nc, aps, out)
    result = run(nc, [arrays], core_ids=[0])
    return result.results[0]["out"].T.reshape(1, S, D)
```
